# Optimizing a Trainium2 kernel written in Bass

```python
import jax, jax.numpy as jnp
from jax import lax
import numpy as np

D_MODEL = 1024
BATCH = 1
SEQ = 256
DEPTH = 2

GRID_W = 64
EPS = 1e-6

MLA_HEADS = 8
MLA_Q_LORA = 256
MLA_KV_LORA = 128
MLA_NOPE = 64
MLA_ROPE = 32
MLA_V = 64
MLA_QK = MLA_NOPE + MLA_ROPE
ROPE_THETA = 10000.0
Q_BLOCK = 128

NA_HEADS = 8
NA_HD = 64
NA_KH = 8
NA_KW = 16

IN_COLS = MLA_Q_LORA + MLA_KV_LORA + MLA_ROPE + 3 * NA_HEADS * NA_HD
MIX_WIDTH = MLA_HEADS * MLA_V + NA_HEADS * NA_HD

CONV_W = 31

N_EXPERTS = 64
TOP_K = 8
N_GROUPS = 8
TOPK_GROUPS = 4
D_EXPERT = 256
D_SHARED = 256
ROUTED_SCALE = 2.5
MOE_BLOCK = 256

kernel_name = "hybrid_mla_natten_conformer_moe_encoder"

def rms_norm(x, w):
    xf = x.astype(jnp.float32)
    y = xf * lax.rsqrt(jnp.mean(xf * xf, axis=-1, keepdims=True) + EPS)
    return (y * w.astype(jnp.float32)).astype(x.dtype)

def layer_norm(x, w, b):
    xf = x.astype(jnp.float32)
    mu = jnp.mean(xf, axis=-1, keepdims=True)
    var = jnp.mean(jnp.square(xf - mu), axis=-1, keepdims=True)
    y = (xf - mu) * lax.rsqrt(var + EPS)
    return (y * w.astype(jnp.float32) + b.astype(jnp.float32)).astype(x.dtype)

def axial_rope(seq_len, dtype):
    t = jnp.arange(seq_len)
    row = (t // GRID_W).astype(jnp.float32)
    col = (t % GRID_W).astype(jnp.float32)
    n_freq = MLA_ROPE // 4
    inv = ROPE_THETA ** (-jnp.arange(n_freq, dtype=jnp.float32) / n_freq)
    ang = jnp.concatenate([row[:, None] * inv, col[:, None] * inv], axis=-1)
    return jnp.cos(ang).astype(dtype), jnp.sin(ang).astype(dtype)

def rope_tail(x, cos, sin):
    xn, xr = x[..., :-MLA_ROPE], x[..., -MLA_ROPE:]
    half = MLA_ROPE // 2
    x1, x2 = xr[..., :half], xr[..., half:]
    c, s = cos[None, :, None, :], sin[None, :, None, :]
    rot = jnp.concatenate([x1 * c - x2 * s, x1 * s + x2 * c], axis=-1)
    return jnp.concatenate([xn, rot], axis=-1)

def dense_bidirectional_attention(q, k, v, scale):
    B, S, H, Dk = q.shape
    Dv = v.shape[-1]
    nb = S // Q_BLOCK
    q_blocks = q.reshape(B, nb, Q_BLOCK, H, Dk).transpose(1, 0, 2, 3, 4)

    def one_block(qb):
        s = jnp.einsum('bqhd,bkhd->bhqk', qb, k, preferred_element_type=jnp.float32) * scale
        p = jax.nn.softmax(s, axis=-1).astype(v.dtype)
        return jnp.einsum('bhqk,bkhd->bqhd', p, v)

    o = lax.map(one_block, q_blocks)
    return o.transpose(1, 0, 2, 3, 4).reshape(B, S, H * Dv)

def mla_heads(cq, ckv, k_pe, q_a_norm_w, kv_a_norm_w, w_q_b, w_kv_b, q_norm_w, k_norm_w):
    B, S, _ = cq.shape
    cos, sin = axial_rope(S, cq.dtype)
    q = (rms_norm(cq, q_a_norm_w) @ w_q_b).reshape(B, S, MLA_HEADS, MLA_QK)
    kv = (rms_norm(ckv, kv_a_norm_w) @ w_kv_b).reshape(B, S, MLA_HEADS, MLA_NOPE + MLA_V)
    k_nope, v = kv[..., :MLA_NOPE], kv[..., MLA_NOPE:]
    k_pe_h = jnp.broadcast_to(k_pe[:, :, None, :], (B, S, MLA_HEADS, MLA_ROPE))
    k = jnp.concatenate([k_nope, k_pe_h], axis=-1)
    q = rope_tail(rms_norm(q, q_norm_w), cos, sin)
    k = rope_tail(rms_norm(k, k_norm_w), cos, sin)
    return dense_bidirectional_attention(q, k, v, MLA_QK ** -0.5)

def neighbourhood_attention(q, k, v, rpb):
    B, S, H, Dh = q.shape
    rows = S // GRID_W
    kh = min(NA_KH, rows)
    qg = q.reshape(B, rows, GRID_W, H, Dh)
    kg = k.reshape(B, rows, GRID_W, H, Dh)
    vg = v.reshape(B, rows, GRID_W, H, Dh)
    cols = jnp.arange(GRID_W)
    col_start = jnp.clip(cols - NA_KW // 2, 0, GRID_W - NA_KW)
    col_idx = col_start[:, None] + jnp.arange(NA_KW)[None, :]
    col_off = col_idx - cols[:, None] + (NA_KW - 1)
    scale = Dh ** -0.5

    def one_row(r):
        rs = jnp.clip(r - kh // 2, 0, rows - kh)
        q_r = lax.dynamic_index_in_dim(qg, r, axis=1, keepdims=False)
        k_rows = lax.dynamic_slice_in_dim(kg, rs, kh, axis=1)
        v_rows = lax.dynamic_slice_in_dim(vg, rs, kh, axis=1)
        k_win = k_rows[:, :, col_idx]
        v_win = v_rows[:, :, col_idx]
        row_off = rs + jnp.arange(kh) - r + (NA_KH - 1)
        bias = rpb[:, row_off][:, :, col_off].transpose(0, 2, 1, 3)
        s = jnp.einsum('bchd,bicjhd->bhcij', q_r, k_win,
                       preferred_element_type=jnp.float32) * scale
        s = s + bias[None].astype(jnp.float32)
        p = jax.nn.softmax(s.reshape(B, H, GRID_W, kh * NA_KW), axis=-1)
        p = p.reshape(B, H, GRID_W, kh, NA_KW).astype(v.dtype)
        return jnp.einsum('bhcij,bicjhd->bchd', p, v_win)

    o = lax.map(one_row, jnp.arange(rows))
    return o.transpose(1, 0, 2, 3, 4).reshape(B, S, H * Dh)

def attention_mixer(h, w_in, q_a_norm_w, kv_a_norm_w, w_q_b, w_kv_b, mla_q_norm_w,
                    mla_k_norm_w, na_q_norm_w, na_k_norm_w, na_rpb, w_out):
    B, S, _ = h.shape
    p = h @ w_in
    o1 = MLA_Q_LORA
    o2 = o1 + MLA_KV_LORA
    o3 = o2 + MLA_ROPE
    cq, ckv, k_pe, qkv_na = p[..., :o1], p[..., o1:o2], p[..., o2:o3], p[..., o3:]
    mla_out = mla_heads(cq, ckv, k_pe, q_a_norm_w, kv_a_norm_w, w_q_b, w_kv_b,
                        mla_q_norm_w, mla_k_norm_w)
    qkv = qkv_na.reshape(B, S, 3, NA_HEADS, NA_HD)
    q_na = rms_norm(qkv[:, :, 0], na_q_norm_w)
    k_na = rms_norm(qkv[:, :, 1], na_k_norm_w)
    na_out = neighbourhood_attention(q_na, k_na, qkv[:, :, 2], na_rpb)
    return jnp.concatenate([mla_out, na_out], axis=-1) @ w_out

def conformer_conv(h, pw1_w, pw1_b, dw_w, dw_b, ln_w, ln_b, pw2_w, pw2_b):
    a = h @ pw1_w + pw1_b
    g = a[..., :D_MODEL] * jax.nn.sigmoid(a[..., D_MODEL:])
    y = lax.conv_general_dilated(g, dw_w[:, None, :], window_strides=(1,),
                                 padding=[(CONV_W // 2, CONV_W // 2)],
                                 dimension_numbers=('NWC', 'WIO', 'NWC'),
                                 feature_group_count=D_MODEL) + dw_b
    y = jax.nn.silu(layer_norm(y, ln_w, ln_b))
    return y @ pw2_w + pw2_b

def moe_ffn(h, router_w, router_b, w_gate, w_up, w_down, ws_gate, ws_up, ws_down):
    B, S, D = h.shape
    T = B * S
    hf = h.reshape(T, D)
    scores = jax.nn.sigmoid(jnp.dot(hf.astype(jnp.float32), router_w.astype(jnp.float32)))
    sel = scores + router_b.astype(jnp.float32)
    grp = sel.reshape(T, N_GROUPS, N_EXPERTS // N_GROUPS)
    grp_score = lax.top_k(grp, 2)[0].sum(-1)
    _, gidx = lax.top_k(grp_score, TOPK_GROUPS)
    gmask = (gidx[..., None] == jnp.arange(N_GROUPS)).any(axis=-2)
    emask = jnp.repeat(gmask, N_EXPERTS // N_GROUPS, axis=-1)
    _, idx = lax.top_k(jnp.where(emask, sel, -jnp.inf), TOP_K)
    gates = jnp.take_along_axis(scores, idx, axis=-1)
    gates = gates / gates.sum(-1, keepdims=True) * ROUTED_SCALE

    A = T * TOP_K
    flat_e = idx.reshape(A)
    flat_tok = jnp.arange(A, dtype=jnp.int32) // TOP_K
    flat_g = gates.reshape(A)
    order = jnp.argsort(flat_e)
    se, stok, sg = flat_e[order], flat_tok[order], flat_g[order]
    counts = jnp.bincount(flat_e, length=N_EXPERTS)
    padded = (counts + MOE_BLOCK - 1) // MOE_BLOCK * MOE_BLOCK
    pend = jnp.cumsum(padded)
    pstart = pend - padded
    start = jnp.cumsum(counts) - counts
    dest = pstart[se] + jnp.arange(A, dtype=jnp.int32) - start[se]
    n_blocks = A // MOE_BLOCK + N_EXPERTS
    buf_tok = jnp.full((n_blocks * MOE_BLOCK,), T, jnp.int32).at[dest].set(stok)
    buf_g = jnp.zeros((n_blocks * MOE_BLOCK,), jnp.float32).at[dest].set(sg)
    blk_e = jnp.minimum(jnp.searchsorted(pend, jnp.arange(n_blocks) * MOE_BLOCK, side='right'),
                        N_EXPERTS - 1)
    h_pad = jnp.concatenate([hf, jnp.zeros((1, D), hf.dtype)], axis=0)

    def expert_block(y, blk):
        tok, g, e = blk
        xb = h_pad[tok]
        u = jax.nn.silu(xb @ w_gate[e]) * (xb @ w_up[e])
        out = u @ w_down[e]
        return y.at[tok].add(out * g[:, None].astype(out.dtype)), None

    y, _ = lax.scan(expert_block, jnp.zeros((T + 1, D), hf.dtype),
                    (buf_tok.reshape(n_blocks, MOE_BLOCK),
                     buf_g.reshape(n_blocks, MOE_BLOCK), blk_e))
    shared = (jax.nn.silu(hf @ ws_gate) * (hf @ ws_up)) @ ws_down
    return (y[:T] + shared).reshape(B, S, D)

def setup_inputs(seed: int = 0) -> dict:
    key = jax.random.key(seed)
    ks = iter(jax.random.split(key, 48))
    D = D_MODEL
    n_att = (DEPTH + 1) // 2
    n_conv = DEPTH // 2

    def nrm(shape, scale):
        return jax.random.normal(next(ks), shape, jnp.float32) * scale

    def gain(shape):
        return 1.0 + nrm(shape, 0.1)

    return {
        "x": nrm((BATCH, SEQ, D), 1.0),
        "c": nrm((BATCH, D), 1.0),
        "norm1_w": gain((DEPTH, D)),
        "norm2_w": gain((DEPTH, D)),
        "ada_w": nrm((DEPTH, D, 6 * D), 0.5 * D ** -0.5),
        "ada_b": nrm((DEPTH, 6 * D), 0.02),
        "w_in": nrm((n_att, D, IN_COLS), D ** -0.5),
        "q_a_norm_w": gain((n_att, MLA_Q_LORA)),
        "kv_a_norm_w": gain((n_att, MLA_KV_LORA)),
        "w_q_b": nrm((n_att, MLA_Q_LORA, MLA_HEADS * MLA_QK), MLA_Q_LORA ** -0.5),
        "w_kv_b": nrm((n_att, MLA_KV_LORA, MLA_HEADS * (MLA_NOPE + MLA_V)), MLA_KV_LORA ** -0.5),
        "mla_q_norm_w": gain((n_att, MLA_QK)),
        "mla_k_norm_w": gain((n_att, MLA_QK)),
        "na_q_norm_w": gain((n_att, NA_HD)),
        "na_k_norm_w": gain((n_att, NA_HD)),
        "na_rpb": nrm((n_att, NA_HEADS, 2 * NA_KH - 1, 2 * NA_KW - 1), 0.1),
        "w_out": nrm((n_att, MIX_WIDTH, D), MIX_WIDTH ** -0.5),
        "pw1_w": nrm((n_conv, D, 2 * D), D ** -0.5),
        "pw1_b": nrm((n_conv, 2 * D), 0.02),
        "dw_w": nrm((n_conv, CONV_W, D), CONV_W ** -0.5),
        "dw_b": nrm((n_conv, D), 0.02),
        "conv_ln_w": gain((n_conv, D)),
        "conv_ln_b": nrm((n_conv, D), 0.02),
        "pw2_w": nrm((n_conv, D, D), D ** -0.5),
        "pw2_b": nrm((n_conv, D), 0.02),
        "router_w": nrm((DEPTH, D, N_EXPERTS), D ** -0.5),
        "router_b": nrm((DEPTH, N_EXPERTS), 0.01),
        "exp_w_gate": nrm((DEPTH, N_EXPERTS, D, D_EXPERT), D ** -0.5),
        "exp_w_up": nrm((DEPTH, N_EXPERTS, D, D_EXPERT), D ** -0.5),
        "exp_w_down": nrm((DEPTH, N_EXPERTS, D_EXPERT, D), D_EXPERT ** -0.5),
        "sh_w_gate": nrm((DEPTH, D, D_SHARED), D ** -0.5),
        "sh_w_up": nrm((DEPTH, D, D_SHARED), D ** -0.5),
        "sh_w_down": nrm((DEPTH, D_SHARED, D), D_SHARED ** -0.5),
    }

def reference(x, c, norm1_w, norm2_w, ada_w, ada_b, w_in, q_a_norm_w, kv_a_norm_w,
              w_q_b, w_kv_b, mla_q_norm_w, mla_k_norm_w, na_q_norm_w, na_k_norm_w,
              na_rpb, w_out, pw1_w, pw1_b, dw_w, dw_b, conv_ln_w, conv_ln_b, pw2_w,
              pw2_b, router_w, router_b, exp_w_gate, exp_w_up, exp_w_down,
              sh_w_gate, sh_w_up, sh_w_down):
    c_act = jax.nn.silu(c)
    for l in range(DEPTH):
        mod = (c_act @ ada_w[l] + ada_b[l])[:, None, :]
        sh1, sc1, g1, sh2, sc2, g2 = jnp.split(mod, 6, axis=-1)
        h = rms_norm(x, norm1_w[l]) * (1 + sc1) + sh1
        i = l // 2
        if l % 2 == 0:
            mix = attention_mixer(h, w_in[i], q_a_norm_w[i], kv_a_norm_w[i], w_q_b[i],
                                  w_kv_b[i], mla_q_norm_w[i], mla_k_norm_w[i],
                                  na_q_norm_w[i], na_k_norm_w[i], na_rpb[i], w_out[i])
        else:
            mix = conformer_conv(h, pw1_w[i], pw1_b[i], dw_w[i], dw_b[i], conv_ln_w[i],
                                 conv_ln_b[i], pw2_w[i], pw2_b[i])
        x = x + g1 * mix
        h = rms_norm(x, norm2_w[l]) * (1 + sc2) + sh2
        x = x + g2 * moe_ffn(h, router_w[l], router_b[l], exp_w_gate[l], exp_w_up[l],
                             exp_w_down[l], sh_w_gate[l], sh_w_up[l], sh_w_down[l])
    return x


_drawn_inputs = setup_inputs


def setup_inputs(seed=0):
    import zlib

    import numpy as np

    out = dict(_drawn_inputs(seed))
    spreads = {}
    factors = {'q_a_norm_w': 2.861,
     'mla_q_norm_w': 2.894,
     'mla_k_norm_w': 2.871,
     'pw1_b': 4.246,
     'dw_b': 3.382,
     'conv_ln_b': 7.346,
     'pw2_b': 3.669}
    for name, (base, spread) in spreads.items():
        noise = np.random.default_rng([zlib.crc32(name.encode()), seed]).standard_normal(out[name].shape)
        drawn = base * np.exp(spread * noise) if base else spread * noise
        out[name] = __import__('jax').numpy.asarray(drawn.astype(out[name].dtype))
    for name, factor in factors.items():
        out[name] = (out[name] * factor).astype(out[name].dtype)
    return out
```

```python
from contextlib import ExitStack, contextmanager

import concourse.bass as bass
from concourse import mybir

P = 128
F32 = mybir.dt.float32
F32R = mybir.dt.float32r
I32 = mybir.dt.int32
ALU = mybir.AluOpType
ACT = mybir.ActivationFunctionType
AX = mybir.AxisListType.X

D = 1024
KC = D // P
T = 256
TT = T // P
EPS = 1e-6
Q_LORA, KV_LORA, ROPE = 256, 128, 32
HEADS, NOPE, HDV = 8, 64, 64
QK_W = NOPE + ROPE
IN_COLS = Q_LORA + KV_LORA + ROPE + 3 * HEADS * HDV
NA0 = Q_LORA + KV_LORA + ROPE
GRID_W, NA_KH, NA_KW = 64, 8, 16
ROWS = T // GRID_W
RPB_H, RPB_W = 2 * NA_KH - 1, 2 * NA_KW - 1
TOE = 2 * GRID_W - 1
CONV_W = 31
PAD = CONV_W // 2
E_N, FF, GROUPS, GROUPS_ON = 64, 256, 8, 4
PER_G = E_N // GROUPS
SCALE_R = 2.5
SLOTS = 64
TOP_K = 8
MAIN_PAIRS = E_N // 2
MAX_MORE = (T * TOP_K) // SLOTS
TAIL_STEPS = MAX_MORE // 4
NX = MAX_MORE + 2
NB = E_N + NX
SLOT_W = KC * 2 * FF + 2 * D
ADA_N = 6 * D // 8
NEG = -1.0e30

C_ID = 0
C_TRI = C_ID + P
C_STRICT = C_TRI + P
C_SLOT = C_STRICT + E_N
C_BLK = C_SLOT + SLOTS
C_GLT = C_BLK + NX
C_EIDX = C_GLT + GROUPS * GROUPS
C_COS = C_EIDX + 1
C_SIN = C_COS + TT * ROPE
C_WIN = C_SIN + TT * ROPE
C_N = C_WIN + GRID_W


class Chain:

    def __init__(self, eng, sem):
        self.eng, self.sem, self.n = eng, sem, 0

    def link(self, ins):
        self.n += 1
        ins.then_inc(self.sem, 1)
        self.eng.wait_ge(self.sem, self.n)


def build_encoder(nc, x, c, norm1_w, norm2_w, ada_w, ada_b, w_in, q_a_norm_w, kv_a_norm_w,
                  w_q_b, w_kv_b, mla_q_norm_w, mla_k_norm_w, na_q_norm_w, na_k_norm_w,
                  na_rpb, w_out, pw1_w, pw1_b, dw_w, dw_b, conv_ln_w, conv_ln_b, pw2_w,
                  pw2_b, router_w, router_b, exp_w_gate, exp_w_up, exp_w_down,
                  sh_w_gate, sh_w_up, sh_w_down, consts, out):
    ctx = ExitStack()
    with ctx:
        def sb(name, shape, dt=F32):
            return ctx.enter_context(nc.sbuf_tensor(name, shape, dt))

        banks = [ctx.enter_context(nc.psum_tensor(f"bank{i}", [P, 512], F32)) for i in range(8)]

        con = sb("con", [P, C_N])
        ident = con[:, C_ID:C_ID + P]
        X = sb("X", [P, TT, D])
        hT = sb("hT", [P, KC, T])
        ring = sb("ring", [P, 4 * SLOT_W])
        W = sb("W", [P, 15232])
        H_hi = sb("H_hi", [P, TT, D], F32R)
        H_lo = sb("H_lo", [P, TT, D], F32R)
        O_hi = sb("O_hi", [P, D], F32R)
        O_lo = sb("O_lo", [P, D], F32R)
        pick = sb("pick", [P, 2, TT, P], F32R)
        zeros = sb("zeros", [P, P], F32R)
        pickT = sb("pickT", [P, T], F32R)
        AB = sb("AB", [P, 2, 2, 2, KC])
        gate_bc = sb("gate_bc", [P, D])
        eps_half = sb("eps_half", [P, 32])
        small = sb("small", [P, 224])
        ids = sb("ids", [1, NX + 2], I32)

        phase_sems = []

        def sem(name):
            s = sem_stack[-1].enter_context(nc.semaphore(name))
            phase_sems.append(s)
            return s

        sem_stack = [ctx]

        @contextmanager
        def phase():
            stack = ExitStack()
            sem_stack.append(stack)
            phase_sems.clear()
            yield
            with nc.Block() as block:
                @block.gpsimd
                def _(pool):
                    for s in phase_sems:
                        pool.sem_clear(s)
            phase_sems.clear()
            stack.close()
            sem_stack.pop()

        wpos = [0]

        def carve(n):
            a = wpos[0]
            wpos[0] += n
            assert wpos[0] <= 15232
            return W[:, a:a + n]

        def slot(s):
            return ring[:, s * SLOT_W:(s + 1) * SLOT_W]

        mod_dram = nc.dram_tensor("mod_scratch", [2, 6 * D], F32).ap()
        toe_dram = nc.dram_tensor("toeplitz_scratch", [HEADS * RPB_H, GRID_W, GRID_W], F32).ap()

        def pk(row):
            return row.rearrange("(p k) -> p k", k=KC)

        def norm_sems(tag):
            return {k: sem(f"{tag}_{k}") for k in
                    ("squared", "mean", "rstd", "xn", "turned", "h_dve", "h_act")}

        XN = W[:, 0:TT * D].rearrange("p (t d) -> p t d", t=TT)
        ss = small[:, 0:2]
        ms = small[:, 2:4]
        rstd = small[:, 4:6]

        def norm_act(act, s, l, which):
            for t in range(TT):
                act.activation(XN[:, t, :], X[:, t, :], ACT.Square,
                               accum_out=ss[:, t:t + 1]).then_inc(s["squared"], 1)
            for j in (1, 3):
                act.wait_ge(s["turned"], j + 1)
                for k in (2 * j, 2 * j + 1):
                    act.activation(hT[:, k, :], banks[j][:, (k % 2) * T:(k % 2 + 1) * T], ACT.Identity,
                                   bias=AB[:, l, which, 1, k:k + 1],
                                   scale=AB[:, l, which, 0, k:k + 1]).then_inc(s["h_act"], 1)

        def norm_pool(pool, s):
            pool.wait_ge(s["mean"], 1)
            pool.tensor_tensor(rstd, ms, eps_half[:, 0:2], ALU.pow).then_inc(s["rstd"], 1)

        def norm_dve(dve, s, l, which):
            dve.wait_ge(s["squared"], 2)
            dve.tensor_scalar(ms, ss, 1.0 / D, EPS, ALU.mult, ALU.add).then_inc(s["mean"], 1)
            dve.wait_ge(s["rstd"], 1)
            for t in range(TT):
                dve.tensor_scalar(XN[:, t, :], X[:, t, :], rstd[:, t:t + 1], None,
                                  ALU.mult).then_inc(s["xn"], 1)
            for j in (0, 2):
                dve.wait_ge(s["turned"], j + 1)
                for k in (2 * j, 2 * j + 1):
                    dve.tensor_scalar(hT[:, k, :], banks[j][:, (k % 2) * T:(k % 2 + 1) * T],
                                      AB[:, l, which, 0, k:k + 1], AB[:, l, which, 1, k:k + 1],
                                      ALU.mult, ALU.add).then_inc(s["h_dve"], 1)

        def norm_pe(pe, s):
            pe.wait_ge(s["xn"], 2)
            for k in range(KC):
                for t in range(TT):
                    last = pe.transpose(banks[k // 2][:, (k % 2) * T + t * P:(k % 2) * T + (t + 1) * P],
                                        XN[:, t, k::KC], ident)
                if k % 2:
                    last.then_inc(s["turned"], 1)

        def wait_h(eng, s):
            eng.wait_ge(s["h_dve"], 4)
            eng.wait_ge(s["h_act"], 4)

        c_in, con_in, x_in, vec_in = sem("c_in"), sem("con_in"), sem("x_in"), sem("vec_in")
        c_silu, c_rep_ready = sem("c_silu"), sem("c_rep_ready")
        ada_in = [sem(f"ada_in{i}") for i in range(4)]
        ada_done, row_copied = sem("ada_done"), sem("row_copied")
        row_stored = [sem("row_stored0"), sem("row_stored1")]
        toe_zeroed, toe_in, toe_stored = sem("toe_zeroed"), sem("toe_in"), sem("toe_stored")
        mod_in = sem("mod_in")
        ab_step = sem("ab_step")
        vecs_in = sem("vecs_in")
        ccol = small[:, 8:16]
        csil = small[:, 16:24]
        c_rep = W[:, 0:KC * 64].rearrange("p (k m) -> p k m", k=KC)
        rows = W[:, 512:512 + 768].rearrange("p (b n) -> p b n", b=2)
        toe = W[0:HEADS * RPB_H, 1280:1280 + TOE + 1]
        skew = W[0:HEADS * RPB_H, 2048:2048 + GRID_W * GRID_W].rearrange("p (c k) -> p c k", c=GRID_W)
        toe_skewed = sem("toe_skewed")
        nw = W[:, 1408:1408 + 32].rearrange("p (w l k) -> p w l k", w=2, l=2)
        bcol = W[:, 1440:1440 + 96].rearrange("p (l j k) -> p l j k", l=2, j=6)
        mcol = W[:, 1536:1536 + 96].rearrange("p (l j k) -> p l j k", l=2, j=6)
        PIECES = 6 * D // ADA_N
        HALF = ADA_N // 2

        with nc.Block() as block:
            @block.sync
            def _(sp):
                sp.dma_start(ccol, pk(c[0, :])).then_inc(c_in, 16)
                sp.dma_start(con[:, :], consts).then_inc(con_in, 16)
                for l in range(2):
                    src = ada_w[l].rearrange("(p k) (h s n) -> p k h s n", k=KC, s=4, n=ADA_N)
                    for i in range(2):
                        for s in range(4):
                            if 2 * l + i:
                                sp.wait_ge(ada_done, 8 * l + i * 4 + s - 3)
                            dst = slot(s).rearrange("p (k n) -> p k n", k=KC)
                            sp.dma_start(dst, src[:, :, bass.ds(i, 1), s, :].rearrange("p k o n -> p k (o n)")
                                         ).then_inc(ada_in[s], 16)
                sp.dma_start(X[:, :, :], x[0].rearrange("(t p) d -> p t d", p=P)).then_inc(x_in, 16)
                sp.wait_ge(x_in, 16)
                sp.wait_ge(toe_stored, 16)

            @block.gpsimd
            def _(pool):
                pool.memset(eps_half[:, :], -0.5)
                pool.memset(toe, 0.0).then_inc(toe_zeroed, 1)
                pool.wait_ge(toe_zeroed, 1)
                pool.dma_start(toe[:, GRID_W - NA_KW:GRID_W - NA_KW + RPB_W],
                               na_rpb[0].rearrange("h i j -> (h i) j")).then_inc(toe_in, 16)
                pool.wait_ge(toe_in, 16)
                last = toe[:, GRID_W - 1:TOE]
                by_query = bass.AP(tensor=last.tensor, offset=last.offset,
                                   ap=[list(last.ap[0]), [-1, GRID_W], [1, GRID_W]])
                pool.tensor_copy(skew, by_query).then_inc(toe_skewed, 1)
                pool.wait_ge(toe_skewed, 1)
                pool.dma_start(toe_dram, skew).then_inc(toe_stored, 16)

            @block.scalar
            def _(act):
                act.wait_ge(c_in, 16)
                act.activation(csil, ccol, ACT.Silu).then_inc(c_silu, 1)
                with nc.allow_non_contiguous_dma("vectors by (p, k)"):
                    act.dma_start(nw[:, 0], norm1_w.rearrange("l (p k) -> p l k", k=KC)).then_inc(vec_in, 16)
                    act.dma_start(nw[:, 1], norm2_w.rearrange("l (p k) -> p l k", k=KC)).then_inc(vec_in, 16)
                    for l in range(2):
                        act.dma_start(bcol[:, l], ada_b[l].rearrange("(j p k) -> p j k", p=P, k=KC)
                                      ).then_inc(vec_in, 16)
                for l in range(2):
                    dst = mod_dram[l].rearrange("(i s q n) -> i s q n", i=2, s=4, q=2)
                    for i in range(2):
                        for s in range(4):
                            act.wait_ge(row_copied, i * 4 + (8 * l + s + 1))
                            act.dma_start(dst[bass.ds(i, 1), s].rearrange("o q n -> (o q) n"),
                                          rows[0:65:64, s % 2, :]).then_inc(row_stored[s % 2], 16)
                for u in range(2):
                    act.wait_ge(row_stored[u], 16 * PIECES)
                with nc.allow_non_contiguous_dma("vectors by (p, k)"):
                    for l in range(2):
                        act.dma_start(mcol[:, l], mod_dram[l].rearrange("(j p k) -> p j k", p=P, k=KC)
                                      ).then_inc(mod_in, 16)

            @block.vector
            def _(dve):
                own = Chain(dve, ab_step)
                dve.wait_ge(c_silu, 1)
                dve.tensor_copy(c_rep, csil.unsqueeze(2).broadcast_to([P, KC, 64])).then_inc(c_rep_ready, 1)
                for l in range(2):
                    for i in range(2):
                        for s in range(4):
                            dve.wait_ge(ada_done, i * 4 + (8 * l + s + 1))
                            n_before = 4 * l + s // 2
                            if i * 32 + 16 * n_before:
                                dve.wait_ge(row_stored[s % 2], i * 32 + 16 * n_before)
                            dve.tensor_copy(rows[:, s % 2, :], banks[s % 2][:, 0:HALF]).then_inc(row_copied, 1)
                dve.wait_ge(vec_in, 64)
                dve.wait_ge(mod_in, 32)
                own.link(dve.tensor_tensor(mcol, mcol, bcol, ALU.add))
                for w in range(2):
                    own.link(dve.tensor_scalar(AB[:, :, w, 0, :], mcol[:, :, 3 * w + 1, :], 1.0, None, ALU.add))
                    own.link(dve.tensor_tensor(AB[:, :, w, 0, :], AB[:, :, w, 0, :], nw[:, w], ALU.mult))
                    own.link(dve.tensor_copy(AB[:, :, w, 1, :], mcol[:, :, 3 * w, :]))

            @block.tensor
            def _(pe):
                pe.wait_ge(c_rep_ready, 1)
                for l in range(2):
                    for i in range(2):
                        for s in range(4):
                            pe.wait_ge(ada_in[s], i * 16 + 16 * (2 * l + 1))
                            if 8 * l + i * 4 + s >= 2:
                                pe.wait_ge(row_copied, i * 4 + (8 * l + s - 1))
                            wv = slot(s).rearrange("p (k q n) -> p k q n", k=KC, q=2)
                            for k in range(KC):
                                for q in range(2):
                                    last = pe.matmul(banks[s % 2][64 * q:64 * q + 64, 0:HALF], c_rep[:, k, :],
                                                     wv[:, k, q, :], start=(k == 0), stop=(k == KC - 1))
                            last.then_inc(ada_done, 1)

        def attention():
            ns = norm_sems("attn_norm")
            win_in, wqkv_in, wout_in = sem("win_in"), sem("wqkv_in"), sem("wout_in")
            bias_in, bias_ready, gate_in, gate_ready = sem("bias_in"), sem("bias_ready"), sem("gate_in"), sem("gate_ready")
            proj_done, proj_dve, proj_act = sem("proj_done"), sem("proj_dve"), sem("proj_act")
            lat_sq, lat_ms, lat_rstd, lat_n, lat_T, cT_dve, cT_act = (
                sem(n) for n in ("lat_sq", "lat_ms", "lat_rstd", "lat_n", "lat_T", "cT_dve", "cT_act"))
            qkv_done, q_out, kv_out = sem("qkv_done"), sem("q_out"), sem("kv_out")
            hd_sq, hd_ms, hd_rstd, hd_ready, hdT, hdT_dve, hdT_act = (
                sem(n) for n in ("hd_sq", "hd_ms", "hd_rstd", "hd_ready", "hdT", "hdT_dve", "hdT_act"))
            s_done, nm_ready, exp_done, pT_done, pT_ready, pv_done = (
                sem(n) for n in ("s_done", "nm_ready", "exp_done", "pT_done", "pT_ready", "pv_done"))
            cat_ready, catT_done, catT_dve, catT_act, mix_done = (
                sem(n) for n in ("cat_ready", "catT_done", "catT_dve", "catT_act", "mix_done"))
            at_dve = sem("at_dve")

            wpos[0] = 0
            proj = carve(TT * IN_COLS).rearrange("p (t n) -> p t n", t=TT)
            CQN = carve(TT * 384).rearrange("p (t n) -> p t n", t=TT)
            cT = carve(3 * T).rearrange("p (c t) -> p c t", c=3)
            QK = carve(TT * 16 * QK_W).rearrange("p (t r w) -> p t r w", t=TT, r=16)
            V = carve(TT * 512).rearrange("p (t h w) -> p t h w", t=TT, h=HEADS)
            SQ = carve(16 * QK_W)
            CAT = carve(TT * D).rearrange("p (t d) -> p t d", t=TT)
            turned_at = carve(1024)
            rope_a = turned_at[:, 0:512].rearrange("p (r w) -> p r w", r=16)
            rope_b = turned_at[:, 512:1024].rearrange("p (r w) -> p r w", r=16)
            qkw = carve(2 * QK_W).rearrange("p (a w) -> p a w", a=2)
            naw = carve(2 * HDV).rearrange("p (a w) -> p a w", a=2)
            qaw = carve(Q_LORA)
            kvaw = carve(KV_LORA)
            Pr = W[:, TT * IN_COLS:TT * IN_COLS + 1536]
            assert TT * 384 + 3 * T == 1536
            prob = Pr[:, 0:1024].rearrange("p (b q k) -> p b q k", b=2, q=2)
            logit = SQ[:, 0:1024].rearrange("p (b q k) -> p b q k", b=2, q=2)
            probT = turned_at.rearrange("p (b c q) -> p b c q", b=2, c=2)
            WIN = ring[:, 0:KC * IN_COLS].rearrange("p (k n) -> p k n", k=KC)
            o = KC * IN_COLS
            WQB = ring[:, o:o + 2 * 768].rearrange("p (k n) -> p k n", k=2)
            WKVB = ring[:, o + 1536:o + 1536 + D]
            assert o + 1536 + D <= 3 * SLOT_W
            WOUT = ring[:, 0:KC * D].rearrange("p (k n) -> p k n", k=KC)
            BIAS = ring[:, KC * D:KC * D + TT * HEADS * T].rearrange("p (t h k) -> p t h k", t=TT, h=HEADS)
            assert KC * D + TT * HEADS * T <= KC * IN_COLS
            QKT = slot(3)[0:QK_W, 0:16 * T].rearrange("p (r t) -> p r t", r=16)
            NT = slot(3)[:, 16 * T:24 * T].rearrange("p (r t) -> p r t", r=8)
            catT = hT
            lat_ss = small[:, 8:12].rearrange("p (t a) -> p t a", t=2)
            lat_m = small[:, 12:16].rearrange("p (t a) -> p t a", t=2)
            lat_r = small[:, 16:20].rearrange("p (t a) -> p t a", t=2)
            hd_ss, hd_m, hd_r = small[:, 32:48], small[:, 48:64], small[:, 64:80]
            mx = small[:, 80:112].rearrange("p (g q) -> p g q", q=2)
            nmx = small[:, 112:144].rearrange("p (g q) -> p g q", q=2)
            sums = small[:, 144:176].rearrange("p (q g) -> p q g", q=2)
            rsum = small[:, 176:208].rearrange("p (q g) -> p q g", q=2)
            PROJ_COLS = [(0, NA0)] + [(NA0 + 512 * i, 512) for i in range(3)]
            proj_bank = [[4, 5, 6, 7], [0, 1, 2, 3]]
            q_bank = [[6, 7], [2, 3]]
            kv_bank = [[0, 1], [4, 5]]
            SC_MLA, SC_NA = QK_W ** -0.5, HDV ** -0.5
            toe_v = toe_dram.rearrange("(h i) c k -> h i c k", h=HEADS)

            def head_norm_steps():
                for t in range(TT):
                    yield t, QK[:, t], QK_W, qkw, "mla"
                for t in range(TT):
                    yield t, proj[:, t, NA0:NA0 + 1024].rearrange("p (r w) -> p r w", r=16), HDV, naw, "na"

            with nc.Block() as block:
                @block.sync
                def _(sp):
                    wv = w_in[0].rearrange("(p k) n -> p k n", k=KC)
                    sp.dma_start(WIN[:, 0:4, :], wv[:, 0:4, :]).then_inc(win_in, 16)
                    sp.dma_start(WIN[:, 4:8, :], wv[:, 4:8, :]).then_inc(win_in, 16)
                    sp.dma_start(WQB, w_q_b[0].rearrange("(k p) n -> p k n", k=2)).then_inc(wqkv_in, 16)
                    sp.dma_start(WKVB, w_kv_b[0]).then_inc(wqkv_in, 16)
                    sp.wait_ge(proj_done, 8)
                    sp.dma_start(WOUT, w_out[0].rearrange("(k p) n -> p k n", k=KC)).then_inc(wout_in, 16)
                    for t in range(TT):
                        for r2 in range(2):
                            r = 2 * t + r2
                            for h in range(HEADS):
                                src = toe_v[h, NA_KH - 1 - r:NA_KH - 1 - r + ROWS].rearrange("r c k -> c r k")
                                sp.dma_start(BIAS[64 * r2:64 * r2 + 64, t, h, :].rearrange("p (r c) -> p r c", r=ROWS),
                                             src).then_inc(bias_in, 16)
                    sp.wait_ge(bias_in, 16 * 2 * TT * HEADS)

                @block.gpsimd
                def _(pool):
                    norm_pool(pool, ns)
                    with nc.allow_non_contiguous_dma("rows for every partition"):
                        pool.dma_start(qkw[:, 0], mla_q_norm_w[0].partition_broadcast(P)).then_inc(vecs_in, 16)
                        pool.dma_start(qkw[:, 1], mla_k_norm_w[0].partition_broadcast(P)).then_inc(vecs_in, 16)
                        pool.dma_start(naw[:, 0], na_q_norm_w[0].partition_broadcast(P)).then_inc(vecs_in, 16)
                        pool.dma_start(naw[:, 1], na_k_norm_w[0].partition_broadcast(P)).then_inc(vecs_in, 16)
                        pool.dma_start(qaw, q_a_norm_w[0].partition_broadcast(P)).then_inc(vecs_in, 16)
                        pool.dma_start(kvaw, kv_a_norm_w[0].partition_broadcast(P)).then_inc(vecs_in, 16)
                    pool.wait_ge(lat_ms, 1)
                    pool.tensor_tensor(lat_r, lat_m, eps_half[:, 0:4].rearrange("p (t a) -> p t a", t=2),
                                       ALU.pow).then_inc(lat_rstd, 1)
                    for n in range(4):
                        pool.wait_ge(hd_ms, n + 1)
                        pool.tensor_tensor(hd_r, hd_m, eps_half[:, 0:16], ALU.pow).then_inc(hd_rstd, 1)
                    pool.wait_ge(bias_in, 16 * 2 * TT * HEADS)
                    for t in range(TT):
                        v = BIAS[:, t].rearrange("p h (r c) -> p (h r) c", r=ROWS)
                        pool.tensor_tensor(v, v, con[:, C_WIN:C_WIN + GRID_W].unsqueeze(1)
                                           .broadcast_to([P, HEADS * ROWS, GRID_W]), ALU.add).then_inc(bias_ready, 1)

                @block.scalar
                def _(act):
                    with nc.allow_non_contiguous_dma("rows for every partition"):
                        act.dma_start(gate_bc[:, :], mod_dram[0, 2 * D:3 * D].partition_broadcast(P)).then_inc(gate_in, 16)
                    norm_act(act, ns, 0, 0)
                    for t in range(TT):
                        for n in (1, 3):
                            act.wait_ge(proj_done, 4 * t + n + 1)
                            c0, w = PROJ_COLS[n]
                            act.copy(proj[:, t, c0:c0 + w], banks[proj_bank[t][n]][:, 0:w]).then_inc(proj_act, 1)
                    for t in range(TT):
                        act.wait_ge(proj_dve, 2 * t + 1)
                        act.activation(SQ[:, 0:Q_LORA] if t == 0 else SQ[:, 512:512 + Q_LORA], proj[:, t, 0:Q_LORA],
                                       ACT.Square, accum_out=lat_ss[:, t, 0:1]).then_inc(lat_sq, 1)
                        act.activation(SQ[:, 256:384] if t == 0 else SQ[:, 768:896], proj[:, t, Q_LORA:Q_LORA + KV_LORA],
                                       ACT.Square, accum_out=lat_ss[:, t, 1:2]).then_inc(lat_sq, 1)
                    act.wait_ge(lat_T, 2)
                    act.copy(cT[:, 2, :], banks[5][:, 0:T]).then_inc(cT_act, 1)
                    for t in range(TT):
                        for b in range(2):
                            act.wait_ge(qkv_done, 4 * t + 3 + b)
                            v = banks[kv_bank[t][b]][:, :].rearrange("p (h w) -> p h w", h=4)
                            act.copy(QK[:, t, 8 + 4 * b:12 + 4 * b, 0:NOPE], v[:, :, 0:NOPE]).then_inc(kv_out, 1)
                            act.copy(V[:, t, 4 * b:4 * b + 4, :], v[:, :, NOPE:NOPE + HDV]).then_inc(kv_out, 1)
                    for n, (t, v, w, _, kind) in enumerate(head_norm_steps()):
                        if kind == "mla":
                            act.wait_ge(q_out, 3 * (t + 1))
                            act.wait_ge(kv_out, 4 * (t + 1))
                        else:
                            act.wait_ge(proj_dve, 4)
                        if n:
                            act.wait_ge(hd_ms, n)
                        act.activation(SQ[:, 0:16 * w].rearrange("p (r w) -> p r w", r=16), v, ACT.Square
                                       ).then_inc(hd_sq, 1)
                    for g in range(1, 12, 2):
                        act.wait_ge(hdT, g + 1)
                        if g < 8:
                            act.copy(QKT[:, 2 * g:2 * g + 2, :], banks[g][0:QK_W, :].rearrange("p (r t) -> p r t", r=2)
                                     ).then_inc(hdT_act, 1)
                        else:
                            act.copy(NT[:, 2 * (g - 8):2 * (g - 8) + 2, :],
                                     banks[g % 8][:, :].rearrange("p (r t) -> p r t", r=2)).then_inc(hdT_act, 1)

                    def turned(g):
                        act.wait_ge(pT_done, g + 1)
                        if g >= 2:
                            act.wait_ge(pv_done, g - 1)
                        act.copy(probT[:, g % 2], banks[2 + g % 2][:, :].rearrange("p (c q) -> p c q", c=2)
                                 ).then_inc(pT_ready, 1)

                    for g in range(16):
                        act.wait_ge(nm_ready, g + 1)
                        if g >= 2:
                            act.wait_ge(pT_done, g - 1)
                        for q in range(2):
                            src = banks[g % 2][:, q * T:(q + 1) * T] if g < 8 else logit[:, g % 2, q, :]
                            last = act.activation(prob[:, g % 2, q, :], src, ACT.Exp, bias=nmx[:, g, q:q + 1],
                                                  scale=SC_MLA if g < 8 else 1.0, accum_out=sums[:, q, g:g + 1])
                        last.then_inc(exp_done, 1)
                        if g:
                            turned(g - 1)
                    turned(15)
                    for j in (1, 3):
                        act.wait_ge(catT_done, j + 1)
                        act.copy(catT[:, 2 * j:2 * j + 2, :], banks[j][:, :].rearrange("p (k t) -> p k t", k=2)
                                 ).then_inc(catT_act, 1)
                    act.wait_ge(pv_done, 16)
                    act.dma_start(W[:, 0:D], ada_b[0, 2 * D:3 * D].partition_broadcast(P)).then_inc(gate_in, 16)

                @block.vector
                def _(dve):
                    own = Chain(dve, at_dve)
                    norm_dve(dve, ns, 0, 0)
                    for t in range(TT):
                        for n in (0, 2):
                            dve.wait_ge(proj_done, 4 * t + n + 1)
                            c0, w = PROJ_COLS[n]
                            if t == 0 and n == 0:
                                dve.wait_ge(ns["turned"], 4)
                            dve.tensor_copy(proj[:, t, c0:c0 + w], banks[proj_bank[t][n]][:, 0:w]).then_inc(proj_dve, 1)
                    dve.wait_ge(lat_sq, 4)
                    own.link(dve.tensor_scalar(lat_m[:, :, 0], lat_ss[:, :, 0], 1.0 / Q_LORA, EPS, ALU.mult, ALU.add))
                    dve.tensor_scalar(lat_m[:, :, 1], lat_ss[:, :, 1], 1.0 / KV_LORA, EPS, ALU.mult,
                                      ALU.add).then_inc(lat_ms, 1)
                    dve.wait_ge(lat_rstd, 1)
                    dve.wait_ge(vecs_in, 96)
                    for t in range(TT):
                        dve.scalar_tensor_tensor(CQN[:, t, 0:Q_LORA], proj[:, t, 0:Q_LORA], lat_r[:, t, 0:1], qaw,
                                                 ALU.mult, ALU.mult)
                        dve.scalar_tensor_tensor(CQN[:, t, Q_LORA:384], proj[:, t, Q_LORA:384], lat_r[:, t, 1:2], kvaw,
                                                 ALU.mult, ALU.mult).then_inc(lat_n, 1)
                    dve.wait_ge(lat_T, 1)
                    dve.tensor_copy(cT[:, 0:2, :], banks[4][:, :].rearrange("p (c t) -> p c t", c=2)).then_inc(cT_dve, 1)
                    for t in range(TT):
                        qf = QK[:, t, 0:8, :].rearrange("p r w -> p (r w)")
                        for b, w in ((0, 512), (1, 256)):
                            dve.wait_ge(qkv_done, 4 * t + 1 + b)
                            dve.tensor_copy(qf[:, 512 * b:512 * b + w], banks[q_bank[t][b]][:, 0:w]).then_inc(q_out, 1)
                        dve.tensor_copy(QK[:, t, 8:16, NOPE:QK_W],
                                        proj[:, t, 384:NA0].unsqueeze(1).broadcast_to([P, 8, ROPE])).then_inc(q_out, 1)
                    dve.wait_ge(con_in, 16)
                    for n, (t, v, w, wt, kind) in enumerate(head_norm_steps()):
                        dve.wait_ge(hd_sq, n + 1)
                        own.link(dve.tensor_reduce(hd_ss, SQ[:, 0:16 * w].rearrange("p (r w) -> p r w", r=16), AX, ALU.add))
                        dve.tensor_scalar(hd_m, hd_ss, 1.0 / w, EPS, ALU.mult, ALU.add).then_inc(hd_ms, 1)
                        dve.wait_ge(hd_rstd, n + 1)
                        if kind == "na":
                            dve.wait_ge(proj_act, 4)
                        own.link(dve.tensor_tensor(v, v, hd_r.unsqueeze(2).broadcast_to([P, 16, w]), ALU.mult))
                        v4 = v.rearrange("p (a r) w -> p a r w", a=2)
                        last = dve.tensor_tensor(v4, v4, wt.unsqueeze(2).broadcast_to([P, 2, 8, w]), ALU.mult)
                        if kind == "mla":
                            own.link(last)
                            co = con[:, C_COS + t * ROPE:C_COS + (t + 1) * ROPE]
                            si = con[:, C_SIN + t * ROPE:C_SIN + (t + 1) * ROPE]
                            h2 = ROPE // 2
                            tail = v[:, :, NOPE:QK_W]
                            dve.tensor_tensor(rope_a, tail, co.unsqueeze(1).broadcast_to([P, 16, ROPE]), ALU.mult)
                            dve.tensor_tensor(rope_b[:, :, 0:h2], tail[:, :, h2:ROPE],
                                              si[:, 0:h2].unsqueeze(1).broadcast_to([P, 16, h2]), ALU.mult)
                            own.link(dve.tensor_tensor(rope_b[:, :, h2:ROPE], tail[:, :, 0:h2],
                                                       si[:, h2:ROPE].unsqueeze(1).broadcast_to([P, 16, h2]), ALU.mult))
                            last = dve.tensor_tensor(tail, rope_a, rope_b, ALU.add)
                        last.then_inc(hd_ready, 1)
                    for g in range(0, 12, 2):
                        dve.wait_ge(hdT, g + 1)
                        if g < 8:
                            dve.tensor_copy(QKT[:, 2 * g:2 * g + 2, :],
                                            banks[g][0:QK_W, :].rearrange("p (r t) -> p r t", r=2)).then_inc(hdT_dve, 1)
                        else:
                            dve.tensor_copy(NT[:, 2 * (g - 8):2 * (g - 8) + 2, :],
                                            banks[g % 8][:, :].rearrange("p (r t) -> p r t", r=2)).then_inc(hdT_dve, 1)

                    def heads_out(kind):
                        dve.wait_ge(pv_done, 8 * (kind + 1))
                        own.link(dve.reciprocal(rsum[:, :, 8 * kind:8 * kind + 8], sums[:, :, 8 * kind:8 * kind + 8]))
                        for q in range(2):
                            dve.tensor_tensor(
                                CAT[:, q, 512 * kind:512 * kind + 512].rearrange("p (h w) -> p h w", h=8),
                                banks[4 + 2 * q + kind][:, :].rearrange("p (h w) -> p h w", h=8),
                                rsum[:, q, 8 * kind:8 * kind + 8].unsqueeze(2).broadcast_to([P, 8, HDV]),
                                ALU.mult).then_inc(cat_ready, 1)

                    for g in range(16):
                        dve.wait_ge(s_done, g + 1)
                        sv = banks[g % 2][:, :].rearrange("p (q k) -> p q k", q=2)
                        if g < 8:
                            own.link(dve.tensor_reduce(mx[:, g], sv, AX, ALU.max))
                            dve.tensor_scalar(nmx[:, g], mx[:, g], -SC_MLA, None, ALU.mult).then_inc(nm_ready, 1)
                        else:
                            if g == 8:
                                dve.wait_ge(bias_ready, 2)
                            else:
                                dve.wait_ge(exp_done, g - 1)
                            own.link(dve.scalar_tensor_tensor(logit[:, g % 2], sv, SC_NA, BIAS[:, :, g - 8, :],
                                                              ALU.mult, ALU.add))
                            own.link(dve.tensor_reduce(mx[:, g], logit[:, g % 2], AX, ALU.max))
                            dve.tensor_scalar(nmx[:, g], mx[:, g], -1.0, None, ALU.mult).then_inc(nm_ready, 1)
                        if g == 10:
                            heads_out(0)
                    heads_out(1)
                    for j in (0, 2):
                        dve.wait_ge(catT_done, j + 1)
                        dve.tensor_copy(catT[:, 2 * j:2 * j + 2, :], banks[j][:, :].rearrange("p (k t) -> p k t", k=2)
                                        ).then_inc(catT_dve, 1)
                    dve.wait_ge(gate_in, 32)
                    own.link(dve.tensor_tensor(gate_bc[:, :], gate_bc[:, :], W[:, 0:D], ALU.add))
                    for t in range(TT):
                        for h in range(2):
                            dve.wait_ge(mix_done, 2 * t + h + 1)
                            cols = slice(512 * h, 512 * h + 512)
                            tmp = W[:, D + 512 * (2 * t + h):D + 512 * (2 * t + h + 1)]
                            own.link(dve.tensor_tensor(tmp, banks[4 + 2 * t + h][:, :], gate_bc[:, cols], ALU.mult))
                            dve.tensor_tensor(X[:, t, cols], X[:, t, cols], tmp, ALU.add)

                @block.tensor
                def _(pe):
                    norm_pe(pe, ns)
                    wait_h(pe, ns)
                    pe.wait_ge(win_in, 32)
                    for t in range(TT):
                        for n, (c0, w) in enumerate(PROJ_COLS):
                            for k in range(KC):
                                last = pe.matmul(banks[proj_bank[t][n]][:, 0:w], hT[:, k, t * P:(t + 1) * P],
                                                 WIN[:, k, c0:c0 + w], start=(k == 0), stop=(k == KC - 1))
                            last.then_inc(proj_done, 1)
                    pe.wait_ge(proj_act, 1)
                    for t in range(TT):
                        pe.wait_ge(lat_n, t + 1)
                        for ch in range(2):
                            last = pe.transpose(banks[4][:, ch * T + t * P:ch * T + (t + 1) * P],
                                                CQN[:, t, ch * P:(ch + 1) * P], ident)
                    last.then_inc(lat_T, 1)
                    for t in range(TT):
                        last = pe.transpose(banks[5][:, t * P:(t + 1) * P], CQN[:, t, 2 * P:3 * P], ident)
                    last.then_inc(lat_T, 1)
                    pe.wait_ge(wqkv_in, 32)
                    pe.wait_ge(cT_dve, 1)
                    pe.wait_ge(cT_act, 1)
                    pe.wait_ge(proj_dve, 4)
                    pe.wait_ge(proj_act, 4)
                    for t in range(TT):
                        for b, w in ((0, 512), (1, 256)):
                            for k in range(2):
                                last = pe.matmul(banks[q_bank[t][b]][:, 0:w], cT[:, k, t * P:(t + 1) * P],
                                                 WQB[:, k, 512 * b:512 * b + w], start=(k == 0), stop=(k == 1))
                            last.then_inc(qkv_done, 1)
                        for b in range(2):
                            pe.matmul(banks[kv_bank[t][b]][:, :], cT[:, 2, t * P:(t + 1) * P],
                                      WKVB[:, 512 * b:512 * b + 512], start=True, stop=True).then_inc(qkv_done, 1)
                    pe.wait_ge(q_out, 6)
                    pe.wait_ge(kv_out, 8)
                    pe.wait_ge(hd_ready, 2)
                    for g in range(12):
                        if g < 8:
                            for r in range(2):
                                for t in range(TT):
                                    last = pe.transpose(banks[g][0:QK_W, r * T + t * P:r * T + (t + 1) * P],
                                                        QK[:, t, 2 * g + r, :], ident)
                        else:
                            if g == 8:
                                pe.wait_ge(hd_ready, 4)
                            if g % 2:
                                pe.wait_ge(hdT_act, (g - 7) // 2)
                            else:
                                pe.wait_ge(hdT_dve, (g - 6) // 2)
                            for r in range(2):
                                for t in range(TT):
                                    c0 = NA0 + (2 * (g - 8) + r) * P
                                    last = pe.transpose(banks[g % 8][:, r * T + t * P:r * T + (t + 1) * P],
                                                        proj[:, t, c0:c0 + P], ident)
                        last.then_inc(hdT, 1)
                    pe.wait_ge(hdT_act, 6)
                    pe.wait_ge(hdT_dve, 6)

                    def scores(g):
                        if g >= 2:
                            pe.wait_ge(exp_done, g - 1)
                        for q in range(2):
                            if g < 8:
                                lhs, rhs = QKT[:, g, q * P:(q + 1) * P], QKT[:, 8 + g, :]
                            else:
                                h = g - 8
                                b = 64 * (h % 2)
                                lhs, rhs = NT[b:b + 64, h // 2, q * P:(q + 1) * P], NT[b:b + 64, 4 + h // 2, :]
                            last = pe.matmul(banks[g % 2][:, q * T:(q + 1) * T], lhs, rhs, start=True, stop=True)
                        last.then_inc(s_done, 1)

                    def values(g):
                        pe.wait_ge(pT_ready, g + 1)
                        kind, h = g // 8, g % 8
                        for q in range(2):
                            for kt in range(2):
                                v = V[:, kt, h, :] if kind == 0 else \
                                    proj[:, kt, NA0 + 1024 + h * HDV:NA0 + 1024 + (h + 1) * HDV]
                                last = pe.matmul(banks[4 + 2 * q + kind][:, h * HDV:(h + 1) * HDV],
                                                 probT[:, g % 2, kt, q * P:(q + 1) * P], v,
                                                 start=(kt == 0), stop=(kt == 1))
                        last.then_inc(pv_done, 1)

                    scores(0)
                    scores(1)
                    for g in range(16):
                        pe.wait_ge(exp_done, g + 1)
                        if g >= 2:
                            pe.wait_ge(pT_ready, g - 1)
                        for kt in range(2):
                            for q in range(2):
                                last = pe.transpose(banks[2 + g % 2][:, kt * T + q * P:kt * T + (q + 1) * P],
                                                    prob[:, g % 2, q, kt * P:(kt + 1) * P], ident)
                        last.then_inc(pT_done, 1)
                        if g + 2 < 16:
                            scores(g + 2)
                        if g:
                            values(g - 1)
                    values(15)
                    pe.wait_ge(cat_ready, 4)
                    for k in range(KC):
                        for t in range(TT):
                            last = pe.transpose(banks[k // 2][:, (k % 2) * T + t * P:(k % 2) * T + (t + 1) * P],
                                                CAT[:, t, k * P:(k + 1) * P], ident)
                        if k % 2:
                            last.then_inc(catT_done, 1)
                    pe.wait_ge(catT_dve, 2)
                    pe.wait_ge(catT_act, 2)
                    pe.wait_ge(wout_in, 16)
                    for t in range(TT):
                        for h in range(2):
                            for k in range(KC):
                                last = pe.matmul(banks[4 + 2 * t + h][:, :], catT[:, k, t * P:(t + 1) * P],
                                                 WOUT[:, k, 512 * h:512 * h + 512], start=(k == 0), stop=(k == KC - 1))
                            last.then_inc(mix_done, 1)

        def moe(l):
            ns = norm_sems(f"moe{l}_norm")
            names = ("router_in gate_in consts_set logits_done score_ready mask_ready hb_done hb_hi hb_lo "
                     "sh_in sgu_done sg_ready su_ready suT_done suT_ready ssd_done pos_done pos_ready "
                     "first_done table_ready pgT_done pgT_ready pgb_done pgb_ready own_dve "
                     "pick_ready pt_done pT_ready ga_done xg_act xg_dve gu_done silu_done u_ready "
                     "uT_done uT_ready d_done o_hi o_lo sc_done y_done").split()
            (router_in, gate_in, consts_set, logits_done, score_ready, mask_ready, hb_done, hb_hi, hb_lo,
             sh_in, sgu_done, sg_ready, su_ready, suT_done, suT_ready, ssd_done, pos_done, pos_ready,
             first_done, table_ready, pgT_done, pgT_ready, pgb_done, pgb_ready, own_dve,
             pick_ready, pt_done, pT_ready, ga_done, xg_act, xg_dve, gu_done, silu_done, u_ready,
             uT_done, uT_ready, d_done, o_hi, o_lo, sc_done, y_done) = (sem(n) for n in names)
            gu_in = [sem(f"gate_up_in{i}") for i in range(4)]
            dn_in = [sem(f"down_in{i}") for i in range(4)]

            wpos[0] = TT * D
            RW = carve(KC * E_N).rearrange("p (k e) -> p k e", k=KC)
            RB = carve(E_N)
            SG = carve(FF)
            U = carve(FF).rearrange("p (j f) -> p j f", j=2)
            UT = carve(FF).rearrange("p (j s) -> p j s", j=2)
            reused = carve(2 * KC * P)
            SU = reused[:, 0:512].rearrange("p (t j f) -> p t j f", t=TT, j=2)
            SSG = reused[:, 512:1024].rearrange("p (t f) -> p t f", t=TT)
            SUT = reused[:, 1024:1536].rearrange("p (j t) -> p j t", j=2)
            xgT = reused.rearrange("p (u k s) -> p u k s", u=2, k=KC)
            score = carve(TT * E_N).rearrange("p (t e) -> p t e", t=TT)
            sel = carve(TT * E_N).rearrange("p (t e) -> p t e", t=TT)
            top2 = carve(TT * GROUPS * 8).rearrange("p (t g m) -> p t g m", t=TT, g=GROUPS)
            gsc = carve(TT * GROUPS).rearrange("p (t g) -> p t g", t=TT)
            beat = carve(TT * 64).rearrange("p (t g o) -> p t g o", t=TT, g=GROUPS)
            tie = carve(TT * 64).rearrange("p (t g o) -> p t g o", t=TT, g=GROUPS)
            rank = carve(TT * GROUPS).rearrange("p (t g) -> p t g", t=TT)
            gon = carve(TT * GROUPS).rearrange("p (t g) -> p t g", t=TT)
            goff = carve(TT * GROUPS).rearrange("p (t g) -> p t g", t=TT)
            best = carve(TT * 8).rearrange("p (t m) -> p t m", t=TT)
            left = carve(TT * E_N).rearrange("p (t e) -> p t e", t=TT)
            mask = carve(TT * E_N).rearrange("p (t e) -> p t e", t=TT)
            table = carve(2 * TT * NB).rearrange("p (a t b) -> p a t b", a=2, t=TT)
            pg = table[:, :, :, 0:E_N]
            gsum = carve(TT)
            pgT = carve(2 * TT * P)[0:E_N].rearrange("p (a t q) -> p a t q", a=2, t=TT)
            count = carve(4)
            nblk = count[0:E_N, 1:2]
            first = count[0:E_N, 2:3]
            off = carve(NX)[0:E_N]
            has = carve(NX)[0:E_N]
            ge0 = carve(NX)[0:E_N]
            rnd = carve(NX)[0:E_N]
            gcur = carve(2 * TT * 2).rearrange("p (u t b) -> p u t b", u=2, t=TT)
            gslot = carve(1)
            minus = carve(P)[0:E_N]
            ones = carve(P)
            shared = carve(SLOT_W)
            gbias = W[:, 0:D]

            def gu(w, k):
                return w[:, 0:2 * KC * FF].rearrange("p (m k f) -> p k m f", m=2, k=KC)[:, k]

            def down(w, j, h):
                return w[:, 2 * KC * FF:].rearrange("p (j n) -> p j n", j=2)[:, j, 512 * h:512 * h + 512]

            def wait(eng, s, v):
                if not isinstance(v, int) or v > 0:
                    eng.wait_ge(s, v)

            def each_pair(eng, main, tail, total):
                half = MAIN_PAIRS // 2
                main(0, 0, 0)
                main(1, 1, 0)
                with eng.Fori(1, half) as i:
                    main(i * 2, 0, i)
                    main(i * 2 + 1, 1, i)
                tail(None, None, None)
                more = total(eng)
                with eng.If(more > 0):
                    tail(MAIN_PAIRS, 0, half)
                with eng.If(more > 2):
                    tail(MAIN_PAIRS + 1, 1, half)
                    with eng.Fori(1, TAIL_STEPS) as i:
                        for v in range(2):
                            with eng.If(more > i * 4 + 2 * v):
                                tail(i * 2 + (MAIN_PAIRS + v), v, i + half)

            def total_blocks(eng):
                return eng.value_load(ids[0:1, NX:NX + 1], min_val=0, max_val=NX)

            with nc.Block() as block:
                @block.sync
                def _(sp):
                    sp.dma_start(RW, router_w[l].rearrange("(p k) e -> p k e", k=KC)).then_inc(router_in, 16)
                    with nc.allow_non_contiguous_dma("rows for every partition"):
                        sp.dma_start(RB, router_b[l].partition_broadcast(P)).then_inc(router_in, 16)
                        sp.dma_start(gate_bc[:, :], mod_dram[l, 5 * D:6 * D].partition_broadcast(P)
                                     ).then_inc(gate_in, 16)
                    g3 = shared[:, 0:2 * KC * FF].rearrange("p (m k f) -> p m k f", m=2, k=KC)
                    sp.dma_start(g3[:, 0], sh_w_gate[l].rearrange("(p k) f -> p k f", k=KC)).then_inc(sh_in, 16)
                    sp.dma_start(g3[:, 1], sh_w_up[l].rearrange("(p k) f -> p k f", k=KC)).then_inc(sh_in, 16)
                    sp.dma_start(shared[:, 2 * KC * FF:].rearrange("p (j n) -> p j n", j=2),
                                 sh_w_down[l].rearrange("(f j) n -> f j n", j=2)).then_inc(sh_in, 16)

                    def load(n, u, e):
                        wait(sp, gu_done, n - 1)
                        for b in range(2):
                            dst = slot(2 * u + b)[:, 0:2 * KC * FF].rearrange("p (m k f) -> p m k f", m=2, k=KC)
                            for w, src in enumerate((exp_w_gate, exp_w_up)):
                                sp.dma_start(dst[:, w], src[l, bass.ds(e[b], 1)]
                                             .rearrange("o (p k) f -> p (o k) f", k=KC)).then_inc(gu_in[2 * u + b], 16)
                        wait(sp, d_done, n * 2 - 2)
                        for b in range(2):
                            dst = slot(2 * u + b)[:, 2 * KC * FF:].rearrange("p (j n) -> p j n", j=2)
                            sp.dma_start(dst, exp_w_down[l, bass.ds(e[b], 1)]
                                         .rearrange("o (f j) n -> f (o j) n", j=2)).then_inc(dn_in[2 * u + b], 16)

                    def main(n, u, m):
                        load(n, u, [n * 2, n * 2 + 1])

                    def tail(n, u, m):
                        if n is None:
                            sp.wait_ge(table_ready, 1)
                        else:
                            load(n, u, [sp.value_load(ids[0:1, bass.ds(n * 2 + (b - E_N), 1)],
                                                      min_val=0, max_val=E_N - 1) for b in range(2)])

                    each_pair(sp, main, tail, total_blocks)
                    if l == 0:
                        sp.wait_ge(y_done, 1)
                        load_conv_weights(sp)

                @block.gpsimd
                def _(pool):
                    norm_pool(pool, ns)
                    pool.memset(minus, -float(SLOTS)).then_inc(consts_set, 1)
                    pool.memset(zeros[:, :].bitcast(F32), 0.0).then_inc(consts_set, 1)
                    pool.memset(ones, 1.0).then_inc(consts_set, 1)

                @block.scalar
                def _(act):
                    norm_act(act, ns, l, 1)
                    act.wait_ge(logits_done, 1)
                    act.activation(score, banks[4][:, 0:TT * E_N].rearrange("p (t e) -> p t e", t=TT),
                                   ACT.Sigmoid).then_inc(score_ready, 1)
                    act.wait_ge(ns["xn"], 2)
                    for g in range(4):
                        act.wait_ge(hb_done, g + 1)
                        act.copy(H_hi[:, g // 2, 512 * (g % 2):512 * (g % 2) + 512], banks[g][:, :]).then_inc(hb_hi, 1)
                    for t in range(TT):
                        act.wait_ge(sgu_done, t + 1)
                        act.activation(SSG[:, t], banks[6 + t][:, 0:FF], ACT.Silu).then_inc(sg_ready, 1)
                    act.wait_ge(ns["turned"], 4)
                    act.dma_start(gbias, ada_b[l, 5 * D:6 * D].partition_broadcast(P)).then_inc(gate_in, 16)

                    def take(n, u):
                        act.wait_ge(ga_done, n * 2 + 1)
                        wait(act, gu_done, n - 1)
                        act.copy(xgT[:, u, 0:4, :], banks[6][:, :].rearrange("p (k s) -> p k s", k=4)
                                 ).then_inc(xg_act, 1)

                    act.wait_ge(ssd_done, 1)
                    take(0, 0)

                    def pair(n, u, m):
                        act.wait_ge(gu_done, n + 1)
                        wait(act, u_ready, n)
                        act.activation(SG, banks[4][:, 0:FF], ACT.Silu).then_inc(silu_done, 1)
                        take(n + 1, 1 - u)
                        wait(act, sc_done, n)
                        act.wait_ge(pT_ready, n + 1)
                        for h in range(2):
                            act.wait_ge(d_done, n * 2 + (h + 1))
                            act.activation(O_hi[:, 512 * h:512 * h + 512], banks[6 + h][:, :], ACT.Copy,
                                           scale=gslot[:, 0:1]).then_inc(o_hi, 1)

                    def tail(n, u, m):
                        if n is not None:
                            pair(n, u, m)

                    act.wait_ge(table_ready, 1)
                    each_pair(act, pair, tail, total_blocks)

                @block.vector
                def _(dve):
                    own = Chain(dve, own_dve)
                    norm_dve(dve, ns, l, 1)
                    dve.wait_ge(con_in, 16)
                    dve.wait_ge(router_in, 32)
                    dve.wait_ge(score_ready, 1)
                    own.link(dve.tensor_tensor(sel, score, RB.unsqueeze(1).broadcast_to([P, TT, E_N]), ALU.add))
                    for t in range(TT):
                        for g in range(GROUPS):
                            last = dve.max(top2[:, t, g, :], sel[:, t, g * PER_G:(g + 1) * PER_G])
                    own.link(last)
                    own.link(dve.tensor_tensor(gsc, top2[:, :, :, 0], top2[:, :, :, 1], ALU.add))
                    glt = con[:, C_GLT:C_GLT + 64].rearrange("p (g o) -> p g o", g=GROUPS)
                    for t in range(TT):
                        mine = gsc[:, t].unsqueeze(2).broadcast_to([P, GROUPS, GROUPS])
                        other = gsc[:, t].unsqueeze(1).broadcast_to([P, GROUPS, GROUPS])
                        dve.tensor_tensor(beat[:, t], other, mine, ALU.is_gt)
                        own.link(dve.tensor_tensor(tie[:, t], other, mine, ALU.is_equal))
                        own.link(dve.tensor_tensor(tie[:, t], tie[:, t], glt, ALU.mult))
                        own.link(dve.tensor_tensor(beat[:, t], beat[:, t], tie[:, t], ALU.add))
                        own.link(dve.tensor_reduce(rank[:, t], beat[:, t], AX, ALU.add))
                    own.link(dve.tensor_scalar(gon, rank, float(GROUPS_ON), None, ALU.is_lt))
                    own.link(dve.tensor_scalar(goff, gon, -1.0, -NEG, ALU.add, ALU.mult))
                    sel4 = sel.rearrange("p t (g e) -> p (t g) e", g=GROUPS)
                    gon3 = gon.rearrange("p t g -> p (t g)").unsqueeze(2).broadcast_to([P, TT * GROUPS, PER_G])
                    goff3 = goff.rearrange("p t g -> p (t g)").unsqueeze(2).broadcast_to([P, TT * GROUPS, PER_G])
                    own.link(dve.tensor_tensor(sel4, sel4, gon3, ALU.mult))
                    own.link(dve.tensor_tensor(sel4, sel4, goff3, ALU.add))
                    for t in range(TT):
                        own.link(dve.max(best[:, t], sel[:, t]))
                        own.link(dve.match_replace(left[:, t], best[:, t], sel[:, t], -3.0e38))
                    dve.tensor_scalar(mask, left, -2.0e38, None, ALU.is_lt).then_inc(mask_ready, 1)
                    dve.wait_ge(mask_ready, 1)
                    own.link(dve.tensor_tensor(pg[:, 1], score, mask, ALU.mult))
                    own.link(dve.tensor_reduce(gsum, pg[:, 1], AX, ALU.add))
                    own.link(dve.reciprocal(gsum, gsum))
                    for t in range(TT):
                        own.link(dve.tensor_scalar(pg[:, 1, t], pg[:, 1, t], gsum[:, t:t + 1], SCALE_R,
                                                   ALU.mult, ALU.mult))
                    for g in range(4):
                        cols = slice(512 * (g % 2), 512 * (g % 2) + 512)
                        dve.wait_ge(hb_hi, g + 1)
                        dve.tensor_tensor(H_lo[:, g // 2, cols], banks[g][:, :],
                                          H_hi[:, g // 2, cols].bitcast(F32), ALU.subtract).then_inc(hb_lo, 1)
                    for t in range(TT):
                        dve.wait_ge(sg_ready, t + 1)
                        dve.tensor_tensor(SU[:, t].rearrange("p j f -> p f j"),
                                          SSG[:, t].rearrange("p (f j) -> p f j", j=2),
                                          banks[6 + t][:, FF:2 * FF].rearrange("p (f j) -> p f j", j=2),
                                          ALU.mult).then_inc(su_ready, 1)
                    places = con[:, C_SLOT:C_SLOT + SLOTS]

                    def choose(n, u):
                        wait(dve, pt_done, n - 1)
                        dve.tensor_copy(gcur[:, u], table[:, 1, :, bass.ds(n * 2, 2)])
                        for t in range(TT):
                            ins = dve.tensor_tensor(pick[:, u, t, :].rearrange("p (b s) -> p b s", b=2),
                                                    table[:, 0, t, bass.ds(n * 2, 2)].unsqueeze(2)
                                                    .broadcast_to([P, 2, SLOTS]),
                                                    places.unsqueeze(1).broadcast_to([P, 2, SLOTS]), ALU.is_equal)
                        ins.then_inc(pick_ready, 1)

                    def take(n, u):
                        dve.wait_ge(ga_done, n * 2 + 2)
                        wait(dve, gu_done, n - 1)
                        dve.tensor_copy(xgT[:, u, 4:8, :], banks[7][:, :].rearrange("p (k s) -> p k s", k=4)
                                        ).then_inc(xg_dve, 1)

                    dve.wait_ge(pos_done, 1)
                    own.link(dve.tensor_tensor(pg[:, 0], banks[4][:, 128:256].rearrange("p (t e) -> p t e", t=TT),
                                               mask, ALU.mult))
                    own.link(dve.tensor_copy(count[0:E_N, 0:1], banks[4][0:E_N, 256:257]))
                    own.link(dve.tensor_scalar(nblk, count[0:E_N, 0:1], float(SLOTS), None, ALU.is_gt))
                    for r in range(2, T // SLOTS):
                        ins = dve.scalar_tensor_tensor(nblk, count[0:E_N, 0:1], float(r * SLOTS), nblk,
                                                       ALU.is_gt, ALU.add)
                        if r < T // SLOTS - 1:
                            own.link(ins)
                    ins.then_inc(pos_ready, 1)
                    dve.wait_ge(suT_done, 1)
                    dve.tensor_copy(SUT, banks[5][:, :].rearrange("p (j t) -> p j t", j=2)).then_inc(suT_ready, 1)
                    dve.wait_ge(first_done, 1)
                    own.link(dve.tensor_copy(first, banks[4][0:E_N, 260:261]))
                    own.link(dve.tensor_scalar(off, con[0:E_N, C_BLK:C_BLK + NX], first, None, ALU.subtract))
                    own.link(dve.tensor_scalar(ge0, off, 0.0, None, ALU.is_ge))
                    own.link(dve.scalar_tensor_tensor(has, off, nblk, ge0, ALU.is_lt, ALU.mult))
                    dve.scalar_tensor_tensor(rnd, off, 1.0, has, ALU.add, ALU.mult).then_inc(pos_ready, 1)
                    choose(0, 0)
                    dve.wait_ge(pgT_done, 1)
                    dve.tensor_copy(pgT, banks[3][0:E_N, :].rearrange("p (a t q) -> p a t q", a=2, t=TT)
                                    ).then_inc(pgT_ready, 1)
                    dve.wait_ge(ssd_done, 1)
                    take(0, 0)
                    dve.wait_ge(pgb_done, 1)
                    dve.tensor_copy(ids[0:1, 0:NX + 1], banks[4][0:1, 272:272 + NX + 1]).then_inc(table_ready, 1)
                    dve.tensor_copy(table[:, :, :, E_N:NB],
                                    banks[4][:, 320:320 + 2 * TT * NX].rearrange("p (a t b) -> p a t b", a=2, t=TT)
                                    ).then_inc(pgb_ready, 1)
                    dve.wait_ge(pgb_ready, 1)

                    def pair(n, u, m):
                        choose(n + 1, 1 - u)
                        dve.wait_ge(silu_done, n + 1)
                        wait(dve, uT_done, n)
                        dve.tensor_tensor(U.rearrange("p j f -> p f j"), SG.rearrange("p (f j) -> p f j", j=2),
                                          banks[4][:, FF:2 * FF].rearrange("p (f j) -> p f j", j=2),
                                          ALU.mult).then_inc(u_ready, 1)
                        dve.wait_ge(pt_done, n + 1)
                        wait(dve, sc_done, n)
                        wait(dve, o_hi, n * 2)
                        dve.tensor_copy(gslot, banks[5][:, T:T + 1])
                        dve.tensor_copy(pickT[:, :], banks[5][:, 0:T]).then_inc(pT_ready, 1)
                        dve.wait_ge(uT_done, n + 1)
                        wait(dve, d_done, n * 2)
                        dve.tensor_copy(UT, banks[5][:, 0:2 * P].rearrange("p (j s) -> p j s", j=2)
                                        ).then_inc(uT_ready, 1)
                        take(n + 1, 1 - u)
                        for h in range(2):
                            cols = slice(512 * h, 512 * h + 512)
                            dve.wait_ge(o_hi, n * 2 + (h + 1))
                            dve.wait_ge(pT_ready, n + 1)
                            dve.scalar_tensor_tensor(O_lo[:, cols], banks[6 + h][:, :], gslot[:, 0:1],
                                                     O_hi[:, cols].bitcast(F32), ALU.mult,
                                                     ALU.subtract).then_inc(o_lo, 1)

                    def tail(n, u, m):
                        if n is not None:
                            pair(n, u, m)

                    each_pair(dve, pair, tail, total_blocks)
                    dve.wait_ge(gate_in, 32)
                    own.link(dve.tensor_tensor(gate_bc[:, :], gate_bc[:, :], gbias, ALU.add))
                    dve.wait_ge(y_done, 1)
                    for t in range(TT):
                        for h in range(2):
                            cols = slice(512 * h, 512 * h + 512)
                            tmp = xgT.rearrange("p u k s -> p (u k s)")[:, 512 * (2 * t + h):512 * (2 * t + h + 1)]
                            own.link(dve.tensor_tensor(tmp, banks[2 * t + h][:, :], gate_bc[:, cols], ALU.mult))
                            dve.tensor_tensor(X[:, t, cols], X[:, t, cols], tmp, ALU.add)

                @block.tensor
                def _(pe):
                    def gather(n, u, half):
                        pe.wait_ge(pick_ready, n + 1)
                        for k in range(4):
                            kk = 4 * half + k
                            for t in range(TT):
                                for part in (H_hi, H_lo):
                                    last = pe.matmul(banks[6 + half][:, k * P:(k + 1) * P],
                                                     part[:, t, kk * P:(kk + 1) * P], pick[:, u, t, :],
                                                     start=(t == 0 and part is H_hi),
                                                     stop=(t == 1 and part is H_lo))
                        last.then_inc(ga_done, 1)

                    norm_pe(pe, ns)
                    wait_h(pe, ns)
                    pe.wait_ge(router_in, 32)
                    for t in range(TT):
                        for k in range(KC):
                            last = pe.matmul(banks[4][:, t * E_N:(t + 1) * E_N], hT[:, k, t * P:(t + 1) * P],
                                             RW[:, k, :], start=(k == 0), stop=(k == KC - 1))
                    last.then_inc(logits_done, 1)
                    for g in range(4):
                        for k in range(4):
                            kk = 4 * (g % 2) + k
                            last = pe.transpose(banks[g][:, k * P:(k + 1) * P],
                                                hT[:, kk, (g // 2) * P:(g // 2 + 1) * P], ident)
                        last.then_inc(hb_done, 1)
                    pe.wait_ge(sh_in, 48)
                    for t in range(TT):
                        for k in range(KC):
                            last = pe.matmul(banks[6 + t][:, :], hT[:, k, t * P:(t + 1) * P], gu(shared, k),
                                             start=(k == 0), stop=(k == KC - 1))
                        last.then_inc(sgu_done, 1)
                    pe.wait_ge(mask_ready, 1)
                    pe.wait_ge(consts_set, 3)
                    tri = con[:, C_TRI:C_TRI + P]
                    pe.matmul(banks[4][:, 128:192], tri, mask[:, 0, :], start=True, stop=True)
                    pe.matmul(banks[4][:, 192:256], tri, mask[:, 1, :], start=True, stop=False)
                    pe.matmul(banks[4][:, 192:256], ones, mask[:, 0, :], start=False, stop=True)
                    for t in range(TT):
                        last = pe.matmul(banks[4][0:E_N, 256:257], mask[:, t, :], ones[:, 0:1],
                                         start=(t == 0), stop=(t == 1))
                    last.then_inc(pos_done, 1)
                    pe.wait_ge(su_ready, 2)
                    for j in range(2):
                        for t in range(TT):
                            last = pe.transpose(banks[5][:, j * T + t * P:j * T + (t + 1) * P], SU[:, t, j, :], ident)
                    last.then_inc(suT_done, 1)
                    pe.wait_ge(pos_ready, 1)
                    pe.matmul(banks[4][0:E_N, 260:261], con[0:E_N, C_STRICT:C_STRICT + E_N], nblk,
                              start=True, stop=True)
                    pe.matmul(banks[4][0:1, 272 + NX:273 + NX], ones[0:E_N, 0:1], nblk,
                              start=True, stop=True).then_inc(first_done, 1)
                    pe.wait_ge(hb_lo, 4)
                    for a in range(2):
                        for t in range(TT):
                            last = pe.transpose(banks[3][0:E_N, (2 * a + t) * P:(2 * a + t + 1) * P],
                                                pg[:, a, t, :], ident)
                    last.then_inc(pgT_done, 1)
                    gather(0, 0, 0)
                    gather(0, 0, 1)
                    pe.wait_ge(suT_ready, 1)
                    for t in range(TT):
                        for h in range(2):
                            if t and h:
                                pe.wait_ge(pgT_ready, 1)
                            for j in range(2):
                                last = pe.matmul(banks[2 * t + h][:, :], SUT[:, j, t * P:(t + 1) * P],
                                                 down(shared, j, h), start=(j == 0), stop=False,
                                                 skip_group_check=True)
                    last.then_inc(ssd_done, 1)
                    pe.wait_ge(pos_ready, 2)
                    pe.matmul(banks[4][0:1, 272:272 + NX], con[0:E_N, C_EIDX:C_EIDX + 1], has, start=True, stop=True)
                    for t in range(TT):
                        pe.matmul(banks[4][:, 320 + t * NX:320 + (t + 1) * NX], pgT[:, 0, t, :], has,
                                  start=True, stop=False)
                        pe.matmul(banks[4][:, 320 + t * NX:320 + (t + 1) * NX], minus, rnd, start=False, stop=True)
                    for t in range(TT):
                        last = pe.matmul(banks[4][:, 320 + (2 + t) * NX:320 + (3 + t) * NX], pgT[:, 1, t, :], has,
                                         start=True, stop=True)
                    last.then_inc(pgb_done, 1)
                    pe.wait_ge(pgb_ready, 1)

                    def scatter(n):
                        pe.wait_ge(pT_ready, n)
                        pe.wait_ge(o_lo, n * 2)
                        for t in range(TT):
                            for h in range(2):
                                for part in (O_hi, O_lo):
                                    last = pe.matmul(banks[2 * t + h][:, :], pickT[:, t * P:(t + 1) * P],
                                                     part[:, 512 * h:512 * h + 512], start=False, stop=False,
                                                     skip_group_check=True)
                        last.then_inc(sc_done, 1)

                    def pair(n, u, m, in_tail=False):
                        for b in range(2):
                            pe.wait_ge(gu_in[2 * u + b], m * 32 + 32)
                        pe.wait_ge(xg_act, n + 1)
                        pe.wait_ge(xg_dve, n + 1)
                        wait(pe, u_ready, n)
                        for k in range(KC):
                            for b in range(2):
                                last = pe.matmul(banks[4][64 * b:64 * b + 64, :], xgT[:, u, k, 64 * b:64 * b + 64],
                                                 gu(slot(2 * u + b), k), start=(k == 0), stop=(k == KC - 1))
                        last.then_inc(gu_done, 1)
                        if not in_tail and not (isinstance(n, int) and n == 0):
                            scatter(n)
                        wait(pe, uT_ready, n)
                        for t in range(TT):
                            pe.transpose(banks[5][:, t * P:(t + 1) * P], pick[:, u, t, :].bitcast(F32), ident)
                        for b in range(2):
                            for t in range(TT):
                                last = pe.matmul(banks[5][64 * b:64 * b + 64, T:T + 1],
                                                 pick[:, u, t, 64 * b:64 * b + 64].bitcast(F32),
                                                 gcur[:, u, t, b:b + 1], start=(t == 0), stop=(t == 1))
                        last.then_inc(pt_done, 1)
                        gather(n + 1, 1 - u, 0)
                        pe.wait_ge(u_ready, n + 1)
                        pe.wait_ge(pT_ready, n + 1)
                        for j in range(2):
                            last = pe.transpose(banks[5][:, j * P:(j + 1) * P], U[:, j, :], ident)
                        last.then_inc(uT_done, 1)
                        gather(n + 1, 1 - u, 1)
                        for b in range(2):
                            pe.wait_ge(dn_in[2 * u + b], m * 16 + 16)
                        pe.wait_ge(uT_ready, n + 1)
                        for h in range(2):
                            pe.wait_ge(xg_dve if h else xg_act, n + 2)
                            for j in range(2):
                                for b in range(2):
                                    last = pe.matmul(banks[6 + h][64 * b:64 * b + 64, :], UT[:, j, 64 * b:64 * b + 64],
                                                     down(slot(2 * u + b), j, h), start=(j == 0), stop=(j == 1))
                            last.then_inc(d_done, 1)
                        if in_tail:
                            scatter(n + 1)

                    def tail(n, u, m):
                        if n is None:
                            scatter(MAIN_PAIRS)
                        else:
                            pair(n, u, m, in_tail=True)

                    each_pair(pe, pair, tail, total_blocks)
                    pe.wait_ge(pgb_ready, 1)
                    for b in range(4):
                        last = pe.matmul(banks[b][:, :], zeros[:, :], pick[:, :, :, :].rearrange("p u t q -> p (u t q)"),
                                         start=False, stop=True, skip_group_check=True)
                    last.then_inc(y_done, 1)

        PW1 = ring[:, 0:KC * 2 * D].rearrange("p (k n) -> p k n", k=KC)
        PW2 = ring[:, KC * 2 * D:KC * 3 * D].rearrange("p (k n) -> p k n", k=KC)
        pw1_in, pw2_in = sem("pw1_in"), sem("pw2_in")

        def load_conv_weights(sp):
            v = pw1_w[0].rearrange("(p k) n -> p k n", k=KC)
            for k in range(0, KC, 2):
                sp.dma_start(PW1[:, k:k + 2], v[:, k:k + 2]).then_inc(pw1_in, 16)
            sp.dma_start(PW2, pw2_w[0].rearrange("(p k) n -> p k n", k=KC)).then_inc(pw2_in, 16)

        def conv():
            ns = norm_sems("conv_norm")
            names = ("cvec_in gate_in bias_in pads_clear pw1_done sig_ready glu_ready tap_done mean_done "
                     "cen_ready csq_ready var_done var_ready rs_ready yn_ready act_ready pw2_done own_dve ones_set").split()
            (cvec_in, gate_in, bias_in, pads_clear, pw1_done, sig_ready, glu_ready, tap_done, mean_done,
             cen_ready, csq_ready, var_done, var_ready, rs_ready, yn_ready, act_ready, pw2_done, own_dve,
             ones_set) = (sem(n) for n in names)
            wpos[0] = TT * D
            GW = T + 2 * PAD
            G = carve(KC * GW).rearrange("p (m t) -> p m t", m=KC)
            Y = carve(KC * T).rearrange("p (m t) -> p m t", m=KC)
            Ysq = carve(KC * T).rearrange("p (m t) -> p m t", m=KC)
            sig = carve(2 * T).rearrange("p (b t) -> p b t", b=2)
            b1 = carve(2 * KC).rearrange("p (s k) -> p s k", s=2)
            taps = carve(CONV_W * KC).rearrange("p (w k) -> p w k", w=CONV_W)
            vec = carve(3 * KC).rearrange("p (a k) -> p a k", a=3)
            ones = carve(P)
            var = carve(T)
            rs = carve(T)
            b2 = carve(D)
            gbias = carve(D)
            S = hT

            with nc.Block() as block:
                @block.sync
                def _(sp):
                    with nc.allow_non_contiguous_dma("vectors by (p, k), rows for every partition"):
                        sp.dma_start(b1, pw1_b[0].rearrange("(s p k) -> p s k", s=2, k=KC)).then_inc(cvec_in, 16)
                        sp.dma_start(taps, dw_w[0].rearrange("w (p k) -> p w k", k=KC)).then_inc(cvec_in, 16)
                        for a, src in enumerate((dw_b, conv_ln_w, conv_ln_b)):
                            sp.dma_start(vec[:, a], pk(src[0])).then_inc(cvec_in, 16)
                        sp.dma_start(gate_bc[:, :], mod_dram[1, 2 * D:3 * D].partition_broadcast(P)
                                      ).then_inc(gate_in, 16)
                        sp.dma_start(gbias, ada_b[1, 2 * D:3 * D].partition_broadcast(P)).then_inc(gate_in, 16)
                        sp.dma_start(b2, pw2_b[0].partition_broadcast(P)).then_inc(gate_in, 16)

                @block.gpsimd
                def _(pool):
                    pool.memset(ones, 1.0).then_inc(ones_set, 1)
                    pool.memset(G[:, :, 0:PAD], 0.0)
                    pool.memset(G[:, :, PAD + T:GW], 0.0).then_inc(pads_clear, 1)
                    norm_pool(pool, ns)

                @block.scalar
                def _(act):
                    norm_act(act, ns, 1, 0)
                    act.wait_ge(cvec_in, 80)
                    for m in range(KC):
                        act.wait_ge(pw1_done, m + 1)
                        if m >= 2:
                            act.wait_ge(glu_ready, m - 1)
                        act.activation(sig[:, m % 2], banks[m][:, T:2 * T], ACT.Sigmoid,
                                       bias=b1[:, 1, m:m + 1]).then_inc(sig_ready, 1)
                    act.wait_ge(cen_ready, 1)
                    act.activation(Ysq, Y, ACT.Square).then_inc(csq_ready, 1)
                    act.wait_ge(var_ready, 1)
                    act.activation(rs, var, ACT.Sqrt).then_inc(rs_ready, 1)
                    for m in range(KC):
                        act.wait_ge(yn_ready, 1)
                        act.activation(S[:, m], Y[:, m], ACT.Silu, bias=vec[:, 2, m:m + 1],
                                       scale=vec[:, 1, m:m + 1]).then_inc(act_ready, 1)

                @block.vector
                def _(dve):
                    own = Chain(dve, own_dve)
                    norm_dve(dve, ns, 1, 0)
                    dve.wait_ge(pads_clear, 1)
                    dve.wait_ge(cvec_in, 80)
                    dve.wait_ge(gate_in, 48)
                    own.link(dve.tensor_tensor(gate_bc[:, :], gate_bc[:, :], gbias, ALU.add))
                    own.link(dve.tensor_tensor(b2, b2, gate_bc[:, :], ALU.mult))
                    for t in range(TT):
                        own.link(dve.tensor_tensor(X[:, t], X[:, t], b2, ALU.add))
                    for m in range(KC):
                        dve.wait_ge(sig_ready, m + 1)
                        dve.scalar_tensor_tensor(G[:, m, PAD:PAD + T], banks[m][:, 0:T], b1[:, 0, m:m + 1],
                                                 sig[:, m % 2], ALU.add, ALU.mult).then_inc(glu_ready, 1)
                        if m % 4 == 3:
                            dve.wait_ge(glu_ready, m + 1)
                            for w in range(CONV_W):
                                for mm in range(m - 3, m + 1):
                                    if w == 0:
                                        ins = dve.tensor_scalar(Y[:, mm], G[:, mm, 0:T], taps[:, 0, mm:mm + 1],
                                                                vec[:, 0, mm:mm + 1], ALU.mult, ALU.add)
                                    else:
                                        dve.wait_ge(tap_done, 4 * CONV_W * (m // 4) + 4 * w + mm % 4 - 3)
                                        ins = dve.scalar_tensor_tensor(Y[:, mm], G[:, mm, w:w + T],
                                                                       taps[:, w, mm:mm + 1], Y[:, mm],
                                                                       ALU.mult, ALU.add)
                                    ins.then_inc(tap_done, 1)
                    dve.wait_ge(mean_done, 1)
                    dve.scalar_tensor_tensor(Y, banks[0][:, 0:T].unsqueeze(1).broadcast_to([P, KC, T]), -1.0 / D, Y,
                                             ALU.mult, ALU.add).then_inc(cen_ready, 1)
                    dve.wait_ge(var_done, 1)
                    dve.tensor_scalar(var, banks[1][:, 0:T], 1.0 / D, EPS, ALU.mult, ALU.add).then_inc(var_ready, 1)
                    dve.wait_ge(rs_ready, 1)
                    own.link(dve.reciprocal(rs, rs))
                    dve.tensor_tensor(Y, Y, rs.unsqueeze(1).broadcast_to([P, KC, T]), ALU.mult).then_inc(yn_ready, 1)
                    for t in range(TT):
                        for h in range(2):
                            cols = slice(512 * h, 512 * h + 512)
                            dve.wait_ge(pw2_done, 2 * t + h + 1)
                            tmp = Ysq.rearrange("p m t -> p (m t)")[:, 512 * (2 * t + h):512 * (2 * t + h + 1)]
                            own.link(dve.tensor_tensor(tmp, banks[4 + 2 * t + h][:, :], gate_bc[:, cols], ALU.mult))
                            dve.tensor_tensor(X[:, t, cols], X[:, t, cols], tmp, ALU.add)

                @block.tensor
                def _(pe):
                    norm_pe(pe, ns)
                    wait_h(pe, ns)
                    pe.wait_ge(pw1_in, 64)
                    for m in range(KC):
                        for s in range(2):
                            for k in range(KC):
                                last = pe.matmul(banks[m][:, s * T:(s + 1) * T], PW1[:, k, s * D + m:(s + 1) * D:KC],
                                                 hT[:, k, :], start=(k == 0), stop=(k == KC - 1))
                        last.then_inc(pw1_done, 1)
                    pe.wait_ge(ones_set, 1)
                    for m in range(KC):
                        pe.wait_ge(tap_done, 4 * CONV_W * (m // 4 + 1) - 3 + m % 4)
                        last = pe.matmul(banks[0][:, 0:T], ones, Y[:, m], start=(m == 0), stop=(m == KC - 1))
                    last.then_inc(mean_done, 1)
                    pe.wait_ge(csq_ready, 1)
                    for m in range(KC):
                        last = pe.matmul(banks[1][:, 0:T], ones, Ysq[:, m], start=(m == 0), stop=(m == KC - 1))
                    last.then_inc(var_done, 1)
                    pe.wait_ge(pw2_in, 16)
                    pe.wait_ge(act_ready, KC)
                    for t in range(TT):
                        for h in range(2):
                            for k in range(KC):
                                last = pe.matmul(banks[4 + 2 * t + h][:, :], S[:, k, t * P:(t + 1) * P],
                                                 PW2[:, k, 512 * h:512 * h + 512], start=(k == 0), stop=(k == KC - 1))
                            last.then_inc(pw2_done, 1)

        with phase():
            attention()
        with phase():
            moe(0)
        with phase():
            conv()
        with phase():
            moe(1)

        stored = sem("stored")
        with nc.Block() as block:
            @block.sync
            def _(sp):
                sp.dma_start(out[0].rearrange("(t p) d -> p t d", p=P), X[:, :, :]).then_inc(stored, 16)
                sp.wait_ge(stored, 16)


def constants():
    import numpy as np
    a = np.zeros((P, C_N), np.float32)
    q = np.arange(P)
    a[:, C_ID:C_ID + P] = np.eye(P)
    a[:, C_TRI:C_TRI + P] = q[:, None] <= q[None, :]
    a[:, C_STRICT:C_STRICT + E_N] = q[:, None] < np.arange(E_N)[None, :]
    a[:, C_SLOT:C_SLOT + SLOTS] = np.arange(1, SLOTS + 1)
    a[:, C_BLK:C_BLK + NX] = np.arange(NX)
    g = np.arange(GROUPS)
    a[:, C_GLT:C_GLT + 64] = (g[None, :] < g[:, None]).reshape(-1)
    a[:, C_EIDX] = q
    n_freq = ROPE // 4
    inv = np.float32(10000.0) ** (-np.arange(n_freq, dtype=np.float32) / np.float32(n_freq))
    t = np.arange(T)
    ang = np.concatenate([(t // GRID_W).astype(np.float32)[:, None] * inv,
                          (t % GRID_W).astype(np.float32)[:, None] * inv], -1).astype(np.float32)
    co, si = np.cos(ang), np.sin(ang)
    for i in range(TT):
        r = slice(i * P, (i + 1) * P)
        a[:, C_COS + i * ROPE:C_COS + (i + 1) * ROPE] = np.concatenate([co[r], co[r]], -1)
        a[:, C_SIN + i * ROPE:C_SIN + (i + 1) * ROPE] = np.concatenate([-si[r], si[r]], -1)
    col = q % GRID_W
    start = np.clip(col - NA_KW // 2, 0, GRID_W - NA_KW)[:, None]
    key = np.arange(GRID_W)[None, :]
    a[:, C_WIN:C_WIN + GRID_W] = np.where((key >= start) & (key < start + NA_KW), 0.0, NEG)
    return a


_INS = ["x", "c", "norm1_w", "norm2_w", "ada_w", "ada_b", "w_in", "q_a_norm_w", "kv_a_norm_w", "w_q_b", "w_kv_b",
        "mla_q_norm_w", "mla_k_norm_w", "na_q_norm_w", "na_k_norm_w", "na_rpb", "w_out", "pw1_w", "pw1_b", "dw_w",
        "dw_b", "conv_ln_w", "conv_ln_b", "pw2_w", "pw2_b", "router_w", "router_b", "exp_w_gate", "exp_w_up",
        "exp_w_down", "sh_w_gate", "sh_w_up", "sh_w_down"]


def kernel(**inputs):
    import numpy as np
    import concourse.bacc as bacc
    from concourse.bass_utils import run_bass_kernel_spmd

    nc = bacc.Bacc("TRN2", target_bir_lowering=False, num_devices=1)
    arrays, args = {}, []
    for name in _INS:
        a = np.ascontiguousarray(inputs[name])
        arrays[f"in_{name}"] = a
        args.append(nc.dram_tensor(f"in_{name}", a.shape, mybir.dt.from_np(a.dtype), kind="ExternalInput").ap())
    arrays["in_consts"] = constants()
    args.append(nc.dram_tensor("in_consts", (P, C_N), F32, kind="ExternalInput").ap())
    args.append(nc.dram_tensor("out_0", (1, T, D), F32, kind="ExternalOutput").ap())
    build_encoder(nc, *args)
    r = run_bass_kernel_spmd(nc, [arrays], core_ids=[0])
    return r.results[0]["out_0"]
```

```python
from contextlib import ExitStack, contextmanager

import concourse.bass as bass
from concourse import mybir

P = 128
F32 = mybir.dt.float32
F32R = mybir.dt.float32r
I32 = mybir.dt.int32
ALU = mybir.AluOpType
ACT = mybir.ActivationFunctionType
AX = mybir.AxisListType.X

D = 1024
KC = D // P
T = 256
TT = T // P
EPS = 1e-6
Q_LORA, KV_LORA, ROPE = 256, 128, 32
HEADS, NOPE, HDV = 8, 64, 64
QK_W = NOPE + ROPE
IN_COLS = Q_LORA + KV_LORA + ROPE + 3 * HEADS * HDV
NA0 = Q_LORA + KV_LORA + ROPE
GRID_W, NA_KH, NA_KW = 64, 8, 16
ROWS = T // GRID_W
RPB_H, RPB_W = 2 * NA_KH - 1, 2 * NA_KW - 1
TOE = 2 * GRID_W - 1
CONV_W = 31
PAD = CONV_W // 2
E_N, FF, GROUPS, GROUPS_ON = 64, 256, 8, 4
PER_G = E_N // GROUPS
SCALE_R = 2.5
SLOTS = 64
TOP_K = 8
MAIN_PAIRS = E_N // 2
MAX_MORE = (T * TOP_K) // SLOTS
TAIL_STEPS = MAX_MORE // 4
NX = MAX_MORE + 2
NB = E_N + NX
SLOT_W = KC * 2 * FF + 2 * D
ADA_N = 2 * D
ADA_G = 6 * D // ADA_N
NEG = -1.0e30

C_ID = 0
C_TRI = C_ID + P
C_STRICT = C_TRI + P
C_SLOT = C_STRICT + E_N
C_BLK = C_SLOT + SLOTS
C_GLT = C_BLK + NX
C_EIDX = C_GLT + GROUPS * GROUPS
C_COS = C_EIDX + 1
C_SIN = C_COS + TT * ROPE
C_WIN = C_SIN + TT * ROPE
C_N = C_WIN + GRID_W


class Chain:

    def __init__(self, eng, sem):
        self.eng, self.sem, self.n = eng, sem, 0

    def link(self, ins):
        self.n += 1
        ins.then_inc(self.sem, 1)
        self.eng.wait_ge(self.sem, self.n)


def build_encoder(nc, x, c, norm1_w, norm2_w, ada_w, ada_b, w_in, q_a_norm_w, kv_a_norm_w,
                  w_q_b, w_kv_b, mla_q_norm_w, mla_k_norm_w, na_q_norm_w, na_k_norm_w,
                  na_rpb, w_out, pw1_w, pw1_b, dw_w, dw_b, conv_ln_w, conv_ln_b, pw2_w,
                  pw2_b, router_w, router_b, exp_w_gate, exp_w_up, exp_w_down,
                  sh_w_gate, sh_w_up, sh_w_down, consts, out):
    ctx = ExitStack()
    with ctx:
        def sb(name, shape, dt=F32):
            return ctx.enter_context(nc.sbuf_tensor(name, shape, dt))

        banks = [ctx.enter_context(nc.psum_tensor(f"bank{i}", [P, 512], F32)) for i in range(8)]

        con = sb("con", [P, C_N])
        ident = con[:, C_ID:C_ID + P]
        X = sb("X", [P, TT, D])
        hT = sb("hT", [P, KC, T])
        ring = sb("ring", [P, 4 * SLOT_W])
        W = sb("W", [P, 15232])
        split = sb("split", [P, 2 * TT * D + 2 * D], F32R)
        H_hi, H_lo = (split[:, a * TT * D:(a + 1) * TT * D].rearrange("p (t d) -> p t d", t=TT) for a in range(2))
        O_hi, O_lo = (split[:, 2 * TT * D + a * D:2 * TT * D + (a + 1) * D] for a in range(2))
        pick = sb("pick", [P, 2, TT, P], F32R)
        zeros = sb("zeros", [P, P], F32R)
        pickT = sb("pickT", [P, T], F32R)
        AB = sb("AB", [P, 2, 2, 2, KC])
        gate_bc = sb("gate_bc", [P, D])
        eps_half = sb("eps_half", [P, 16])
        small = sb("small", [P, 440])
        ids = sb("ids", [1, NX + 2], I32)

        phase_sems = []

        def sem(name):
            s = sem_stack[-1].enter_context(nc.semaphore(name))
            phase_sems.append(s)
            return s

        sem_stack = [ctx]

        @contextmanager
        def phase():
            stack = ExitStack()
            sem_stack.append(stack)
            phase_sems.clear()
            yield
            with nc.Block() as block:
                @block.gpsimd
                def _(pool):
                    for s in phase_sems:
                        pool.sem_clear(s)
            phase_sems.clear()
            stack.close()
            sem_stack.pop()

        wpos = [0]

        def carve(n):
            a = wpos[0]
            wpos[0] += n
            assert wpos[0] <= 15232
            return W[:, a:a + n]

        def slot(s):
            return ring[:, s * SLOT_W:(s + 1) * SLOT_W]

        mod_dram = nc.dram_tensor("mod_scratch", [2, 6 * D], F32).ap()
        toe_dram = nc.dram_tensor("toeplitz_scratch", [HEADS * RPB_H, GRID_W, GRID_W], F32).ap()

        def pk(row):
            return row.rearrange("(p k) -> p k", k=KC)

        def norm_sems(tag):
            return {k: sem(f"{tag}_{k}") for k in
                    ("squared", "mean", "rstd", "xn", "turned", "h_dve", "h_act")}

        XN = W[:, 0:TT * D].rearrange("p (t d) -> p t d", t=TT)
        ss = small[:, 0:2]
        ms = small[:, 2:4]
        rstd = small[:, 4:6]

        def norm_act(act, s, l, which):
            for t in range(TT):
                act.activation(XN[:, t, :], X[:, t, :], ACT.Square,
                               accum_out=ss[:, t:t + 1]).then_inc(s["squared"], 1)
            for j in (1, 3):
                act.wait_ge(s["turned"], j + 1)
                for k in (2 * j, 2 * j + 1):
                    act.activation(hT[:, k, :], banks[j][:, (k % 2) * T:(k % 2 + 1) * T], ACT.Identity,
                                   bias=AB[:, l, which, 1, k:k + 1],
                                   scale=AB[:, l, which, 0, k:k + 1]).then_inc(s["h_act"], 1)

        def norm_pool(pool, s):
            pool.wait_ge(s["mean"], 1)
            pool.tensor_tensor(rstd, ms, eps_half[:, 0:2], ALU.pow).then_inc(s["rstd"], 1)

        def norm_dve(dve, s, l, which):
            dve.wait_ge(s["squared"], 2)
            dve.tensor_scalar(ms, ss, 1.0 / D, EPS, ALU.mult, ALU.add).then_inc(s["mean"], 1)
            dve.wait_ge(s["rstd"], 1)
            for t in range(TT):
                dve.tensor_scalar(XN[:, t, :], X[:, t, :], rstd[:, t:t + 1], None,
                                  ALU.mult).then_inc(s["xn"], 1)
            for j in (0, 2):
                dve.wait_ge(s["turned"], j + 1)
                for k in (2 * j, 2 * j + 1):
                    dve.tensor_scalar(hT[:, k, :], banks[j][:, (k % 2) * T:(k % 2 + 1) * T],
                                      AB[:, l, which, 0, k:k + 1], AB[:, l, which, 1, k:k + 1],
                                      ALU.mult, ALU.add).then_inc(s["h_dve"], 1)

        def norm_pe(pe, s):
            pe.wait_ge(s["xn"], 2)
            for k in range(KC):
                for t in range(TT):
                    last = pe.transpose(banks[k // 2][:, (k % 2) * T + t * P:(k % 2) * T + (t + 1) * P],
                                        XN[:, t, k::KC], ident)
                if k % 2:
                    last.then_inc(s["turned"], 1)

        def wait_h(eng, s):
            eng.wait_ge(s["h_dve"], 4)
            eng.wait_ge(s["h_act"], 4)

        ada_in = [sem(f"ada_in{i}") for i in range(3)]
        ada_done, row_copied, row_stored = sem("ada_done"), sem("row_copied"), sem("row_stored")
        mod_in, ab_step, c_rep_ready = sem("mod_in"), sem("ab_step"), sem("c_rep_ready")
        row0 = gate_bc[:, 0:ADA_N // 4]
        c_rep0 = gate_bc[:, 512:768].rearrange("p (k m) -> p k m", k=KC)
        nw = small[:, 208:240].rearrange("p (w l k) -> p w l k", w=2, l=2)
        bcol = small[:, 240:336].rearrange("p (l j k) -> p l j k", l=2, j=6)
        mcol = small[:, 336:432].rearrange("p (l j k) -> p l j k", l=2, j=6)
        csil = small[:, 432:440]
        mod_groups = mod_dram.rearrange("l (j q n) -> (l j) q n", j=ADA_G, q=4)

        def ada_buf(n):
            return slot(0 if n >= 4 * KC else 3)[:, n % 3 * ADA_N:(n % 3 + 1) * ADA_N]

        def load_units(sp, n0, n1):
            for n in range(n0, n1):
                g, k = divmod(n, KC)
                l, j = divmod(g, ADA_G)
                if n >= 3:
                    sp.wait_ge(ada_done, n - 2)
                sp.dma_start(ada_buf(n),
                             ada_w[l].rearrange("(p k) n -> p k n", k=KC)[:, k, j * ADA_N:(j + 1) * ADA_N]
                             ).then_inc(ada_in[n % 3], 16)

        def multiply_units(pe, n0, n1, bank, c_rep):
            for n in range(n0, n1):
                g, k = divmod(n, KC)
                if k == 0 and g:
                    pe.wait_ge(row_copied, g)
                pe.wait_ge(ada_in[n % 3], 16 * (n // 3 + 1))
                for q in range(4):
                    last = pe.matmul(bank[32 * q:32 * q + 32, :], c_rep[:, k, :],
                                     ada_buf(n)[:, 512 * q:512 * q + 512], start=(k == 0), stop=(k == KC - 1))
                last.then_inc(ada_done, 1)

        def row_out(act, g, bank, row):
            act.wait_ge(ada_done, KC * (g + 1))
            if g:
                act.wait_ge(row_stored, 16 * g)
            act.copy(row, bank[:, :]).then_inc(row_copied, 1)
            act.wait_ge(row_copied, g + 1)
            act.dma_start(mod_groups[g], row[0:97:32, :]).then_inc(row_stored, 16)

        def load_mod(act, l, j0, j1, groups):
            act.wait_ge(row_stored, 16 * groups)
            with nc.allow_non_contiguous_dma("vectors by (p, k)"):
                act.dma_start(mcol[:, l, j0:j1], mod_dram[l, j0 * D:j1 * D].rearrange("(j p k) -> p j k", p=P, k=KC)
                              ).then_inc(mod_in, 16)

        def affine(dve, own, l, which):
            own.eng = dve
            j = slice(3 * which, 3 * which + 2)
            own.link(dve.tensor_tensor(mcol[:, l, j], mcol[:, l, j], bcol[:, l, j], ALU.add))
            own.link(dve.scalar_tensor_tensor(AB[:, l, which, 0], mcol[:, l, 3 * which + 1], 1.0, nw[:, which, l],
                                              ALU.add, ALU.mult))
            own.link(dve.tensor_copy(AB[:, l, which, 1], mcol[:, l, 3 * which]))

        c_in, con_in, x_in, vec_in = sem("c_in"), sem("con_in"), sem("x_in"), sem("vec_in")
        c_silu = sem("c_silu")
        toe_zeroed, toe_in, toe_stored = sem("toe_zeroed"), sem("toe_in"), sem("toe_stored")
        vecs_in = sem("vecs_in")
        win_in, wqkv_in = sem("win_in"), sem("wqkv_in")
        ccol = small[:, 8:16]
        toe = W[0:HEADS * RPB_H, 1280:1280 + TOE + 1]
        skew = W[0:HEADS * RPB_H, 2048:2048 + GRID_W * GRID_W].rearrange("p (c k) -> p c k", c=GRID_W)
        toe_skewed = sem("toe_skewed")
        WIN = ring[:, 0:KC * IN_COLS].rearrange("p (k n) -> p k n", k=KC)
        WQB = ring[:, KC * IN_COLS:KC * IN_COLS + 2 * 768].rearrange("p (k n) -> p k n", k=2)
        WKVB = ring[:, KC * IN_COLS + 1536:KC * IN_COLS + 1536 + D]
        own_ab = [None]

        with nc.Block() as block:
            @block.sync
            def _(sp):
                with nc.allow_non_contiguous_dma("vectors by (p, k)"):
                    sp.dma_start(ccol, pk(c[0, :])).then_inc(c_in, 16)
                load_units(sp, 0, 3)
                sp.dma_start(con[:, :], consts).then_inc(con_in, 16)
                load_units(sp, 3, KC)
                sp.dma_start(X[:, :, :], x[0].rearrange("(t p) d -> p t d", p=P)).then_inc(x_in, 16)
                wv = w_in[0].rearrange("(p k) n -> p k n", k=KC)
                for k in range(0, KC, 2):
                    sp.dma_start(WIN[:, k:k + 2, :], wv[:, k:k + 2, :]).then_inc(win_in, 16)
                sp.dma_start(WQB, w_q_b[0].rearrange("(k p) n -> p k n", k=2)).then_inc(wqkv_in, 16)
                sp.dma_start(WKVB, w_kv_b[0]).then_inc(wqkv_in, 16)
                sp.wait_ge(x_in, 16)
                sp.wait_ge(toe_stored, 16)

            @block.gpsimd
            def _(pool):
                pool.memset(eps_half[:, :], -0.5)
                pool.memset(toe, 0.0).then_inc(toe_zeroed, 1)
                pool.wait_ge(toe_zeroed, 1)
                pool.dma_start(toe[:, GRID_W - NA_KW:GRID_W - NA_KW + RPB_W],
                               na_rpb[0].rearrange("h i j -> (h i) j")).then_inc(toe_in, 16)
                pool.wait_ge(toe_in, 16)
                last = toe[:, GRID_W - 1:TOE]
                by_query = bass.AP(tensor=last.tensor, offset=last.offset,
                                   ap=[list(last.ap[0]), [-1, GRID_W], [1, GRID_W]])
                pool.tensor_copy(skew, by_query).then_inc(toe_skewed, 1)
                pool.wait_ge(toe_skewed, 1)
                pool.dma_start(toe_dram, skew).then_inc(toe_stored, 16)

            @block.scalar
            def _(act):
                act.wait_ge(c_in, 16)
                act.activation(csil, ccol, ACT.Silu).then_inc(c_silu, 1)
                with nc.allow_non_contiguous_dma("vectors by (p, k)"):
                    act.dma_start(nw[:, 0], norm1_w.rearrange("l (p k) -> p l k", k=KC)).then_inc(vec_in, 16)
                    act.dma_start(nw[:, 1], norm2_w.rearrange("l (p k) -> p l k", k=KC)).then_inc(vec_in, 16)
                    for l in range(2):
                        act.dma_start(bcol[:, l], ada_b[l].rearrange("(j p k) -> p j k", p=P, k=KC)
                                      ).then_inc(vec_in, 16)
                row_out(act, 0, banks[7], row0)
                load_mod(act, 0, 0, 2, 1)

            @block.vector
            def _(dve):
                own = own_ab[0] = Chain(dve, ab_step)
                dve.wait_ge(c_silu, 1)
                dve.tensor_copy(c_rep0, csil.unsqueeze(2).broadcast_to([P, KC, 32])).then_inc(c_rep_ready, 1)
                dve.wait_ge(vec_in, 64)
                dve.wait_ge(mod_in, 16)
                affine(dve, own, 0, 0)

            @block.tensor
            def _(pe):
                pe.wait_ge(c_rep_ready, 1)
                multiply_units(pe, 0, KC, banks[7], c_rep0)

        def attention():
            ns = norm_sems("attn_norm")
            wout_in = sem("wout_in")
            bias_in, bias_ready, gate_in, gate_ready = sem("bias_in"), sem("bias_ready"), sem("gate_in"), sem("gate_ready")
            proj_done, proj_dve, proj_act = sem("proj_done"), sem("proj_dve"), sem("proj_act")
            lat_sq, lat_ms, lat_rstd, lat_n, lat_T, cT_dve, cT_act = (
                sem(n) for n in ("lat_sq", "lat_ms", "lat_rstd", "lat_n", "lat_T", "cT_dve", "cT_act"))
            qkv_done, q_out, kv_out = sem("qkv_done"), sem("q_out"), sem("kv_out")
            hd_sq, hd_ms, hd_rstd, hd_ready, hdT, hdT_dve, hdT_act = (
                sem(n) for n in ("hd_sq", "hd_ms", "hd_rstd", "hd_ready", "hdT", "hdT_dve", "hdT_act"))
            s_done, nm_ready, exp_done, pT_done, pT_ready, pv_done = (
                sem(n) for n in ("s_done", "nm_ready", "exp_done", "pT_done", "pT_ready", "pv_done"))
            cat_ready, catT_done, catT_dve, catT_act, mix_done = (
                sem(n) for n in ("cat_ready", "catT_done", "catT_dve", "catT_act", "mix_done"))
            at_dve = sem("at_dve")

            wpos[0] = 0
            proj = carve(TT * IN_COLS).rearrange("p (t n) -> p t n", t=TT)
            CQN = carve(TT * 384).rearrange("p (t n) -> p t n", t=TT)
            cT = carve(3 * T).rearrange("p (c t) -> p c t", c=3)
            QK = carve(TT * 16 * QK_W).rearrange("p (t r w) -> p t r w", t=TT, r=16)
            V = carve(TT * 512).rearrange("p (t h w) -> p t h w", t=TT, h=HEADS)
            SQ = carve(16 * QK_W)
            CAT = carve(TT * D).rearrange("p (t d) -> p t d", t=TT)
            turned_at = carve(1024)
            rope_a = turned_at[:, 0:512].rearrange("p (r w) -> p r w", r=16)
            rope_b = turned_at[:, 512:1024].rearrange("p (r w) -> p r w", r=16)
            qkw = carve(2 * QK_W).rearrange("p (a w) -> p a w", a=2)
            naw = carve(2 * HDV).rearrange("p (a w) -> p a w", a=2)
            qaw = carve(Q_LORA)
            kvaw = carve(KV_LORA)
            Pr = W[:, TT * IN_COLS:TT * IN_COLS + 1536]
            assert TT * 384 + 3 * T == 1536
            prob = Pr[:, 0:1024].rearrange("p (b q k) -> p b q k", b=2, q=2)
            logit = SQ[:, 0:1024].rearrange("p (b q k) -> p b q k", b=2, q=2)
            probT = turned_at.rearrange("p (b c q) -> p b c q", b=2, c=2)
            assert KC * IN_COLS + 1536 + D <= 3 * SLOT_W
            WOUT = ring[:, 0:KC * D].rearrange("p (k n) -> p k n", k=KC)
            BIAS = ring[:, KC * D:KC * D + TT * HEADS * T].rearrange("p (t h k) -> p t h k", t=TT, h=HEADS)
            assert KC * D + TT * HEADS * T <= KC * IN_COLS
            QKT = slot(3)[0:QK_W, 0:16 * T].rearrange("p (r t) -> p r t", r=16)
            NT = slot(3)[:, 16 * T:24 * T].rearrange("p (r t) -> p r t", r=8)
            catT = hT
            lat_ss = small[:, 8:12].rearrange("p (t a) -> p t a", t=2)
            lat_m = small[:, 12:16].rearrange("p (t a) -> p t a", t=2)
            lat_r = small[:, 16:20].rearrange("p (t a) -> p t a", t=2)
            hd_ss, hd_m, hd_r = small[:, 32:48], small[:, 48:64], small[:, 64:80]
            mx = small[:, 80:112].rearrange("p (g q) -> p g q", q=2)
            nmx = small[:, 112:144].rearrange("p (g q) -> p g q", q=2)
            sums = small[:, 144:176].rearrange("p (q g) -> p q g", q=2)
            rsum = small[:, 176:208].rearrange("p (q g) -> p q g", q=2)
            PROJ_COLS = [(0, NA0)] + [(NA0 + 512 * i, 512) for i in range(3)]
            proj_bank = [[4, 5, 6, 0], [1, 2, 3, 4]]
            q_bank = [[0, 1], [4, 5]]
            kv_bank = [[2, 3], [6, 0]]
            MOD_END = 4 * KC
            SC_MLA, SC_NA = QK_W ** -0.5, HDV ** -0.5
            toe_v = toe_dram.rearrange("(h i) c k -> h i c k", h=HEADS)

            def head_norm_steps():
                for t in range(TT):
                    yield t, QK[:, t], QK_W, qkw, "mla"
                for t in range(TT):
                    yield t, proj[:, t, NA0:NA0 + 1024].rearrange("p (r w) -> p r w", r=16), HDV, naw, "na"

            with nc.Block() as block:
                @block.sync
                def _(sp):
                    load_units(sp, KC, MOD_END)
                    sp.wait_ge(proj_done, 8)
                    for t in range(TT):
                        for r2 in range(2):
                            r = 2 * t + r2
                            for h in range(HEADS):
                                src = toe_v[h, NA_KH - 1 - r:NA_KH - 1 - r + ROWS].rearrange("r c k -> c r k")
                                sp.dma_start(BIAS[64 * r2:64 * r2 + 64, t, h, :].rearrange("p (r c) -> p r c", r=ROWS),
                                             src).then_inc(bias_in, 16)
                    sp.dma_start(WOUT, w_out[0].rearrange("(k p) n -> p k n", k=KC)).then_inc(wout_in, 16)
                    sp.wait_ge(bias_in, 16 * 2 * TT * HEADS)

                @block.gpsimd
                def _(pool):
                    norm_pool(pool, ns)
                    with nc.allow_non_contiguous_dma("rows for every partition"):
                        pool.dma_start(qkw[:, 0], mla_q_norm_w[0].partition_broadcast(P)).then_inc(vecs_in, 16)
                        pool.dma_start(qkw[:, 1], mla_k_norm_w[0].partition_broadcast(P)).then_inc(vecs_in, 16)
                        pool.dma_start(naw[:, 0], na_q_norm_w[0].partition_broadcast(P)).then_inc(vecs_in, 16)
                        pool.dma_start(naw[:, 1], na_k_norm_w[0].partition_broadcast(P)).then_inc(vecs_in, 16)
                        pool.dma_start(qaw, q_a_norm_w[0].partition_broadcast(P)).then_inc(vecs_in, 16)
                        pool.dma_start(kvaw, kv_a_norm_w[0].partition_broadcast(P)).then_inc(vecs_in, 16)
                    pool.wait_ge(lat_ms, 1)
                    pool.tensor_tensor(lat_r, lat_m, eps_half[:, 0:4].rearrange("p (t a) -> p t a", t=2),
                                       ALU.pow).then_inc(lat_rstd, 1)
                    for n in range(4):
                        pool.wait_ge(hd_ms, n + 1)
                        pool.tensor_tensor(hd_r, hd_m, eps_half[:, 0:16], ALU.pow).then_inc(hd_rstd, 1)
                    pool.wait_ge(bias_in, 16 * 2 * TT * HEADS)
                    for t in range(TT):
                        v = BIAS[:, t].rearrange("p h (r c) -> p (h r) c", r=ROWS)
                        pool.tensor_tensor(v, v, con[:, C_WIN:C_WIN + GRID_W].unsqueeze(1)
                                           .broadcast_to([P, HEADS * ROWS, GRID_W]), ALU.add).then_inc(bias_ready, 1)

                @block.scalar
                def _(act):
                    norm_act(act, ns, 0, 0)
                    for t in range(TT):
                        for n in (1, 3):
                            act.wait_ge(proj_done, 4 * t + n + 1)
                            c0, w = PROJ_COLS[n]
                            act.copy(proj[:, t, c0:c0 + w], banks[proj_bank[t][n]][:, 0:w]).then_inc(proj_act, 1)
                        row_out(act, t + 1, banks[7], row0)
                    for t in range(TT):
                        act.wait_ge(proj_dve, 2 * t + 1)
                        act.activation(SQ[:, 0:Q_LORA] if t == 0 else SQ[:, 512:512 + Q_LORA], proj[:, t, 0:Q_LORA],
                                       ACT.Square, accum_out=lat_ss[:, t, 0:1]).then_inc(lat_sq, 1)
                        act.activation(SQ[:, 256:384] if t == 0 else SQ[:, 768:896], proj[:, t, Q_LORA:Q_LORA + KV_LORA],
                                       ACT.Square, accum_out=lat_ss[:, t, 1:2]).then_inc(lat_sq, 1)
                    act.wait_ge(lat_T, 2)
                    act.copy(cT[:, 2, :], banks[6][:, 0:T]).then_inc(cT_act, 1)
                    for t in range(TT):
                        for b in range(2):
                            act.wait_ge(qkv_done, 4 * t + 3 + b)
                            v = banks[kv_bank[t][b]][:, :].rearrange("p (h w) -> p h w", h=4)
                            act.copy(QK[:, t, 8 + 4 * b:12 + 4 * b, 0:NOPE], v[:, :, 0:NOPE]).then_inc(kv_out, 1)
                            act.copy(V[:, t, 4 * b:4 * b + 4, :], v[:, :, NOPE:NOPE + HDV]).then_inc(kv_out, 1)
                    for n, (t, v, w, _, kind) in enumerate(head_norm_steps()):
                        if kind == "mla":
                            act.wait_ge(q_out, 3 * (t + 1))
                            act.wait_ge(kv_out, 4 * (t + 1))
                        else:
                            act.wait_ge(proj_dve, 4)
                        if n:
                            act.wait_ge(hd_ms, n)
                        act.activation(SQ[:, 0:16 * w].rearrange("p (r w) -> p r w", r=16), v, ACT.Square
                                       ).then_inc(hd_sq, 1)
                    row_out(act, 3, banks[7], row0)
                    for g in range(1, 12, 2):
                        act.wait_ge(hdT, g + 1)
                        if g < 8:
                            act.copy(QKT[:, 2 * g:2 * g + 2, :], banks[g % 6][0:QK_W, :].rearrange("p (r t) -> p r t", r=2)
                                     ).then_inc(hdT_act, 1)
                        else:
                            act.copy(NT[:, 2 * (g - 8):2 * (g - 8) + 2, :],
                                     banks[g % 6][:, :].rearrange("p (r t) -> p r t", r=2)).then_inc(hdT_act, 1)

                    def turned(g):
                        act.wait_ge(pT_done, g + 1)
                        if g >= 2:
                            act.wait_ge(pv_done, g - 1)
                        act.copy(probT[:, g % 2], banks[2 + g % 2][:, :].rearrange("p (c q) -> p c q", c=2)
                                 ).then_inc(pT_ready, 1)

                    for g in range(16):
                        act.wait_ge(nm_ready, g + 1)
                        if g >= 2:
                            act.wait_ge(pT_done, g - 1)
                        for q in range(2):
                            src = banks[g % 2][:, q * T:(q + 1) * T] if g < 8 else logit[:, g % 2, q, :]
                            last = act.activation(prob[:, g % 2, q, :], src, ACT.Exp, bias=nmx[:, g, q:q + 1],
                                                  scale=SC_MLA if g < 8 else 1.0, accum_out=sums[:, q, g:g + 1])
                        last.then_inc(exp_done, 1)
                        if g:
                            turned(g - 1)
                    turned(15)
                    load_mod(act, 0, 3, 5, 4)
                    load_mod(act, 1, 0, 2, 4)
                    act.dma_start(gate_bc[:, :], mod_dram[0, 2 * D:3 * D].partition_broadcast(P)).then_inc(gate_in, 16)
                    act.wait_ge(pv_done, 16)
                    act.dma_start(W[:, 0:D], ada_b[0, 2 * D:3 * D].partition_broadcast(P)).then_inc(gate_in, 16)
                    for j in (1, 3):
                        act.wait_ge(catT_done, j + 1)
                        act.copy(catT[:, 2 * j:2 * j + 2, :], banks[j][:, :].rearrange("p (k t) -> p k t", k=2)
                                 ).then_inc(catT_act, 1)

                @block.vector
                def _(dve):
                    own = Chain(dve, at_dve)
                    norm_dve(dve, ns, 0, 0)
                    for t in range(TT):
                        for n in (0, 2):
                            dve.wait_ge(proj_done, 4 * t + n + 1)
                            c0, w = PROJ_COLS[n]
                            if t == 0 and n == 0:
                                dve.wait_ge(ns["turned"], 4)
                            dve.tensor_copy(proj[:, t, c0:c0 + w], banks[proj_bank[t][n]][:, 0:w]).then_inc(proj_dve, 1)
                    dve.wait_ge(lat_sq, 4)
                    own.link(dve.tensor_scalar(lat_m[:, :, 0], lat_ss[:, :, 0], 1.0 / Q_LORA, EPS, ALU.mult, ALU.add))
                    dve.tensor_scalar(lat_m[:, :, 1], lat_ss[:, :, 1], 1.0 / KV_LORA, EPS, ALU.mult,
                                      ALU.add).then_inc(lat_ms, 1)
                    dve.wait_ge(lat_rstd, 1)
                    dve.wait_ge(vecs_in, 96)
                    for t in range(TT):
                        dve.scalar_tensor_tensor(CQN[:, t, 0:Q_LORA], proj[:, t, 0:Q_LORA], lat_r[:, t, 0:1], qaw,
                                                 ALU.mult, ALU.mult)
                        dve.scalar_tensor_tensor(CQN[:, t, Q_LORA:384], proj[:, t, Q_LORA:384], lat_r[:, t, 1:2], kvaw,
                                                 ALU.mult, ALU.mult).then_inc(lat_n, 1)
                    dve.wait_ge(lat_T, 1)
                    dve.tensor_copy(cT[:, 0:2, :], banks[5][:, :].rearrange("p (c t) -> p c t", c=2)).then_inc(cT_dve, 1)
                    for t in range(TT):
                        qf = QK[:, t, 0:8, :].rearrange("p r w -> p (r w)")
                        for b, w in ((0, 512), (1, 256)):
                            dve.wait_ge(qkv_done, 4 * t + 1 + b)
                            dve.tensor_copy(qf[:, 512 * b:512 * b + w], banks[q_bank[t][b]][:, 0:w]).then_inc(q_out, 1)
                        dve.tensor_copy(QK[:, t, 8:16, NOPE:QK_W],
                                        proj[:, t, 384:NA0].unsqueeze(1).broadcast_to([P, 8, ROPE])).then_inc(q_out, 1)
                    dve.wait_ge(con_in, 16)
                    for n, (t, v, w, wt, kind) in enumerate(head_norm_steps()):
                        dve.wait_ge(hd_sq, n + 1)
                        own.link(dve.tensor_reduce(hd_ss, SQ[:, 0:16 * w].rearrange("p (r w) -> p r w", r=16), AX, ALU.add))
                        dve.tensor_scalar(hd_m, hd_ss, 1.0 / w, EPS, ALU.mult, ALU.add).then_inc(hd_ms, 1)
                        dve.wait_ge(hd_rstd, n + 1)
                        if kind == "na":
                            dve.wait_ge(proj_act, 4)
                        own.link(dve.tensor_tensor(v, v, hd_r.unsqueeze(2).broadcast_to([P, 16, w]), ALU.mult))
                        v4 = v.rearrange("p (a r) w -> p a r w", a=2)
                        last = dve.tensor_tensor(v4, v4, wt.unsqueeze(2).broadcast_to([P, 2, 8, w]), ALU.mult)
                        if kind == "mla":
                            own.link(last)
                            co = con[:, C_COS + t * ROPE:C_COS + (t + 1) * ROPE]
                            si = con[:, C_SIN + t * ROPE:C_SIN + (t + 1) * ROPE]
                            h2 = ROPE // 2
                            tail = v[:, :, NOPE:QK_W]
                            dve.tensor_tensor(rope_a, tail, co.unsqueeze(1).broadcast_to([P, 16, ROPE]), ALU.mult)
                            dve.tensor_tensor(rope_b[:, :, 0:h2], tail[:, :, h2:ROPE],
                                              si[:, 0:h2].unsqueeze(1).broadcast_to([P, 16, h2]), ALU.mult)
                            own.link(dve.tensor_tensor(rope_b[:, :, h2:ROPE], tail[:, :, 0:h2],
                                                       si[:, h2:ROPE].unsqueeze(1).broadcast_to([P, 16, h2]), ALU.mult))
                            last = dve.tensor_tensor(tail, rope_a, rope_b, ALU.add)
                        last.then_inc(hd_ready, 1)
                    for g in range(0, 12, 2):
                        dve.wait_ge(hdT, g + 1)
                        if g < 8:
                            dve.tensor_copy(QKT[:, 2 * g:2 * g + 2, :],
                                            banks[g % 6][0:QK_W, :].rearrange("p (r t) -> p r t", r=2)).then_inc(hdT_dve, 1)
                        else:
                            dve.tensor_copy(NT[:, 2 * (g - 8):2 * (g - 8) + 2, :],
                                            banks[g % 6][:, :].rearrange("p (r t) -> p r t", r=2)).then_inc(hdT_dve, 1)

                    def heads_out(kind):
                        dve.wait_ge(pv_done, 8 * (kind + 1))
                        own.link(dve.reciprocal(rsum[:, :, 8 * kind:8 * kind + 8], sums[:, :, 8 * kind:8 * kind + 8]))
                        for q in range(2):
                            dve.tensor_tensor(
                                CAT[:, q, 512 * kind:512 * kind + 512].rearrange("p (h w) -> p h w", h=8),
                                banks[4 + 2 * q + kind][:, :].rearrange("p (h w) -> p h w", h=8),
                                rsum[:, q, 8 * kind:8 * kind + 8].unsqueeze(2).broadcast_to([P, 8, HDV]),
                                ALU.mult).then_inc(cat_ready, 1)

                    for g in range(16):
                        dve.wait_ge(s_done, g + 1)
                        sv = banks[g % 2][:, :].rearrange("p (q k) -> p q k", q=2)
                        if g < 8:
                            own.link(dve.tensor_reduce(mx[:, g], sv, AX, ALU.max))
                            dve.tensor_scalar(nmx[:, g], mx[:, g], -SC_MLA, None, ALU.mult).then_inc(nm_ready, 1)
                        else:
                            if g == 8:
                                dve.wait_ge(bias_ready, 2)
                            else:
                                dve.wait_ge(exp_done, g - 1)
                            own.link(dve.scalar_tensor_tensor(logit[:, g % 2], sv, SC_NA, BIAS[:, :, g - 8, :],
                                                              ALU.mult, ALU.add))
                            own.link(dve.tensor_reduce(mx[:, g], logit[:, g % 2], AX, ALU.max))
                            dve.tensor_scalar(nmx[:, g], mx[:, g], -1.0, None, ALU.mult).then_inc(nm_ready, 1)
                        if g == 10:
                            heads_out(0)
                    heads_out(1)
                    for j in (0, 2):
                        dve.wait_ge(catT_done, j + 1)
                        dve.tensor_copy(catT[:, 2 * j:2 * j + 2, :], banks[j][:, :].rearrange("p (k t) -> p k t", k=2)
                                        ).then_inc(catT_dve, 1)
                    dve.wait_ge(mod_in, 48)
                    affine(dve, own_ab[0], 0, 1)
                    affine(dve, own_ab[0], 1, 0)
                    dve.wait_ge(gate_in, 32)
                    own.link(dve.tensor_tensor(gate_bc[:, :], gate_bc[:, :], W[:, 0:D], ALU.add))
                    for t in range(TT):
                        for h in range(2):
                            dve.wait_ge(mix_done, 2 * t + h + 1)
                            cols = slice(512 * h, 512 * h + 512)
                            tmp = W[:, D + 512 * (2 * t + h):D + 512 * (2 * t + h + 1)]
                            own.link(dve.tensor_tensor(tmp, banks[4 + 2 * t + h][:, :], gate_bc[:, cols], ALU.mult))
                            dve.tensor_tensor(X[:, t, cols], X[:, t, cols], tmp, ALU.add)

                @block.tensor
                def _(pe):
                    norm_pe(pe, ns)
                    wait_h(pe, ns)
                    pe.wait_ge(win_in, 64)
                    for t in range(TT):
                        for n, (c0, w) in enumerate(PROJ_COLS):
                            if t and n == 3:
                                pe.wait_ge(proj_dve, 1)
                            for k in range(KC):
                                last = pe.matmul(banks[proj_bank[t][n]][:, 0:w], hT[:, k, t * P:(t + 1) * P],
                                                 WIN[:, k, c0:c0 + w], start=(k == 0), stop=(k == KC - 1))
                            last.then_inc(proj_done, 1)
                            first_unit = KC + 2 * (4 * t + n)
                            multiply_units(pe, first_unit, first_unit + 2, banks[7], c_rep0)
                    pe.wait_ge(proj_act, 1)
                    pe.wait_ge(proj_dve, 2)
                    for t in range(TT):
                        pe.wait_ge(lat_n, t + 1)
                        for ch in range(2):
                            last = pe.transpose(banks[5][:, ch * T + t * P:ch * T + (t + 1) * P],
                                                CQN[:, t, ch * P:(ch + 1) * P], ident)
                    last.then_inc(lat_T, 1)
                    for t in range(TT):
                        last = pe.transpose(banks[6][:, t * P:(t + 1) * P], CQN[:, t, 2 * P:3 * P], ident)
                    last.then_inc(lat_T, 1)
                    pe.wait_ge(wqkv_in, 32)
                    pe.wait_ge(cT_dve, 1)
                    pe.wait_ge(cT_act, 1)
                    pe.wait_ge(proj_dve, 4)
                    pe.wait_ge(proj_act, 4)
                    for t in range(TT):
                        for b, w in ((0, 512), (1, 256)):
                            for k in range(2):
                                last = pe.matmul(banks[q_bank[t][b]][:, 0:w], cT[:, k, t * P:(t + 1) * P],
                                                 WQB[:, k, 512 * b:512 * b + w], start=(k == 0), stop=(k == 1))
                            last.then_inc(qkv_done, 1)
                        for b in range(2):
                            if t and b:
                                pe.wait_ge(q_out, 1)
                            pe.matmul(banks[kv_bank[t][b]][:, :], cT[:, 2, t * P:(t + 1) * P],
                                      WKVB[:, 512 * b:512 * b + 512], start=True, stop=True).then_inc(qkv_done, 1)
                    multiply_units(pe, 3 * KC, MOD_END, banks[7], c_rep0)
                    pe.wait_ge(q_out, 6)
                    pe.wait_ge(kv_out, 8)
                    pe.wait_ge(hd_ready, 2)
                    for g in range(12):
                        if g >= 6:
                            if g % 2:
                                pe.wait_ge(hdT_act, (g - 5) // 2)
                            else:
                                pe.wait_ge(hdT_dve, (g - 4) // 2)
                        if g < 8:
                            for r in range(2):
                                for t in range(TT):
                                    last = pe.transpose(banks[g % 6][0:QK_W, r * T + t * P:r * T + (t + 1) * P],
                                                        QK[:, t, 2 * g + r, :], ident)
                        else:
                            if g == 8:
                                pe.wait_ge(hd_ready, 4)
                            for r in range(2):
                                for t in range(TT):
                                    c0 = NA0 + (2 * (g - 8) + r) * P
                                    last = pe.transpose(banks[g % 6][:, r * T + t * P:r * T + (t + 1) * P],
                                                        proj[:, t, c0:c0 + P], ident)
                        last.then_inc(hdT, 1)
                    pe.wait_ge(hdT_act, 6)
                    pe.wait_ge(hdT_dve, 6)
                    pe.wait_ge(row_copied, 4)

                    def scores(g):
                        if g >= 2:
                            pe.wait_ge(exp_done, g - 1)
                        for q in range(2):
                            if g < 8:
                                lhs, rhs = QKT[:, g, q * P:(q + 1) * P], QKT[:, 8 + g, :]
                            else:
                                h = g - 8
                                b = 64 * (h % 2)
                                lhs, rhs = NT[b:b + 64, h // 2, q * P:(q + 1) * P], NT[b:b + 64, 4 + h // 2, :]
                            last = pe.matmul(banks[g % 2][:, q * T:(q + 1) * T], lhs, rhs, start=True, stop=True)
                        last.then_inc(s_done, 1)

                    def values(g):
                        pe.wait_ge(pT_ready, g + 1)
                        kind, h = g // 8, g % 8
                        for q in range(2):
                            for kt in range(2):
                                v = V[:, kt, h, :] if kind == 0 else \
                                    proj[:, kt, NA0 + 1024 + h * HDV:NA0 + 1024 + (h + 1) * HDV]
                                last = pe.matmul(banks[4 + 2 * q + kind][:, h * HDV:(h + 1) * HDV],
                                                 probT[:, g % 2, kt, q * P:(q + 1) * P], v,
                                                 start=(kt == 0), stop=(kt == 1))
                        last.then_inc(pv_done, 1)

                    scores(0)
                    scores(1)
                    for g in range(16):
                        pe.wait_ge(exp_done, g + 1)
                        if g >= 2:
                            pe.wait_ge(pT_ready, g - 1)
                        for kt in range(2):
                            for q in range(2):
                                last = pe.transpose(banks[2 + g % 2][:, kt * T + q * P:kt * T + (q + 1) * P],
                                                    prob[:, g % 2, q, kt * P:(kt + 1) * P], ident)
                        last.then_inc(pT_done, 1)
                        if g + 2 < 16:
                            scores(g + 2)
                        if g:
                            values(g - 1)
                    values(15)
                    pe.wait_ge(cat_ready, 4)
                    for k in range(KC):
                        for t in range(TT):
                            last = pe.transpose(banks[k // 2][:, (k % 2) * T + t * P:(k % 2) * T + (t + 1) * P],
                                                CAT[:, t, k * P:(k + 1) * P], ident)
                        if k % 2:
                            last.then_inc(catT_done, 1)
                    pe.wait_ge(catT_dve, 2)
                    pe.wait_ge(catT_act, 2)
                    pe.wait_ge(wout_in, 16)
                    for t in range(TT):
                        for h in range(2):
                            for k in range(KC):
                                last = pe.matmul(banks[4 + 2 * t + h][:, :], catT[:, k, t * P:(t + 1) * P],
                                                 WOUT[:, k, 512 * h:512 * h + 512], start=(k == 0), stop=(k == KC - 1))
                            last.then_inc(mix_done, 1)

        def moe(l):
            ns = norm_sems(f"moe{l}_norm")
            names = ("router_in gate_in consts_set logits_done score_ready mask_ready hb_done hb_hi hb_lo "
                     "sh_in sgu_done sg_ready su_ready suT_done suT_ready ssd_done pos_done pos_ready "
                     "first_done table_ready pgT_done pgT_ready pgb_done pgb_ready own_dve "
                     "pick_ready pt_done pT_ready ga_done xg_act xg_dve gu_done silu_done u_ready "
                     "uT_done uT_ready d_done o_hi o_lo sc_done y_done").split()
            (router_in, gate_in, consts_set, logits_done, score_ready, mask_ready, hb_done, hb_hi, hb_lo,
             sh_in, sgu_done, sg_ready, su_ready, suT_done, suT_ready, ssd_done, pos_done, pos_ready,
             first_done, table_ready, pgT_done, pgT_ready, pgb_done, pgb_ready, own_dve,
             pick_ready, pt_done, pT_ready, ga_done, xg_act, xg_dve, gu_done, silu_done, u_ready,
             uT_done, uT_ready, d_done, o_hi, o_lo, sc_done, y_done) = (sem(n) for n in names)
            gu_in = [sem(f"gate_up_in{i}") for i in range(4)]
            dn_in = [sem(f"down_in{i}") for i in range(4)]

            wpos[0] = TT * D
            RW = carve(KC * E_N).rearrange("p (k e) -> p k e", k=KC)
            RB = carve(E_N)
            SG = carve(FF)
            U = carve(FF).rearrange("p (j f) -> p j f", j=2)
            UT = carve(FF).rearrange("p (j s) -> p j s", j=2)
            reused = carve(2 * KC * P)
            SU = reused[:, 0:512].rearrange("p (t j f) -> p t j f", t=TT, j=2)
            SSG = reused[:, 512:1024].rearrange("p (t f) -> p t f", t=TT)
            SUT = reused[:, 1024:1536].rearrange("p (j t) -> p j t", j=2)
            xgT = reused.rearrange("p (u k s) -> p u k s", u=2, k=KC)
            score = carve(TT * E_N).rearrange("p (t e) -> p t e", t=TT)
            sel = carve(TT * E_N).rearrange("p (t e) -> p t e", t=TT)
            top2 = carve(TT * GROUPS * 8).rearrange("p (t g m) -> p t g m", t=TT, g=GROUPS)
            gsc = carve(TT * GROUPS).rearrange("p (t g) -> p t g", t=TT)
            beat = carve(TT * 64).rearrange("p (t g o) -> p t g o", t=TT, g=GROUPS)
            tie = carve(TT * 64).rearrange("p (t g o) -> p t g o", t=TT, g=GROUPS)
            rank = carve(TT * GROUPS).rearrange("p (t g) -> p t g", t=TT)
            gon = carve(TT * GROUPS).rearrange("p (t g) -> p t g", t=TT)
            goff = carve(TT * GROUPS).rearrange("p (t g) -> p t g", t=TT)
            best = carve(TT * 8).rearrange("p (t m) -> p t m", t=TT)
            left = carve(TT * E_N).rearrange("p (t e) -> p t e", t=TT)
            mask = carve(TT * E_N).rearrange("p (t e) -> p t e", t=TT)
            table = carve(2 * TT * NB).rearrange("p (a t b) -> p a t b", a=2, t=TT)
            pg = table[:, :, :, 0:E_N]
            gsum = carve(TT)
            pgT = carve(2 * TT * P)[0:E_N].rearrange("p (a t q) -> p a t q", a=2, t=TT)
            count = carve(4)
            nblk = count[0:E_N, 1:2]
            first = count[0:E_N, 2:3]
            off = carve(NX)[0:E_N]
            has = carve(NX)[0:E_N]
            ge0 = carve(NX)[0:E_N]
            rnd = carve(NX)[0:E_N]
            gcur = carve(2 * TT * 2).rearrange("p (u t b) -> p u t b", u=2, t=TT)
            gslot = carve(1)
            minus = carve(P)[0:E_N]
            ones = carve(P)
            shared = carve(SLOT_W)
            gbias = W[:, 0:D]

            def gu(w, k):
                return w[:, 0:2 * KC * FF].rearrange("p (m k f) -> p k m f", m=2, k=KC)[:, k]

            def down(w, j, h):
                return w[:, 2 * KC * FF:].rearrange("p (j n) -> p j n", j=2)[:, j, 512 * h:512 * h + 512]

            def wait(eng, s, v):
                if not isinstance(v, int) or v > 0:
                    eng.wait_ge(s, v)

            def each_pair(eng, main, tail, total):
                half = MAIN_PAIRS // 2
                main(0, 0, 0)
                main(1, 1, 0)
                with eng.Fori(1, half) as i:
                    main(i * 2, 0, i)
                    main(i * 2 + 1, 1, i)
                tail(None, None, None)
                more = total(eng)
                with eng.If(more > 0):
                    tail(MAIN_PAIRS, 0, half)
                with eng.If(more > 2):
                    tail(MAIN_PAIRS + 1, 1, half)
                    with eng.Fori(1, TAIL_STEPS) as i:
                        for v in range(2):
                            with eng.If(more > i * 4 + 2 * v):
                                tail(i * 2 + (MAIN_PAIRS + v), v, i + half)

            def total_blocks(eng):
                return eng.value_load(ids[0:1, NX:NX + 1], min_val=0, max_val=NX)

            with nc.Block() as block:
                @block.sync
                def _(sp):
                    sp.dma_start(RW, router_w[l].rearrange("(p k) e -> p k e", k=KC)).then_inc(router_in, 16)
                    with nc.allow_non_contiguous_dma("rows for every partition"):
                        sp.dma_start(RB, router_b[l].partition_broadcast(P)).then_inc(router_in, 16)
                        sp.dma_start(gate_bc[:, :], mod_dram[l, 5 * D:6 * D].partition_broadcast(P)
                                     ).then_inc(gate_in, 16)
                    g3 = shared[:, 0:2 * KC * FF].rearrange("p (m k f) -> p m k f", m=2, k=KC)
                    sp.dma_start(g3[:, 0], sh_w_gate[l].rearrange("(p k) f -> p k f", k=KC)).then_inc(sh_in, 16)
                    sp.dma_start(g3[:, 1], sh_w_up[l].rearrange("(p k) f -> p k f", k=KC)).then_inc(sh_in, 16)
                    sp.dma_start(shared[:, 2 * KC * FF:].rearrange("p (j n) -> p j n", j=2),
                                 sh_w_down[l].rearrange("(f j) n -> f j n", j=2)).then_inc(sh_in, 16)

                    def load(n, u, e):
                        wait(sp, gu_done, n - 1)
                        for b in range(2):
                            dst = slot(2 * u + b)[:, 0:2 * KC * FF].rearrange("p (m k f) -> p m k f", m=2, k=KC)
                            for w, src in enumerate((exp_w_gate, exp_w_up)):
                                sp.dma_start(dst[:, w], src[l, bass.ds(e[b], 1)]
                                             .rearrange("o (p k) f -> p (o k) f", k=KC)).then_inc(gu_in[2 * u + b], 16)
                        wait(sp, d_done, n * 2 - 2)
                        for b in range(2):
                            dst = slot(2 * u + b)[:, 2 * KC * FF:].rearrange("p (j n) -> p j n", j=2)
                            sp.dma_start(dst, exp_w_down[l, bass.ds(e[b], 1)]
                                         .rearrange("o (f j) n -> f (o j) n", j=2)).then_inc(dn_in[2 * u + b], 16)

                    def main(n, u, m):
                        load(n, u, [n * 2, n * 2 + 1])

                    def tail(n, u, m):
                        if n is None:
                            sp.wait_ge(table_ready, 1)
                        else:
                            load(n, u, [sp.value_load(ids[0:1, bass.ds(n * 2 + (b - E_N), 1)],
                                                      min_val=0, max_val=E_N - 1) for b in range(2)])

                    each_pair(sp, main, tail, total_blocks)
                    if l == 0:
                        sp.wait_ge(y_done, 1)
                        load_conv_weights(sp)

                @block.gpsimd
                def _(pool):
                    norm_pool(pool, ns)
                    pool.memset(minus, -float(SLOTS)).then_inc(consts_set, 1)
                    pool.memset(zeros[:, :].bitcast(F32), 0.0).then_inc(consts_set, 1)
                    pool.memset(ones, 1.0).then_inc(consts_set, 1)

                @block.scalar
                def _(act):
                    norm_act(act, ns, l, 1)
                    act.wait_ge(logits_done, 1)
                    act.activation(score, banks[4][:, 0:TT * E_N].rearrange("p (t e) -> p t e", t=TT),
                                   ACT.Sigmoid).then_inc(score_ready, 1)
                    act.wait_ge(ns["xn"], 2)
                    for g in range(4):
                        act.wait_ge(hb_done, g + 1)
                        act.copy(H_hi[:, g // 2, 512 * (g % 2):512 * (g % 2) + 512], banks[g][:, :]).then_inc(hb_hi, 1)
                    for t in range(TT):
                        act.wait_ge(sgu_done, t + 1)
                        act.activation(SSG[:, t], banks[6 + t][:, 0:FF], ACT.Silu).then_inc(sg_ready, 1)
                    act.wait_ge(ns["turned"], 4)
                    act.dma_start(gbias, ada_b[l, 5 * D:6 * D].partition_broadcast(P)).then_inc(gate_in, 16)

                    def take(n, u):
                        act.wait_ge(ga_done, n * 2 + 1)
                        wait(act, gu_done, n - 1)
                        act.copy(xgT[:, u, 0:4, :], banks[6][:, :].rearrange("p (k s) -> p k s", k=4)
                                 ).then_inc(xg_act, 1)

                    act.wait_ge(ssd_done, 1)
                    take(0, 0)

                    def pair(n, u, m):
                        act.wait_ge(gu_done, n + 1)
                        wait(act, u_ready, n)
                        act.activation(SG, banks[4][:, 0:FF], ACT.Silu).then_inc(silu_done, 1)
                        take(n + 1, 1 - u)
                        wait(act, sc_done, n)
                        act.wait_ge(pT_ready, n + 1)
                        for h in range(2):
                            act.wait_ge(d_done, n * 2 + (h + 1))
                            act.activation(O_hi[:, 512 * h:512 * h + 512], banks[6 + h][:, :], ACT.Copy,
                                           scale=gslot[:, 0:1]).then_inc(o_hi, 1)

                    def tail(n, u, m):
                        if n is not None:
                            pair(n, u, m)

                    act.wait_ge(table_ready, 1)
                    each_pair(act, pair, tail, total_blocks)

                @block.vector
                def _(dve):
                    own = Chain(dve, own_dve)
                    norm_dve(dve, ns, l, 1)
                    dve.wait_ge(con_in, 16)
                    dve.wait_ge(router_in, 32)
                    dve.wait_ge(score_ready, 1)
                    own.link(dve.tensor_tensor(sel, score, RB.unsqueeze(1).broadcast_to([P, TT, E_N]), ALU.add))
                    for t in range(TT):
                        for g in range(GROUPS):
                            last = dve.max(top2[:, t, g, :], sel[:, t, g * PER_G:(g + 1) * PER_G])
                    own.link(last)
                    own.link(dve.tensor_tensor(gsc, top2[:, :, :, 0], top2[:, :, :, 1], ALU.add))
                    glt = con[:, C_GLT:C_GLT + 64].rearrange("p (g o) -> p g o", g=GROUPS)
                    for t in range(TT):
                        mine = gsc[:, t].unsqueeze(2).broadcast_to([P, GROUPS, GROUPS])
                        other = gsc[:, t].unsqueeze(1).broadcast_to([P, GROUPS, GROUPS])
                        dve.tensor_tensor(beat[:, t], other, mine, ALU.is_gt)
                        own.link(dve.tensor_tensor(tie[:, t], other, mine, ALU.is_equal))
                        own.link(dve.tensor_tensor(tie[:, t], tie[:, t], glt, ALU.mult))
                        own.link(dve.tensor_tensor(beat[:, t], beat[:, t], tie[:, t], ALU.add))
                        own.link(dve.tensor_reduce(rank[:, t], beat[:, t], AX, ALU.add))
                    own.link(dve.tensor_scalar(gon, rank, float(GROUPS_ON), None, ALU.is_lt))
                    own.link(dve.tensor_scalar(goff, gon, -1.0, -NEG, ALU.add, ALU.mult))
                    sel4 = sel.rearrange("p t (g e) -> p (t g) e", g=GROUPS)
                    gon3 = gon.rearrange("p t g -> p (t g)").unsqueeze(2).broadcast_to([P, TT * GROUPS, PER_G])
                    goff3 = goff.rearrange("p t g -> p (t g)").unsqueeze(2).broadcast_to([P, TT * GROUPS, PER_G])
                    own.link(dve.tensor_tensor(sel4, sel4, gon3, ALU.mult))
                    own.link(dve.tensor_tensor(sel4, sel4, goff3, ALU.add))
                    for t in range(TT):
                        own.link(dve.max(best[:, t], sel[:, t]))
                        own.link(dve.match_replace(left[:, t], best[:, t], sel[:, t], -3.0e38))
                    dve.tensor_scalar(mask, left, -2.0e38, None, ALU.is_lt).then_inc(mask_ready, 1)
                    dve.wait_ge(mask_ready, 1)
                    own.link(dve.tensor_tensor(pg[:, 1], score, mask, ALU.mult))
                    own.link(dve.tensor_reduce(gsum, pg[:, 1], AX, ALU.add))
                    own.link(dve.reciprocal(gsum, gsum))
                    for t in range(TT):
                        own.link(dve.tensor_scalar(pg[:, 1, t], pg[:, 1, t], gsum[:, t:t + 1], SCALE_R,
                                                   ALU.mult, ALU.mult))
                    for g in range(4):
                        cols = slice(512 * (g % 2), 512 * (g % 2) + 512)
                        dve.wait_ge(hb_hi, g + 1)
                        dve.tensor_tensor(H_lo[:, g // 2, cols], banks[g][:, :],
                                          H_hi[:, g // 2, cols].bitcast(F32), ALU.subtract).then_inc(hb_lo, 1)
                    for t in range(TT):
                        dve.wait_ge(sg_ready, t + 1)
                        dve.tensor_tensor(SU[:, t].rearrange("p j f -> p f j"),
                                          SSG[:, t].rearrange("p (f j) -> p f j", j=2),
                                          banks[6 + t][:, FF:2 * FF].rearrange("p (f j) -> p f j", j=2),
                                          ALU.mult).then_inc(su_ready, 1)
                    places = con[:, C_SLOT:C_SLOT + SLOTS]

                    def choose(n, u):
                        wait(dve, pt_done, n - 1)
                        dve.tensor_copy(gcur[:, u], table[:, 1, :, bass.ds(n * 2, 2)])
                        for t in range(TT):
                            ins = dve.tensor_tensor(pick[:, u, t, :].rearrange("p (b s) -> p b s", b=2),
                                                    table[:, 0, t, bass.ds(n * 2, 2)].unsqueeze(2)
                                                    .broadcast_to([P, 2, SLOTS]),
                                                    places.unsqueeze(1).broadcast_to([P, 2, SLOTS]), ALU.is_equal)
                        ins.then_inc(pick_ready, 1)

                    def take(n, u):
                        dve.wait_ge(ga_done, n * 2 + 2)
                        wait(dve, gu_done, n - 1)
                        dve.tensor_copy(xgT[:, u, 4:8, :], banks[7][:, :].rearrange("p (k s) -> p k s", k=4)
                                        ).then_inc(xg_dve, 1)

                    dve.wait_ge(pos_done, 1)
                    own.link(dve.tensor_tensor(pg[:, 0], banks[4][:, 128:256].rearrange("p (t e) -> p t e", t=TT),
                                               mask, ALU.mult))
                    own.link(dve.tensor_copy(count[0:E_N, 0:1], banks[4][0:E_N, 256:257]))
                    own.link(dve.tensor_scalar(nblk, count[0:E_N, 0:1], float(SLOTS), None, ALU.is_gt))
                    for r in range(2, T // SLOTS):
                        ins = dve.scalar_tensor_tensor(nblk, count[0:E_N, 0:1], float(r * SLOTS), nblk,
                                                       ALU.is_gt, ALU.add)
                        if r < T // SLOTS - 1:
                            own.link(ins)
                    ins.then_inc(pos_ready, 1)
                    dve.wait_ge(suT_done, 1)
                    dve.tensor_copy(SUT, banks[5][:, :].rearrange("p (j t) -> p j t", j=2)).then_inc(suT_ready, 1)
                    dve.wait_ge(first_done, 1)
                    own.link(dve.tensor_copy(first, banks[4][0:E_N, 260:261]))
                    own.link(dve.tensor_scalar(off, con[0:E_N, C_BLK:C_BLK + NX], first, None, ALU.subtract))
                    own.link(dve.tensor_scalar(ge0, off, 0.0, None, ALU.is_ge))
                    own.link(dve.scalar_tensor_tensor(has, off, nblk, ge0, ALU.is_lt, ALU.mult))
                    dve.scalar_tensor_tensor(rnd, off, 1.0, has, ALU.add, ALU.mult).then_inc(pos_ready, 1)
                    choose(0, 0)
                    dve.wait_ge(pgT_done, 1)
                    dve.tensor_copy(pgT, banks[3][0:E_N, :].rearrange("p (a t q) -> p a t q", a=2, t=TT)
                                    ).then_inc(pgT_ready, 1)
                    dve.wait_ge(ssd_done, 1)
                    take(0, 0)
                    dve.wait_ge(pgb_done, 1)
                    dve.tensor_copy(ids[0:1, 0:NX + 1], banks[4][0:1, 272:272 + NX + 1]).then_inc(table_ready, 1)
                    dve.tensor_copy(table[:, :, :, E_N:NB],
                                    banks[4][:, 320:320 + 2 * TT * NX].rearrange("p (a t b) -> p a t b", a=2, t=TT)
                                    ).then_inc(pgb_ready, 1)
                    dve.wait_ge(pgb_ready, 1)

                    def pair(n, u, m):
                        choose(n + 1, 1 - u)
                        dve.wait_ge(silu_done, n + 1)
                        wait(dve, uT_done, n)
                        dve.tensor_tensor(U.rearrange("p j f -> p f j"), SG.rearrange("p (f j) -> p f j", j=2),
                                          banks[4][:, FF:2 * FF].rearrange("p (f j) -> p f j", j=2),
                                          ALU.mult).then_inc(u_ready, 1)
                        dve.wait_ge(pt_done, n + 1)
                        wait(dve, sc_done, n)
                        wait(dve, o_hi, n * 2)
                        dve.tensor_copy(gslot, banks[5][:, T:T + 1])
                        dve.tensor_copy(pickT[:, :], banks[5][:, 0:T]).then_inc(pT_ready, 1)
                        dve.wait_ge(uT_done, n + 1)
                        wait(dve, d_done, n * 2)
                        dve.tensor_copy(UT, banks[5][:, 0:2 * P].rearrange("p (j s) -> p j s", j=2)
                                        ).then_inc(uT_ready, 1)
                        take(n + 1, 1 - u)
                        for h in range(2):
                            cols = slice(512 * h, 512 * h + 512)
                            dve.wait_ge(o_hi, n * 2 + (h + 1))
                            dve.wait_ge(pT_ready, n + 1)
                            dve.scalar_tensor_tensor(O_lo[:, cols], banks[6 + h][:, :], gslot[:, 0:1],
                                                     O_hi[:, cols].bitcast(F32), ALU.mult,
                                                     ALU.subtract).then_inc(o_lo, 1)

                    def tail(n, u, m):
                        if n is not None:
                            pair(n, u, m)

                    each_pair(dve, pair, tail, total_blocks)
                    dve.wait_ge(gate_in, 32)
                    own.link(dve.tensor_tensor(gate_bc[:, :], gate_bc[:, :], gbias, ALU.add))
                    dve.wait_ge(y_done, 1)
                    for t in range(TT):
                        for h in range(2):
                            cols = slice(512 * h, 512 * h + 512)
                            tmp = xgT.rearrange("p u k s -> p (u k s)")[:, 512 * (2 * t + h):512 * (2 * t + h + 1)]
                            own.link(dve.tensor_tensor(tmp, banks[2 * t + h][:, :], gate_bc[:, cols], ALU.mult))
                            dve.tensor_tensor(X[:, t, cols], X[:, t, cols], tmp, ALU.add)

                @block.tensor
                def _(pe):
                    def gather(n, u, half):
                        pe.wait_ge(pick_ready, n + 1)
                        for k in range(4):
                            kk = 4 * half + k
                            for t in range(TT):
                                for part in (H_hi, H_lo):
                                    last = pe.matmul(banks[6 + half][:, k * P:(k + 1) * P],
                                                     part[:, t, kk * P:(kk + 1) * P], pick[:, u, t, :],
                                                     start=(t == 0 and part is H_hi),
                                                     stop=(t == 1 and part is H_lo))
                        last.then_inc(ga_done, 1)

                    norm_pe(pe, ns)
                    wait_h(pe, ns)
                    pe.wait_ge(router_in, 32)
                    for t in range(TT):
                        for k in range(KC):
                            last = pe.matmul(banks[4][:, t * E_N:(t + 1) * E_N], hT[:, k, t * P:(t + 1) * P],
                                             RW[:, k, :], start=(k == 0), stop=(k == KC - 1))
                    last.then_inc(logits_done, 1)
                    for g in range(4):
                        for k in range(4):
                            kk = 4 * (g % 2) + k
                            last = pe.transpose(banks[g][:, k * P:(k + 1) * P],
                                                hT[:, kk, (g // 2) * P:(g // 2 + 1) * P], ident)
                        last.then_inc(hb_done, 1)
                    pe.wait_ge(sh_in, 48)
                    for t in range(TT):
                        for k in range(KC):
                            last = pe.matmul(banks[6 + t][:, :], hT[:, k, t * P:(t + 1) * P], gu(shared, k),
                                             start=(k == 0), stop=(k == KC - 1))
                        last.then_inc(sgu_done, 1)
                    pe.wait_ge(mask_ready, 1)
                    pe.wait_ge(consts_set, 3)
                    tri = con[:, C_TRI:C_TRI + P]
                    pe.matmul(banks[4][:, 128:192], tri, mask[:, 0, :], start=True, stop=True)
                    pe.matmul(banks[4][:, 192:256], tri, mask[:, 1, :], start=True, stop=False)
                    pe.matmul(banks[4][:, 192:256], ones, mask[:, 0, :], start=False, stop=True)
                    for t in range(TT):
                        last = pe.matmul(banks[4][0:E_N, 256:257], mask[:, t, :], ones[:, 0:1],
                                         start=(t == 0), stop=(t == 1))
                    last.then_inc(pos_done, 1)
                    pe.wait_ge(su_ready, 2)
                    for j in range(2):
                        for t in range(TT):
                            last = pe.transpose(banks[5][:, j * T + t * P:j * T + (t + 1) * P], SU[:, t, j, :], ident)
                    last.then_inc(suT_done, 1)
                    pe.wait_ge(pos_ready, 1)
                    pe.matmul(banks[4][0:E_N, 260:261], con[0:E_N, C_STRICT:C_STRICT + E_N], nblk,
                              start=True, stop=True)
                    pe.matmul(banks[4][0:1, 272 + NX:273 + NX], ones[0:E_N, 0:1], nblk,
                              start=True, stop=True).then_inc(first_done, 1)
                    pe.wait_ge(hb_lo, 4)
                    for a in range(2):
                        for t in range(TT):
                            last = pe.transpose(banks[3][0:E_N, (2 * a + t) * P:(2 * a + t + 1) * P],
                                                pg[:, a, t, :], ident)
                    last.then_inc(pgT_done, 1)
                    gather(0, 0, 0)
                    gather(0, 0, 1)
                    pe.wait_ge(suT_ready, 1)
                    for t in range(TT):
                        for h in range(2):
                            if t and h:
                                pe.wait_ge(pgT_ready, 1)
                            for j in range(2):
                                last = pe.matmul(banks[2 * t + h][:, :], SUT[:, j, t * P:(t + 1) * P],
                                                 down(shared, j, h), start=(j == 0), stop=False,
                                                 skip_group_check=True)
                    last.then_inc(ssd_done, 1)
                    pe.wait_ge(pos_ready, 2)
                    pe.matmul(banks[4][0:1, 272:272 + NX], con[0:E_N, C_EIDX:C_EIDX + 1], has, start=True, stop=True)
                    for t in range(TT):
                        pe.matmul(banks[4][:, 320 + t * NX:320 + (t + 1) * NX], pgT[:, 0, t, :], has,
                                  start=True, stop=False)
                        pe.matmul(banks[4][:, 320 + t * NX:320 + (t + 1) * NX], minus, rnd, start=False, stop=True)
                    for t in range(TT):
                        last = pe.matmul(banks[4][:, 320 + (2 + t) * NX:320 + (3 + t) * NX], pgT[:, 1, t, :], has,
                                         start=True, stop=True)
                    last.then_inc(pgb_done, 1)
                    pe.wait_ge(pgb_ready, 1)

                    def scatter(n):
                        pe.wait_ge(pT_ready, n)
                        pe.wait_ge(o_lo, n * 2)
                        for t in range(TT):
                            for h in range(2):
                                for part in (O_hi, O_lo):
                                    last = pe.matmul(banks[2 * t + h][:, :], pickT[:, t * P:(t + 1) * P],
                                                     part[:, 512 * h:512 * h + 512], start=False, stop=False,
                                                     skip_group_check=True)
                        last.then_inc(sc_done, 1)

                    def pair(n, u, m, in_tail=False):
                        for b in range(2):
                            pe.wait_ge(gu_in[2 * u + b], m * 32 + 32)
                        pe.wait_ge(xg_act, n + 1)
                        pe.wait_ge(xg_dve, n + 1)
                        wait(pe, u_ready, n)
                        for k in range(KC):
                            for b in range(2):
                                last = pe.matmul(banks[4][64 * b:64 * b + 64, :], xgT[:, u, k, 64 * b:64 * b + 64],
                                                 gu(slot(2 * u + b), k), start=(k == 0), stop=(k == KC - 1))
                        last.then_inc(gu_done, 1)
                        if not in_tail and not (isinstance(n, int) and n == 0):
                            scatter(n)
                        wait(pe, uT_ready, n)
                        for t in range(TT):
                            pe.transpose(banks[5][:, t * P:(t + 1) * P], pick[:, u, t, :].bitcast(F32), ident)
                        for b in range(2):
                            for t in range(TT):
                                last = pe.matmul(banks[5][64 * b:64 * b + 64, T:T + 1],
                                                 pick[:, u, t, 64 * b:64 * b + 64].bitcast(F32),
                                                 gcur[:, u, t, b:b + 1], start=(t == 0), stop=(t == 1))
                        last.then_inc(pt_done, 1)
                        gather(n + 1, 1 - u, 0)
                        pe.wait_ge(u_ready, n + 1)
                        pe.wait_ge(pT_ready, n + 1)
                        for j in range(2):
                            last = pe.transpose(banks[5][:, j * P:(j + 1) * P], U[:, j, :], ident)
                        last.then_inc(uT_done, 1)
                        gather(n + 1, 1 - u, 1)
                        for b in range(2):
                            pe.wait_ge(dn_in[2 * u + b], m * 16 + 16)
                        pe.wait_ge(uT_ready, n + 1)
                        for h in range(2):
                            pe.wait_ge(xg_dve if h else xg_act, n + 2)
                            for j in range(2):
                                for b in range(2):
                                    last = pe.matmul(banks[6 + h][64 * b:64 * b + 64, :], UT[:, j, 64 * b:64 * b + 64],
                                                     down(slot(2 * u + b), j, h), start=(j == 0), stop=(j == 1))
                            last.then_inc(d_done, 1)
                        if in_tail:
                            scatter(n + 1)

                    def tail(n, u, m):
                        if n is None:
                            scatter(MAIN_PAIRS)
                        else:
                            pair(n, u, m, in_tail=True)

                    each_pair(pe, pair, tail, total_blocks)
                    pe.wait_ge(pgb_ready, 1)
                    for b in range(4):
                        last = pe.matmul(banks[b][:, :], zeros[:, :], pick[:, :, :, :].rearrange("p u t q -> p (u t q)"),
                                         start=False, stop=True, skip_group_check=True)
                    last.then_inc(y_done, 1)

        PW1 = ring[:, 0:KC * 2 * D].rearrange("p (k n) -> p k n", k=KC)
        PW2 = ring[:, KC * 2 * D:KC * 3 * D].rearrange("p (k n) -> p k n", k=KC)
        pw1_in, pw2_in = sem("pw1_in"), sem("pw2_in")

        def load_conv_weights(sp):
            v = pw1_w[0].rearrange("(p k) n -> p k n", k=KC)
            for k in range(0, KC, 2):
                sp.dma_start(PW1[:, k:k + 2], v[:, k:k + 2]).then_inc(pw1_in, 16)
            sp.dma_start(PW2, pw2_w[0].rearrange("(p k) n -> p k n", k=KC)).then_inc(pw2_in, 16)

        def conv():
            ns = norm_sems("conv_norm")
            names = ("cvec_in gate_in bias_in pads_clear pw1_done sig_ready glu_ready tap_done diag_ready diag_used y_act mean_done "
                     "cen_ready csq_ready var_done var_ready rs_ready yn_ready act_ready pw2_done own_dve ones_set").split()
            (cvec_in, gate_in, bias_in, pads_clear, pw1_done, sig_ready, glu_ready, tap_done, diag_ready, diag_used, y_act, mean_done,
             cen_ready, csq_ready, var_done, var_ready, rs_ready, yn_ready, act_ready, pw2_done, own_dve,
             ones_set) = (sem(n) for n in names)
            wpos[0] = TT * D
            GW = T + 2 * PAD
            G = carve(KC * GW).rearrange("p (m t) -> p m t", m=KC)
            Y = carve(KC * T).rearrange("p (m t) -> p m t", m=KC)
            Ysq = carve(KC * T).rearrange("p (m t) -> p m t", m=KC)
            sig = carve(2 * T).rearrange("p (b t) -> p b t", b=2)
            b1 = carve(2 * KC).rearrange("p (s k) -> p s k", s=2)
            taps = carve(CONV_W * KC).rearrange("p (w k) -> p w k", w=CONV_W)
            vec = carve(3 * KC).rearrange("p (a k) -> p a k", a=3)
            ones = carve(P)
            var = carve(T)
            rs = carve(T)
            b2 = carve(D)
            gbias = carve(D)
            row = carve(ADA_N // 4)
            c_rep = carve(KC * 32).rearrange("p (k m) -> p k m", k=KC)
            S = hT
            VEC_CHUNKS = 6
            HALF_V = VEC_CHUNKS // 2
            PE_TAPS = (KC - VEC_CHUNKS) * CONV_W
            RING = TT * D // P
            diag = W[:, 0:TT * D].rearrange("p (i c) -> p i c", i=RING)
            MOD_FIRST, MOD_MID, MOD_END = 4 * KC, 5 * KC, 6 * KC

            with nc.Block() as block:
                @block.sync
                def _(sp):
                    with nc.allow_non_contiguous_dma("vectors by (p, k), rows for every partition"):
                        sp.dma_start(b1, pw1_b[0].rearrange("(s p k) -> p s k", s=2, k=KC)).then_inc(cvec_in, 16)
                        sp.dma_start(taps, dw_w[0].rearrange("w (p k) -> p w k", k=KC)).then_inc(cvec_in, 16)
                        for a, src in enumerate((dw_b, conv_ln_w, conv_ln_b)):
                            sp.dma_start(vec[:, a], pk(src[0])).then_inc(cvec_in, 16)
                        sp.dma_start(gbias, ada_b[1, 2 * D:3 * D].partition_broadcast(P)).then_inc(gate_in, 16)
                        sp.dma_start(b2, pw2_b[0].partition_broadcast(P)).then_inc(gate_in, 16)
                        sp.wait_ge(pw1_done, KC)
                        load_units(sp, MOD_FIRST, MOD_END)
                        sp.wait_ge(row_stored, 16 * 5)
                        sp.dma_start(gate_bc[:, :], mod_dram[1, 2 * D:3 * D].partition_broadcast(P)
                                     ).then_inc(gate_in, 16)

                @block.gpsimd
                def _(pool):
                    pool.memset(ones, 1.0).then_inc(ones_set, 1)
                    pool.memset(G[:, :, 0:PAD], 0.0)
                    pool.memset(G[:, :, PAD + T:GW], 0.0).then_inc(pads_clear, 1)
                    norm_pool(pool, ns)

                @block.scalar
                def _(act):
                    norm_act(act, ns, 1, 0)
                    act.wait_ge(cvec_in, 80)
                    act.wait_ge(ns["turned"], 4)

                    def diagonal(i):
                        c, w = divmod(i, CONV_W)
                        if i >= RING:
                            act.wait_ge(diag_used, i - RING + 1)
                        act.activation(diag[:, i % RING, :], ident, ACT.Copy,
                                       scale=taps[:, w, VEC_CHUNKS + c:VEC_CHUNKS + c + 1]).then_inc(diag_ready, 1)

                    for i in range(RING):
                        diagonal(i)
                    for m in range(KC):
                        act.wait_ge(pw1_done, m + 1)
                        if m >= 2:
                            act.wait_ge(glu_ready, m - 1)
                        act.activation(sig[:, m % 2], banks[m][:, T:2 * T], ACT.Sigmoid,
                                       bias=b1[:, 1, m:m + 1]).then_inc(sig_ready, 1)
                    for i in range(RING, PE_TAPS):
                        diagonal(i)
                    for c in range(KC - VEC_CHUNKS):
                        m = VEC_CHUNKS + c
                        act.wait_ge(diag_used, (c + 1) * CONV_W)
                        act.activation(Y[:, m], banks[4 + c][:, 0:T], ACT.Identity, bias=vec[:, 0, m:m + 1]
                                       ).then_inc(y_act, 1)
                    row_out(act, 4, banks[3], row)
                    act.wait_ge(cen_ready, 1)
                    act.activation(Ysq, Y, ACT.Square).then_inc(csq_ready, 1)
                    act.wait_ge(var_ready, 1)
                    act.activation(rs, var, ACT.Sqrt).then_inc(rs_ready, 1)
                    for m in range(KC):
                        act.wait_ge(yn_ready, 1)
                        act.activation(S[:, m], Y[:, m], ACT.Silu, bias=vec[:, 2, m:m + 1],
                                       scale=vec[:, 1, m:m + 1]).then_inc(act_ready, 1)
                    row_out(act, 5, banks[3], row)
                    load_mod(act, 1, 3, 5, 6)

                @block.vector
                def _(dve):
                    own = Chain(dve, own_dve)
                    norm_dve(dve, ns, 1, 0)
                    dve.wait_ge(pads_clear, 1)
                    dve.wait_ge(cvec_in, 80)
                    dve.tensor_copy(c_rep, csil.unsqueeze(2).broadcast_to([P, KC, 32])).then_inc(c_rep_ready, 1)

                    def glu(m):
                        dve.wait_ge(sig_ready, m + 1)
                        dve.scalar_tensor_tensor(G[:, m, PAD:PAD + T], banks[m][:, 0:T], b1[:, 0, m:m + 1],
                                                 sig[:, m % 2], ALU.add, ALU.mult).then_inc(glu_ready, 1)

                    def tap(a, w):
                        for j in range(HALF_V):
                            m = HALF_V * a + j
                            if w == 0:
                                ins = dve.tensor_scalar(Y[:, m], G[:, m, 0:T], taps[:, 0, m:m + 1],
                                                        vec[:, 0, m:m + 1], ALU.mult, ALU.add)
                            else:
                                dve.wait_ge(tap_done, HALF_V * (CONV_W * a + w - 1) + j + 1)
                                ins = dve.scalar_tensor_tensor(Y[:, m], G[:, m, w:w + T], taps[:, w, m:m + 1],
                                                               Y[:, m], ALU.mult, ALU.add)
                            ins.then_inc(tap_done, 1)

                    for m in range(HALF_V):
                        glu(m)
                    dve.wait_ge(glu_ready, HALF_V)
                    for w in range(CONV_W):
                        tap(0, w)
                    for m in range(HALF_V, KC - 1):
                        glu(m)
                    dve.wait_ge(glu_ready, VEC_CHUNKS)
                    for w in range(CONV_W):
                        tap(1, w)
                        if w == 3:
                            glu(KC - 1)
                    dve.wait_ge(mean_done, 1)
                    dve.scalar_tensor_tensor(Y, banks[0][:, 0:T].unsqueeze(1).broadcast_to([P, KC, T]), -1.0 / D, Y,
                                             ALU.mult, ALU.add).then_inc(cen_ready, 1)
                    dve.wait_ge(var_done, 1)
                    dve.tensor_scalar(var, banks[1][:, 0:T], 1.0 / D, EPS, ALU.mult, ALU.add).then_inc(var_ready, 1)
                    dve.wait_ge(rs_ready, 1)
                    own.link(dve.reciprocal(rs, rs))
                    dve.tensor_tensor(Y, Y, rs.unsqueeze(1).broadcast_to([P, KC, T]), ALU.mult).then_inc(yn_ready, 1)
                    dve.wait_ge(gate_in, 48)
                    own.link(dve.tensor_tensor(gate_bc[:, :], gate_bc[:, :], gbias, ALU.add))
                    own.link(dve.tensor_tensor(b2, b2, gate_bc[:, :], ALU.mult))
                    for t in range(TT):
                        own.link(dve.tensor_tensor(X[:, t], X[:, t], b2, ALU.add))
                    dve.wait_ge(mod_in, 64)
                    affine(dve, own_ab[0], 1, 1)
                    for t in range(TT):
                        for h in range(2):
                            cols = slice(512 * h, 512 * h + 512)
                            dve.wait_ge(pw2_done, 2 * t + h + 1)
                            tmp = Ysq.rearrange("p m t -> p (m t)")[:, 512 * (2 * t + h):512 * (2 * t + h + 1)]
                            own.link(dve.tensor_tensor(tmp, banks[4 + 2 * t + h][:, :], gate_bc[:, cols], ALU.mult))
                            dve.tensor_tensor(X[:, t, cols], X[:, t, cols], tmp, ALU.add)

                @block.tensor
                def _(pe):
                    norm_pe(pe, ns)
                    wait_h(pe, ns)
                    pe.wait_ge(pw1_in, 64)
                    for m in range(KC):
                        for s in range(2):
                            for k in range(KC):
                                last = pe.matmul(banks[m][:, s * T:(s + 1) * T], PW1[:, k, s * D + m:(s + 1) * D:KC],
                                                 hT[:, k, :], start=(k == 0), stop=(k == KC - 1))
                        last.then_inc(pw1_done, 1)
                    pe.wait_ge(c_rep_ready, 2)
                    pe.wait_ge(pads_clear, 1)
                    pe.wait_ge(ones_set, 1)
                    every = -(-PE_TAPS // (MOD_MID - MOD_FIRST))
                    for i in range(PE_TAPS):
                        c, w = divmod(i, CONV_W)
                        if w == 0:
                            pe.wait_ge(glu_ready, VEC_CHUNKS + c + 1)
                        if i % every == 0:
                            n = MOD_FIRST + i // every
                            multiply_units(pe, n, n + 1, banks[3], c_rep)
                        pe.wait_ge(diag_ready, i + 1)
                        pe.matmul(banks[4 + c][:, 0:T], diag[:, i % RING, :], G[:, VEC_CHUNKS + c, w:w + T],
                                  start=(w == 0), stop=(w == CONV_W - 1)).then_inc(diag_used, 1)
                    for m in range(KC):
                        if m < VEC_CHUNKS:
                            pe.wait_ge(tap_done, HALF_V * (CONV_W * (m // HALF_V + 1) - 1) + m % HALF_V + 1)
                        else:
                            pe.wait_ge(y_act, m - VEC_CHUNKS + 1)
                        last = pe.matmul(banks[0][:, 0:T], ones, Y[:, m], start=(m == 0), stop=(m == KC - 1))
                    last.then_inc(mean_done, 1)
                    multiply_units(pe, MOD_MID, MOD_MID + 3, banks[3], c_rep)
                    pe.wait_ge(csq_ready, 1)
                    for m in range(KC):
                        last = pe.matmul(banks[1][:, 0:T], ones, Ysq[:, m], start=(m == 0), stop=(m == KC - 1))
                    last.then_inc(var_done, 1)
                    multiply_units(pe, MOD_MID + 3, MOD_END, banks[3], c_rep)
                    pe.wait_ge(pw2_in, 16)
                    pe.wait_ge(act_ready, KC)
                    for t in range(TT):
                        for h in range(2):
                            for k in range(KC):
                                last = pe.matmul(banks[4 + 2 * t + h][:, :], S[:, k, t * P:(t + 1) * P],
                                                 PW2[:, k, 512 * h:512 * h + 512], start=(k == 0), stop=(k == KC - 1))
                            last.then_inc(pw2_done, 1)

        with phase():
            attention()
        with phase():
            moe(0)
        with phase():
            conv()
        with phase():
            moe(1)

        stored = sem("stored")
        with nc.Block() as block:
            @block.sync
            def _(sp):
                sp.dma_start(out[0].rearrange("(t p) d -> p t d", p=P), X[:, :, :]).then_inc(stored, 16)
                sp.wait_ge(stored, 16)


def constants():
    import numpy as np
    a = np.zeros((P, C_N), np.float32)
    q = np.arange(P)
    a[:, C_ID:C_ID + P] = np.eye(P)
    a[:, C_TRI:C_TRI + P] = q[:, None] <= q[None, :]
    a[:, C_STRICT:C_STRICT + E_N] = q[:, None] < np.arange(E_N)[None, :]
    a[:, C_SLOT:C_SLOT + SLOTS] = np.arange(1, SLOTS + 1)
    a[:, C_BLK:C_BLK + NX] = np.arange(NX)
    g = np.arange(GROUPS)
    a[:, C_GLT:C_GLT + 64] = (g[None, :] < g[:, None]).reshape(-1)
    a[:, C_EIDX] = q
    n_freq = ROPE // 4
    inv = np.float32(10000.0) ** (-np.arange(n_freq, dtype=np.float32) / np.float32(n_freq))
    t = np.arange(T)
    ang = np.concatenate([(t // GRID_W).astype(np.float32)[:, None] * inv,
                          (t % GRID_W).astype(np.float32)[:, None] * inv], -1).astype(np.float32)
    co, si = np.cos(ang), np.sin(ang)
    for i in range(TT):
        r = slice(i * P, (i + 1) * P)
        a[:, C_COS + i * ROPE:C_COS + (i + 1) * ROPE] = np.concatenate([co[r], co[r]], -1)
        a[:, C_SIN + i * ROPE:C_SIN + (i + 1) * ROPE] = np.concatenate([-si[r], si[r]], -1)
    col = q % GRID_W
    start = np.clip(col - NA_KW // 2, 0, GRID_W - NA_KW)[:, None]
    key = np.arange(GRID_W)[None, :]
    a[:, C_WIN:C_WIN + GRID_W] = np.where((key >= start) & (key < start + NA_KW), 0.0, NEG)
    return a


_INS = ["x", "c", "norm1_w", "norm2_w", "ada_w", "ada_b", "w_in", "q_a_norm_w", "kv_a_norm_w", "w_q_b", "w_kv_b",
        "mla_q_norm_w", "mla_k_norm_w", "na_q_norm_w", "na_k_norm_w", "na_rpb", "w_out", "pw1_w", "pw1_b", "dw_w",
        "dw_b", "conv_ln_w", "conv_ln_b", "pw2_w", "pw2_b", "router_w", "router_b", "exp_w_gate", "exp_w_up",
        "exp_w_down", "sh_w_gate", "sh_w_up", "sh_w_down"]


def kernel(**inputs):
    import numpy as np
    import concourse.bacc as bacc
    from concourse.bass_utils import run_bass_kernel_spmd

    nc = bacc.Bacc("TRN2", target_bir_lowering=False, num_devices=1)
    arrays, args = {}, []
    for name in _INS:
        a = np.ascontiguousarray(inputs[name])
        arrays[f"in_{name}"] = a
        args.append(nc.dram_tensor(f"in_{name}", a.shape, mybir.dt.from_np(a.dtype), kind="ExternalInput").ap())
    arrays["in_consts"] = constants()
    args.append(nc.dram_tensor("in_consts", (P, C_N), F32, kind="ExternalInput").ap())
    args.append(nc.dram_tensor("out_0", (1, T, D), F32, kind="ExternalOutput").ap())
    build_encoder(nc, *args)
    r = run_bass_kernel_spmd(nc, [arrays], core_ids=[0])
    return r.results[0]["out_0"]
```

```python
from contextlib import ExitStack, contextmanager

import concourse.bass as bass
from concourse import mybir

P = 128
F32 = mybir.dt.float32
F32R = mybir.dt.float32r
I32 = mybir.dt.int32
ALU = mybir.AluOpType
ACT = mybir.ActivationFunctionType
AX = mybir.AxisListType.X

D = 1024
KC = D // P
T = 256
TT = T // P
EPS = 1e-6
Q_LORA, KV_LORA, ROPE = 256, 128, 32
HEADS, NOPE, HDV = 8, 64, 64
QK_W = NOPE + ROPE
IN_COLS = Q_LORA + KV_LORA + ROPE + 3 * HEADS * HDV
NA0 = Q_LORA + KV_LORA + ROPE
GRID_W, NA_KH, NA_KW = 64, 8, 16
ROWS = T // GRID_W
RPB_H, RPB_W = 2 * NA_KH - 1, 2 * NA_KW - 1
TOE = 2 * GRID_W - 1
CONV_W = 31
PAD = CONV_W // 2
E_N, FF, GROUPS, GROUPS_ON = 64, 256, 8, 4
PER_G = E_N // GROUPS
SCALE_R = 2.5
SLOTS = 64
TOP_K = 8
MAIN_PAIRS = E_N // 2
MAX_MORE = (T * TOP_K) // SLOTS
TAIL_STEPS = MAX_MORE // 4
NX = MAX_MORE + 2
NB = E_N + NX
SLOT_W = KC * 2 * FF + 2 * D
ADA_N = 2 * D
ADA_G = 6 * D // ADA_N
NEG = -1.0e30
W_COLS = 15232

C_ID = 0
C_TRI = C_ID + P
C_STRICT = C_TRI + P
C_SLOT = C_STRICT + E_N
C_BLK = C_SLOT + SLOTS
C_GLT = C_BLK + NX
C_EIDX = C_GLT + GROUPS * GROUPS
C_COS = C_EIDX + 1
C_SIN = C_COS + TT * ROPE
C_WIN = C_SIN + TT * ROPE
C_N = C_WIN + GRID_W


class Chain:

    def __init__(self, eng, sem):
        self.eng, self.sem, self.n = eng, sem, 0

    def link(self, ins):
        self.n += 1
        ins.then_inc(self.sem, 1)
        self.eng.wait_ge(self.sem, self.n)


def build_encoder(nc, x, c, norm1_w, norm2_w, ada_w, ada_b, w_in, q_a_norm_w, kv_a_norm_w,
                  w_q_b, w_kv_b, mla_q_norm_w, mla_k_norm_w, na_q_norm_w, na_k_norm_w,
                  na_rpb, w_out, pw1_w, pw1_b, dw_w, dw_b, conv_ln_w, conv_ln_b, pw2_w,
                  pw2_b, router_w, router_b, exp_w_gate, exp_w_up, exp_w_down,
                  sh_w_gate, sh_w_up, sh_w_down, consts, out):
    ctx = ExitStack()
    with ctx:
        def sb(name, shape, dt=F32):
            return ctx.enter_context(nc.sbuf_tensor(name, shape, dt))

        banks = [ctx.enter_context(nc.psum_tensor(f"bank{i}", [P, 512], F32)) for i in range(8)]

        con = sb("con", [P, C_N])
        ident = con[:, C_ID:C_ID + P]
        X = sb("X", [P, TT, D])
        hT = sb("hT", [P, KC, T])
        ring = sb("ring", [P, 4 * SLOT_W])
        W = sb("W", [P, W_COLS])
        split = sb("split", [P, 2 * TT * D + 2 * D], F32R)
        H_hi, H_lo = (split[:, a * TT * D:(a + 1) * TT * D].rearrange("p (t d) -> p t d", t=TT) for a in range(2))
        O_hi, O_lo = (split[:, 2 * TT * D + a * D:2 * TT * D + (a + 1) * D] for a in range(2))
        pick = sb("pick", [P, 2, TT, P], F32R)
        zeros = sb("zeros", [P, P], F32R)
        pickT = sb("pickT", [P, T], F32R)
        AB = sb("AB", [P, 2, 2, 2, KC])
        gate_bc = sb("gate_bc", [P, D])
        eps_half = sb("eps_half", [P, 16])
        small = sb("small", [P, 440])
        ids = sb("ids", [1, NX + 2], I32)

        sem_stack = [ctx]
        phase_sems, last_sems, last_stack = [], [], []
        phase_tag = [""]

        def sem(name):
            s = sem_stack[-1].enter_context(nc.semaphore(phase_tag[0] + name))
            phase_sems.append(s)
            return s

        @contextmanager
        def phase(tag):
            stack = ExitStack()
            phase_tag[0] = tag + "_"
            sem_stack.append(stack)
            phase_sems.clear()
            yield
            sem_stack.pop()
            last_sems[:] = phase_sems
            for old in last_stack:
                old.close()
            last_stack[:] = [stack]

        def clear_last_phase(pool):
            for s in last_sems:
                pool.sem_clear(s)

        wpos = [0]

        def carve(n):
            a = wpos[0]
            wpos[0] += n
            assert wpos[0] <= W_COLS
            return W[:, a:a + n]

        def slot(s):
            return ring[:, s * SLOT_W:(s + 1) * SLOT_W]

        mod_dram = nc.dram_tensor("mod_scratch", [2, 6 * D], F32).ap()
        toe_dram = nc.dram_tensor("toeplitz_scratch", [HEADS * RPB_H, GRID_W, GRID_W], F32).ap()

        def pk(row):
            return row.rearrange("(p k) -> p k", k=KC)

        def norm_sems(tag):
            return {k: sem(f"{tag}_{k}") for k in
                    ("squared", "mean", "rstd", "xn", "turned", "h_dve", "h_act")}

        XN = W[:, 0:TT * D].rearrange("p (t d) -> p t d", t=TT)
        ss = small[:, 0:2]
        ms = small[:, 2:4]
        rstd = small[:, 4:6]

        def norm_act(act, s, l, which):
            for t in range(TT):
                act.activation(XN[:, t, :], X[:, t, :], ACT.Square,
                               accum_out=ss[:, t:t + 1]).then_inc(s["squared"], 1)
            for j in (1, 3):
                act.wait_ge(s["turned"], j + 1)
                for k in (2 * j, 2 * j + 1):
                    act.activation(hT[:, k, :], banks[j][:, (k % 2) * T:(k % 2 + 1) * T], ACT.Identity,
                                   bias=AB[:, l, which, 1, k:k + 1],
                                   scale=AB[:, l, which, 0, k:k + 1]).then_inc(s["h_act"], 1)

        def norm_pool(pool, s):
            pool.wait_ge(s["mean"], 1)
            pool.tensor_tensor(rstd, ms, eps_half[:, 0:2], ALU.pow).then_inc(s["rstd"], 1)

        def norm_dve(dve, s, l, which):
            dve.wait_ge(s["squared"], 2)
            dve.tensor_scalar(ms, ss, 1.0 / D, EPS, ALU.mult, ALU.add).then_inc(s["mean"], 1)
            dve.wait_ge(s["rstd"], 1)
            for t in range(TT):
                dve.tensor_scalar(XN[:, t, :], X[:, t, :], rstd[:, t:t + 1], None,
                                  ALU.mult).then_inc(s["xn"], 1)
            for j in (0, 2):
                dve.wait_ge(s["turned"], j + 1)
                for k in (2 * j, 2 * j + 1):
                    dve.tensor_scalar(hT[:, k, :], banks[j][:, (k % 2) * T:(k % 2 + 1) * T],
                                      AB[:, l, which, 0, k:k + 1], AB[:, l, which, 1, k:k + 1],
                                      ALU.mult, ALU.add).then_inc(s["h_dve"], 1)

        def norm_pe(pe, s):
            pe.wait_ge(s["xn"], 2)
            for k in range(KC):
                for t in range(TT):
                    last = pe.transpose(banks[k // 2][:, (k % 2) * T + t * P:(k % 2) * T + (t + 1) * P],
                                        XN[:, t, k::KC], ident)
                if k % 2:
                    last.then_inc(s["turned"], 1)

        def wait_h(eng, s):
            eng.wait_ge(s["h_dve"], 4)
            eng.wait_ge(s["h_act"], 4)

        first_gu = [[sem(f"gate_up_in_l{l}_pair{n}") for n in range(2)] for l in range(2)]
        first_dn = [[sem(f"down_in_l{l}_pair{n}") for n in range(2)] for l in range(2)]

        def load_gate_up(sp, l, u, experts, sems):
            for b in range(2):
                dst = slot(2 * u + b)[:, 0:2 * KC * FF].rearrange("p (m k f) -> p m k f", m=2, k=KC)
                for w, src in enumerate((exp_w_gate, exp_w_up)):
                    sp.dma_start(dst[:, w], src[l, bass.ds(experts[b], 1)].rearrange("o (p k) f -> p (o k) f", k=KC)
                                 ).then_inc(sems[b], 16)

        def load_down(sp, l, u, experts, sems):
            for b in range(2):
                dst = slot(2 * u + b)[:, 2 * KC * FF:].rearrange("p (j n) -> p j n", j=2)
                sp.dma_start(dst, exp_w_down[l, bass.ds(experts[b], 1)].rearrange("o (f j) n -> f (o j) n", j=2)
                             ).then_inc(sems[b], 16)

        def load_first_pair(sp, l, n):
            load_gate_up(sp, l, n, [2 * n, 2 * n + 1], [first_gu[l][n]] * 2)
            load_down(sp, l, n, [2 * n, 2 * n + 1], [first_dn[l][n]] * 2)

        ada_in = [sem(f"ada_in{i}") for i in range(3)]
        ada_done, row_copied, row_stored = sem("ada_done"), sem("row_copied"), sem("row_stored")
        mod_in, ab_step, c_rep_ready = sem("mod_in"), sem("ab_step"), sem("c_rep_ready")
        row0 = gate_bc[:, 0:ADA_N // 4]
        c_rep0 = gate_bc[:, 512:768].rearrange("p (k m) -> p k m", k=KC)
        nw = small[:, 208:240].rearrange("p (w l k) -> p w l k", w=2, l=2)
        bcol = small[:, 240:336].rearrange("p (l j k) -> p l j k", l=2, j=6)
        mcol = small[:, 336:432].rearrange("p (l j k) -> p l j k", l=2, j=6)
        csil = small[:, 432:440]
        mod_groups = mod_dram.rearrange("l (j q n) -> (l j) q n", j=ADA_G, q=4)

        def ada_buf(n):
            return slot(2 if n >= 4 * KC else 3)[:, n % 3 * ADA_N:(n % 3 + 1) * ADA_N]

        def load_units(sp, n0, n1):
            for n in range(n0, n1):
                g, k = divmod(n, KC)
                l, j = divmod(g, ADA_G)
                if n >= 3:
                    sp.wait_ge(ada_done, n - 2)
                sp.dma_start(ada_buf(n),
                             ada_w[l].rearrange("(p k) n -> p k n", k=KC)[:, k, j * ADA_N:(j + 1) * ADA_N]
                             ).then_inc(ada_in[n % 3], 16)

        def multiply_units(pe, n0, n1, bank, c_rep):
            for n in range(n0, n1):
                g, k = divmod(n, KC)
                if k == 0 and g:
                    pe.wait_ge(row_copied, g)
                pe.wait_ge(ada_in[n % 3], 16 * (n // 3 + 1))
                for q in range(4):
                    last = pe.matmul(bank[32 * q:32 * q + 32, :], c_rep[:, k, :],
                                     ada_buf(n)[:, 512 * q:512 * q + 512], start=(k == 0), stop=(k == KC - 1))
                last.then_inc(ada_done, 1)

        def row_out(act, g, bank, row):
            act.wait_ge(ada_done, KC * (g + 1))
            if g:
                act.wait_ge(row_stored, 16 * g)
            act.copy(row, bank[:, :]).then_inc(row_copied, 1)
            act.wait_ge(row_copied, g + 1)
            act.dma_start(mod_groups[g], row[0:97:32, :]).then_inc(row_stored, 16)

        def load_mod(act, l, j0, j1, groups):
            act.wait_ge(row_stored, 16 * groups)
            with nc.allow_non_contiguous_dma("vectors by (p, k)"):
                act.dma_start(mcol[:, l, j0:j1], mod_dram[l, j0 * D:j1 * D].rearrange("(j p k) -> p j k", p=P, k=KC)
                              ).then_inc(mod_in, 16)

        def affine(dve, own, l, which):
            own.eng = dve
            j = slice(3 * which, 3 * which + 2)
            own.link(dve.tensor_tensor(mcol[:, l, j], mcol[:, l, j], bcol[:, l, j], ALU.add))
            own.link(dve.scalar_tensor_tensor(AB[:, l, which, 0], mcol[:, l, 3 * which + 1], 1.0, nw[:, which, l],
                                              ALU.add, ALU.mult))
            own.link(dve.tensor_copy(AB[:, l, which, 1], mcol[:, l, 3 * which]))

        c_in, con_in, x_in, vec_in = sem("c_in"), sem("con_in"), sem("x_in"), sem("vec_in")
        c_silu = sem("c_silu")
        toe_zeroed, toe_in, toe_stored = sem("toe_zeroed"), sem("toe_in"), sem("toe_stored")
        vecs_in = sem("vecs_in")
        win_in, wqkv_in = [sem(f"win_in{c}") for c in range(KC // 2)], sem("wqkv_in")
        ccol = small[:, 8:16]
        QK_AT = TT * IN_COLS + TT * 384 + 3 * T
        toe = W[0:HEADS * RPB_H, QK_AT + GRID_W * GRID_W:QK_AT + GRID_W * GRID_W + TOE + 1]
        skew = W[0:HEADS * RPB_H, QK_AT:QK_AT + GRID_W * GRID_W].rearrange("p (c k) -> p c k", c=GRID_W)
        toe_skewed = sem("toe_skewed")
        WIN = ring[:, 0:KC * IN_COLS].rearrange("p (k n) -> p k n", k=KC)
        WQB = ring[:, KC * IN_COLS:KC * IN_COLS + 2 * 768].rearrange("p (k n) -> p k n", k=2)
        WKVB = ring[:, KC * IN_COLS + 1536:KC * IN_COLS + 1536 + D]
        mod_chain = [None]

        with nc.Block() as block:
            @block.sync
            def _(sp):
                with nc.allow_non_contiguous_dma("vectors by (p, k)"):
                    sp.dma_start(ccol, pk(c[0, :])).then_inc(c_in, 16)
                load_units(sp, 0, 3)
                sp.dma_start(con[:, :], consts).then_inc(con_in, 16)
                load_units(sp, 3, KC)
                sp.dma_start(X[:, :, :], x[0].rearrange("(t p) d -> p t d", p=P)).then_inc(x_in, 16)
                wv = w_in[0].rearrange("(p k) n -> p k n", k=KC)
                for k in range(0, KC, 2):
                    if k == 2:
                        sp.wait_ge(mod_in, 16)
                    sp.dma_start(WIN[:, k:k + 2, :], wv[:, k:k + 2, :]).then_inc(win_in[k // 2], 16)

            @block.gpsimd
            def _(pool):
                pool.memset(eps_half[:, :], -0.5)
                pool.memset(toe, 0.0).then_inc(toe_zeroed, 1)
                pool.wait_ge(toe_zeroed, 1)
                pool.dma_start(toe[:, GRID_W - NA_KW:GRID_W - NA_KW + RPB_W],
                               na_rpb[0].rearrange("h i j -> (h i) j")).then_inc(toe_in, 16)
                pool.wait_ge(toe_in, 16)

            @block.scalar
            def _(act):
                act.wait_ge(c_in, 16)
                act.activation(csil, ccol, ACT.Silu).then_inc(c_silu, 1)
                with nc.allow_non_contiguous_dma("vectors by (p, k)"):
                    act.dma_start(nw[:, 0], norm1_w.rearrange("l (p k) -> p l k", k=KC)).then_inc(vec_in, 16)
                    act.dma_start(nw[:, 1], norm2_w.rearrange("l (p k) -> p l k", k=KC)).then_inc(vec_in, 16)
                    for l in range(2):
                        act.dma_start(bcol[:, l], ada_b[l].rearrange("(j p k) -> p j k", p=P, k=KC)
                                      ).then_inc(vec_in, 16)
                row_out(act, 0, banks[7], row0)
                load_mod(act, 0, 0, 2, 1)

            @block.vector
            def _(dve):
                own = mod_chain[0] = Chain(dve, ab_step)
                dve.wait_ge(c_silu, 1)
                dve.tensor_copy(c_rep0, csil.unsqueeze(2).broadcast_to([P, KC, 32])).then_inc(c_rep_ready, 1)
                dve.wait_ge(toe_in, 16)
                last = toe[:, GRID_W - 1:TOE]
                by_query = bass.AP(tensor=last.tensor, offset=last.offset,
                                   ap=[list(last.ap[0]), [-1, GRID_W], [1, GRID_W]])
                dve.tensor_copy(skew, by_query).then_inc(toe_skewed, 1)
                dve.wait_ge(vec_in, 64)
                dve.wait_ge(mod_in, 16)
                affine(dve, own, 0, 0)

            @block.tensor
            def _(pe):
                pe.wait_ge(c_rep_ready, 1)
                multiply_units(pe, 0, KC, banks[7], c_rep0)

        def attention():
            ns = norm_sems("attn_norm")
            wout_in = sem("wout_in")
            bias_in, bias_ready, gate_in = sem("bias_in"), sem("bias_ready"), sem("gate_in")
            proj_done, proj_dve, proj_act = sem("proj_done"), sem("proj_dve"), sem("proj_act")
            lat_sq, lat_ms, lat_rstd, lat_n, lat_T, cT_dve, cT_act = (
                sem(n) for n in ("lat_sq", "lat_ms", "lat_rstd", "lat_n", "lat_T", "cT_dve", "cT_act"))
            qkv_done, q_out, kv_out = sem("qkv_done"), sem("q_out"), sem("kv_out")
            hd_sq, hd_ms, hd_rstd, hd_ready, hdT, hdT_dve, hdT_act = (
                sem(n) for n in ("hd_sq", "hd_ms", "hd_rstd", "hd_ready", "hdT", "hdT_dve", "hdT_act"))
            s_done, nm_ready, exp_done, pT_done, pT_ready, pv_done = (
                sem(n) for n in ("s_done", "nm_ready", "exp_done", "pT_done", "pT_ready", "pv_done"))
            cat_ready, catT_done, catT_dve, catT_act, mix_done = (
                sem(n) for n in ("cat_ready", "catT_done", "catT_dve", "catT_act", "mix_done"))
            at_dve = sem("at_dve")

            wpos[0] = 0
            proj = carve(TT * IN_COLS).rearrange("p (t n) -> p t n", t=TT)
            CQN = carve(TT * 384).rearrange("p (t n) -> p t n", t=TT)
            cT = carve(3 * T).rearrange("p (c t) -> p c t", c=3)
            assert wpos[0] == QK_AT
            QK = carve(TT * 16 * QK_W).rearrange("p (t r w) -> p t r w", t=TT, r=16)
            V = carve(TT * 512).rearrange("p (t h w) -> p t h w", t=TT, h=HEADS)
            SQ = carve(16 * QK_W)
            CAT = carve(TT * D).rearrange("p (t d) -> p t d", t=TT)
            turned_at = carve(1024)
            rope_a = turned_at[:, 0:512].rearrange("p (r w) -> p r w", r=16)
            rope_b = turned_at[:, 512:1024].rearrange("p (r w) -> p r w", r=16)
            qkw = carve(2 * QK_W).rearrange("p (a w) -> p a w", a=2)
            naw = carve(2 * HDV).rearrange("p (a w) -> p a w", a=2)
            qaw = carve(Q_LORA)
            kvaw = carve(KV_LORA)
            Pr = W[:, TT * IN_COLS:TT * IN_COLS + 1536]
            assert TT * 384 + 3 * T == 1536
            prob = Pr[:, 0:1024].rearrange("p (b q k) -> p b q k", b=2, q=2)
            logit = SQ[:, 0:1024].rearrange("p (b q k) -> p b q k", b=2, q=2)
            probT = turned_at.rearrange("p (b c q) -> p b c q", b=2, c=2)
            assert KC * IN_COLS + 1536 + D <= 3 * SLOT_W
            WOUT = ring[:, 0:KC * D].rearrange("p (k n) -> p k n", k=KC)
            BIAS = ring[:, KC * D:KC * D + TT * HEADS * T].rearrange("p (t h k) -> p t h k", t=TT, h=HEADS)
            assert KC * D + TT * HEADS * T <= KC * IN_COLS
            QKT = slot(3)[0:QK_W, 0:16 * T].rearrange("p (r t) -> p r t", r=16)
            NT = slot(2)[:, 0:8 * T].rearrange("p (r t) -> p r t", r=8)
            catT = hT
            lat_ss = small[:, 8:12].rearrange("p (t a) -> p t a", t=2)
            lat_m = small[:, 12:16].rearrange("p (t a) -> p t a", t=2)
            lat_r = small[:, 16:20].rearrange("p (t a) -> p t a", t=2)
            hd_ss, hd_m, hd_r = ([small[:, 32 + 48 * u + 16 * a:48 + 48 * u + 16 * a] for u in range(2)]
                                 for a in range(3))
            mx = small[:, 80:112].rearrange("p (g q) -> p g q", q=2)
            nmx = small[:, 112:144].rearrange("p (g q) -> p g q", q=2)
            sums = small[:, 144:176].rearrange("p (q g) -> p q g", q=2)
            rsum = small[:, 176:208].rearrange("p (q g) -> p q g", q=2)
            PROJ_COLS = [(0, NA0)] + [(NA0 + 512 * i, 512) for i in range(3)]
            proj_bank = [[4, 5, 6, 0], [1, 2, 3, 4]]
            q_bank = [[0, 1], [4, 5]]
            kv_bank = [[2, 3], [6, 0]]
            MOD_END = 4 * KC
            UNITS_AFTER = [0, 1, 2, 3, 2, 3, 3, 2]
            SC_MLA, SC_NA = QK_W ** -0.5, HDV ** -0.5
            toe_v = toe_dram.rearrange("(h i) c k -> h i c k", h=HEADS)

            HD = [(t, proj[:, t, NA0:NA0 + 1024].rearrange("p (r w) -> p r w", r=16), HDV, naw, False)
                  for t in range(TT)]
            HD += [(t, QK[:, t], QK_W, qkw, True) for t in range(TT)]
            hd_square = [SQ, CAT.rearrange("p t d -> p (t d)")]

            def square_heads(act, n):
                t, v, w, _, latent = HD[n]
                if n >= 2:
                    act.wait_ge(hd_ms, n - 1)
                if latent:
                    act.wait_ge(q_out, 3 * (t + 1))
                    act.wait_ge(kv_out, 4 * (t + 1))
                else:
                    act.wait_ge(proj_dve, 2 * (t + 1))
                    act.wait_ge(proj_act, 2 * t + 1)
                act.activation(hd_square[n % 2][:, 0:16 * w].rearrange("p (r w) -> p r w", r=16), v, ACT.Square
                               ).then_inc(hd_sq, 1)

            def head_means(dve, own, n):
                _, _, w, _, _ = HD[n]
                dve.wait_ge(hd_sq, n + 1)
                own.link(dve.tensor_reduce(hd_ss[n % 2], hd_square[n % 2][:, 0:16 * w]
                                           .rearrange("p (r w) -> p r w", r=16), AX, ALU.add))
                dve.tensor_scalar(hd_m[n % 2], hd_ss[n % 2], 1.0 / w, EPS, ALU.mult, ALU.add).then_inc(hd_ms, 1)

            def scale_heads(dve, own, n):
                t, v, w, wt, latent = HD[n]
                dve.wait_ge(hd_rstd, n + 1)
                if not latent:
                    dve.wait_ge(proj_act, 2 * t + 1)
                own.link(dve.tensor_tensor(v, v, hd_r[n % 2].unsqueeze(2).broadcast_to([P, 16, w]), ALU.mult))
                v4 = v.rearrange("p (a r) w -> p a r w", a=2)
                last = dve.tensor_tensor(v4, v4, wt.unsqueeze(2).broadcast_to([P, 2, 8, w]), ALU.mult)
                if latent:
                    own.link(last)
                    co = con[:, C_COS + t * ROPE:C_COS + (t + 1) * ROPE]
                    si = con[:, C_SIN + t * ROPE:C_SIN + (t + 1) * ROPE]
                    h2 = ROPE // 2
                    tail = v[:, :, NOPE:QK_W]
                    dve.tensor_tensor(rope_a, tail, co.unsqueeze(1).broadcast_to([P, 16, ROPE]), ALU.mult)
                    dve.tensor_tensor(rope_b[:, :, 0:h2], tail[:, :, h2:ROPE],
                                      si[:, 0:h2].unsqueeze(1).broadcast_to([P, 16, h2]), ALU.mult)
                    own.link(dve.tensor_tensor(rope_b[:, :, h2:ROPE], tail[:, :, 0:h2],
                                               si[:, h2:ROPE].unsqueeze(1).broadcast_to([P, 16, h2]), ALU.mult))
                    last = dve.tensor_tensor(tail, rope_a, rope_b, ALU.add)
                last.then_inc(hd_ready, 1)

            TURN = list(range(8, 12)) + list(range(8))

            def turned_to(i):
                g = TURN[i]
                if g < 8:
                    return QKT[:, 2 * g:2 * g + 2, :], banks[i % 6][0:QK_W, :].rearrange("p (r t) -> p r t", r=2)
                return NT[:, 2 * (g - 8):2 * (g - 8) + 2, :], banks[i % 6][:, :].rearrange("p (r t) -> p r t", r=2)

            with nc.Block() as block:
                @block.sync
                def _(sp):
                    load_units(sp, KC, 2 * KC)
                    sp.dma_start(WQB, w_q_b[0].rearrange("(k p) n -> p k n", k=2)).then_inc(wqkv_in, 16)
                    sp.dma_start(WKVB, w_kv_b[0]).then_inc(wqkv_in, 16)
                    load_units(sp, 2 * KC, MOD_END)
                    sp.wait_ge(proj_done, 8)
                    sp.wait_ge(toe_stored, 16)
                    for t in range(TT):
                        for r2 in range(2):
                            r = 2 * t + r2
                            for h in range(HEADS):
                                src = toe_v[h, NA_KH - 1 - r:NA_KH - 1 - r + ROWS].rearrange("r c k -> c r k")
                                sp.dma_start(BIAS[64 * r2:64 * r2 + 64, t, h, :].rearrange("p (r c) -> p r c", r=ROWS),
                                             src).then_inc(bias_in, 16)
                    sp.dma_start(WOUT, w_out[0].rearrange("(k p) n -> p k n", k=KC)).then_inc(wout_in, 16)
                    sp.wait_ge(bias_in, 16 * 2 * TT * HEADS)
                    sp.wait_ge(s_done, 2 * HEADS)
                    load_first_pair(sp, 0, 1)

                @block.gpsimd
                def _(pool):
                    norm_pool(pool, ns)
                    with nc.allow_non_contiguous_dma("rows for every partition"):
                        pool.dma_start(qkw[:, 0], mla_q_norm_w[0].partition_broadcast(P)).then_inc(vecs_in, 16)
                        pool.dma_start(qkw[:, 1], mla_k_norm_w[0].partition_broadcast(P)).then_inc(vecs_in, 16)
                        pool.dma_start(naw[:, 0], na_q_norm_w[0].partition_broadcast(P)).then_inc(vecs_in, 16)
                        pool.dma_start(naw[:, 1], na_k_norm_w[0].partition_broadcast(P)).then_inc(vecs_in, 16)
                        pool.dma_start(qaw, q_a_norm_w[0].partition_broadcast(P)).then_inc(vecs_in, 16)
                        pool.dma_start(kvaw, kv_a_norm_w[0].partition_broadcast(P)).then_inc(vecs_in, 16)
                    pool.wait_ge(toe_skewed, 1)
                    pool.wait_ge(win_in[-1], 16)
                    pool.dma_start(toe_dram, skew).then_inc(toe_stored, 16)
                    for n in range(len(HD)):
                        pool.wait_ge(hd_ms, n + 1)
                        pool.tensor_tensor(hd_r[n % 2], hd_m[n % 2], eps_half[:, 0:16], ALU.pow).then_inc(hd_rstd, 1)
                        if n == 0:
                            pool.wait_ge(lat_ms, 1)
                            pool.tensor_tensor(lat_r, lat_m, eps_half[:, 0:4].rearrange("p (t a) -> p t a", t=2),
                                               ALU.pow).then_inc(lat_rstd, 1)
                    pool.wait_ge(bias_in, 16 * 2 * TT * HEADS)
                    for t in range(TT):
                        v = BIAS[:, t].rearrange("p h (r c) -> p (h r) c", r=ROWS)
                        pool.tensor_tensor(v, v, con[:, C_WIN:C_WIN + GRID_W].unsqueeze(1)
                                           .broadcast_to([P, HEADS * ROWS, GRID_W]), ALU.add).then_inc(bias_ready, 1)

                @block.scalar
                def _(act):
                    act.wait_ge(x_in, 16)
                    norm_act(act, ns, 0, 0)
                    for t in range(TT):
                        for n in (1, 3):
                            act.wait_ge(proj_done, 4 * t + n + 1)
                            c0, w = PROJ_COLS[n]
                            act.copy(proj[:, t, c0:c0 + w], banks[proj_bank[t][n]][:, 0:w]).then_inc(proj_act, 1)
                        if t == 0:
                            square_heads(act, 0)
                        row_out(act, t + 1, banks[7], row0)
                    act.wait_ge(hd_ms, 1)
                    for t in range(TT):
                        act.wait_ge(proj_dve, 2 * t + 1)
                        act.activation(SQ[:, 0:Q_LORA] if t == 0 else SQ[:, 512:512 + Q_LORA], proj[:, t, 0:Q_LORA],
                                       ACT.Square, accum_out=lat_ss[:, t, 0:1]).then_inc(lat_sq, 1)
                        act.activation(SQ[:, 256:384] if t == 0 else SQ[:, 768:896], proj[:, t, Q_LORA:Q_LORA + KV_LORA],
                                       ACT.Square, accum_out=lat_ss[:, t, 1:2]).then_inc(lat_sq, 1)
                    act.wait_ge(toe_stored, 16)
                    act.wait_ge(lat_T, 2)
                    act.copy(cT[:, 2, :], banks[6][:, 0:T]).then_inc(cT_act, 1)
                    square_heads(act, 1)
                    for t in range(TT):
                        for b in range(2):
                            act.wait_ge(qkv_done, 4 * t + 3 + b)
                            v = banks[kv_bank[t][b]][:, :].rearrange("p (h w) -> p h w", h=4)
                            act.copy(QK[:, t, 8 + 4 * b:12 + 4 * b, 0:NOPE], v[:, :, 0:NOPE]).then_inc(kv_out, 1)
                            act.copy(V[:, t, 4 * b:4 * b + 4, :], v[:, :, NOPE:NOPE + HDV]).then_inc(kv_out, 1)
                        square_heads(act, 2 + t)
                    row_out(act, 3, banks[7], row0)
                    for i in range(1, 12, 2):
                        act.wait_ge(hdT, i + 1)
                        act.copy(*turned_to(i)).then_inc(hdT_act, 1)

                    def turned(g):
                        act.wait_ge(pT_done, g + 1)
                        if g >= 2:
                            act.wait_ge(pv_done, g - 1)
                        act.copy(probT[:, g % 2], banks[2 + g % 2][:, :].rearrange("p (c q) -> p c q", c=2)
                                 ).then_inc(pT_ready, 1)

                    for g in range(16):
                        act.wait_ge(nm_ready, g + 1)
                        if g >= 2:
                            act.wait_ge(pT_done, g - 1)
                        for q in range(2):
                            src = banks[g % 2][:, q * T:(q + 1) * T] if g < 8 else logit[:, g % 2, q, :]
                            last = act.activation(prob[:, g % 2, q, :], src, ACT.Exp, bias=nmx[:, g, q:q + 1],
                                                  scale=SC_MLA if g < 8 else 1.0, accum_out=sums[:, q, g:g + 1])
                        last.then_inc(exp_done, 1)
                        if g:
                            turned(g - 1)
                    turned(15)
                    load_mod(act, 0, 3, 5, 4)
                    load_mod(act, 1, 0, 2, 4)
                    act.dma_start(gate_bc[:, :], mod_dram[0, 2 * D:3 * D].partition_broadcast(P)).then_inc(gate_in, 16)
                    act.wait_ge(pv_done, 16)
                    act.dma_start(W[:, 0:D], ada_b[0, 2 * D:3 * D].partition_broadcast(P)).then_inc(gate_in, 16)
                    for j in (1, 3):
                        act.wait_ge(catT_done, j + 1)
                        act.copy(catT[:, 2 * j:2 * j + 2, :], banks[j][:, :].rearrange("p (k t) -> p k t", k=2)
                                 ).then_inc(catT_act, 1)

                @block.vector
                def _(dve):
                    own = Chain(dve, at_dve)
                    dve.wait_ge(x_in, 16)
                    norm_dve(dve, ns, 0, 0)
                    for t in range(TT):
                        for n in (0, 2):
                            dve.wait_ge(proj_done, 4 * t + n + 1)
                            c0, w = PROJ_COLS[n]
                            if t == 0 and n == 0:
                                dve.wait_ge(ns["turned"], 4)
                            dve.tensor_copy(proj[:, t, c0:c0 + w], banks[proj_bank[t][n]][:, 0:w]).then_inc(proj_dve, 1)
                        if t == 0:
                            dve.wait_ge(vecs_in, 96)
                            head_means(dve, own, 0)
                            scale_heads(dve, own, 0)
                    dve.wait_ge(lat_sq, 4)
                    own.link(dve.tensor_scalar(lat_m[:, :, 0], lat_ss[:, :, 0], 1.0 / Q_LORA, EPS, ALU.mult, ALU.add))
                    dve.tensor_scalar(lat_m[:, :, 1], lat_ss[:, :, 1], 1.0 / KV_LORA, EPS, ALU.mult,
                                      ALU.add).then_inc(lat_ms, 1)
                    dve.wait_ge(lat_rstd, 1)
                    for t in range(TT):
                        dve.scalar_tensor_tensor(CQN[:, t, 0:Q_LORA], proj[:, t, 0:Q_LORA], lat_r[:, t, 0:1], qaw,
                                                 ALU.mult, ALU.mult)
                        dve.scalar_tensor_tensor(CQN[:, t, Q_LORA:384], proj[:, t, Q_LORA:384], lat_r[:, t, 1:2], kvaw,
                                                 ALU.mult, ALU.mult).then_inc(lat_n, 1)
                    dve.wait_ge(toe_stored, 16)
                    dve.wait_ge(lat_T, 1)
                    dve.tensor_copy(cT[:, 0:2, :], banks[5][:, :].rearrange("p (c t) -> p c t", c=2)).then_inc(cT_dve, 1)
                    head_means(dve, own, 1)
                    scale_heads(dve, own, 1)
                    for t in range(TT):
                        qf = QK[:, t, 0:8, :].rearrange("p r w -> p (r w)")
                        for b, w in ((0, 512), (1, 256)):
                            dve.wait_ge(qkv_done, 4 * t + 1 + b)
                            dve.tensor_copy(qf[:, 512 * b:512 * b + w], banks[q_bank[t][b]][:, 0:w]).then_inc(q_out, 1)
                        dve.tensor_copy(QK[:, t, 8:16, NOPE:QK_W],
                                        proj[:, t, 384:NA0].unsqueeze(1).broadcast_to([P, 8, ROPE])).then_inc(q_out, 1)
                    dve.wait_ge(con_in, 16)
                    for t in range(TT):
                        head_means(dve, own, 2 + t)
                    for t in range(TT):
                        scale_heads(dve, own, 2 + t)
                    for i in range(0, 12, 2):
                        dve.wait_ge(hdT, i + 1)
                        dve.tensor_copy(*turned_to(i)).then_inc(hdT_dve, 1)

                    def heads_out(kind):
                        dve.wait_ge(pv_done, 8 * (kind + 1))
                        own.link(dve.reciprocal(rsum[:, :, 8 * kind:8 * kind + 8], sums[:, :, 8 * kind:8 * kind + 8]))
                        for q in range(2):
                            dve.tensor_tensor(
                                CAT[:, q, 512 * kind:512 * kind + 512].rearrange("p (h w) -> p h w", h=8),
                                banks[4 + 2 * q + kind][:, :].rearrange("p (h w) -> p h w", h=8),
                                rsum[:, q, 8 * kind:8 * kind + 8].unsqueeze(2).broadcast_to([P, 8, HDV]),
                                ALU.mult).then_inc(cat_ready, 1)

                    for g in range(16):
                        dve.wait_ge(s_done, g + 1)
                        sv = banks[g % 2][:, :].rearrange("p (q k) -> p q k", q=2)
                        if g < 8:
                            own.link(dve.tensor_reduce(mx[:, g], sv, AX, ALU.max))
                            dve.tensor_scalar(nmx[:, g], mx[:, g], -SC_MLA, None, ALU.mult).then_inc(nm_ready, 1)
                        else:
                            if g == 8:
                                dve.wait_ge(bias_ready, 2)
                            else:
                                dve.wait_ge(exp_done, g - 1)
                            own.link(dve.scalar_tensor_tensor(logit[:, g % 2], sv, SC_NA, BIAS[:, :, g - 8, :],
                                                              ALU.mult, ALU.add))
                            own.link(dve.tensor_reduce(mx[:, g], logit[:, g % 2], AX, ALU.max))
                            dve.tensor_scalar(nmx[:, g], mx[:, g], -1.0, None, ALU.mult).then_inc(nm_ready, 1)
                        if g == 10:
                            heads_out(0)
                    heads_out(1)
                    for j in (0, 2):
                        dve.wait_ge(catT_done, j + 1)
                        dve.tensor_copy(catT[:, 2 * j:2 * j + 2, :], banks[j][:, :].rearrange("p (k t) -> p k t", k=2)
                                        ).then_inc(catT_dve, 1)
                    dve.wait_ge(mod_in, 48)
                    affine(dve, mod_chain[0], 0, 1)
                    affine(dve, mod_chain[0], 1, 0)
                    dve.wait_ge(gate_in, 32)
                    own.link(dve.tensor_tensor(gate_bc[:, :], gate_bc[:, :], W[:, 0:D], ALU.add))
                    for t in range(TT):
                        for h in range(2):
                            dve.wait_ge(mix_done, 2 * t + h + 1)
                            cols = slice(512 * h, 512 * h + 512)
                            tmp = W[:, D + 512 * (2 * t + h):D + 512 * (2 * t + h + 1)]
                            own.link(dve.tensor_tensor(tmp, banks[4 + 2 * t + h][:, :], gate_bc[:, cols], ALU.mult))
                            dve.tensor_tensor(X[:, t, cols], X[:, t, cols], tmp, ALU.add)

                @block.tensor
                def _(pe):
                    norm_pe(pe, ns)
                    wait_h(pe, ns)
                    unit = KC
                    for c in range(KC // 2):
                        pe.wait_ge(win_in[c], 16)
                        for n, (c0, w) in enumerate(PROJ_COLS):
                            for k in (2 * c, 2 * c + 1):
                                last = pe.matmul(banks[proj_bank[0][n]][:, 0:w], hT[:, k, 0:P],
                                                 WIN[:, k, c0:c0 + w], start=(k == 0), stop=(k == KC - 1))
                            if c == KC // 2 - 1:
                                last.then_inc(proj_done, 1)
                        multiply_units(pe, unit, unit + UNITS_AFTER[c], banks[7], c_rep0)
                        unit += UNITS_AFTER[c]
                    for n, (c0, w) in enumerate(PROJ_COLS):
                        if n == 3:
                            pe.wait_ge(proj_dve, 1)
                        for k in range(KC):
                            last = pe.matmul(banks[proj_bank[1][n]][:, 0:w], hT[:, k, P:2 * P],
                                             WIN[:, k, c0:c0 + w], start=(k == 0), stop=(k == KC - 1))
                        last.then_inc(proj_done, 1)
                        multiply_units(pe, unit, unit + UNITS_AFTER[4 + n], banks[7], c_rep0)
                        unit += UNITS_AFTER[4 + n]
                    multiply_units(pe, 3 * KC, 3 * KC + 3, banks[7], c_rep0)
                    pe.wait_ge(proj_act, 1)
                    pe.wait_ge(proj_dve, 2)
                    for t in range(TT):
                        pe.wait_ge(lat_n, t + 1)
                        for ch in range(2):
                            last = pe.transpose(banks[5][:, ch * T + t * P:ch * T + (t + 1) * P],
                                                CQN[:, t, ch * P:(ch + 1) * P], ident)
                    last.then_inc(lat_T, 1)
                    for t in range(TT):
                        last = pe.transpose(banks[6][:, t * P:(t + 1) * P], CQN[:, t, 2 * P:3 * P], ident)
                    last.then_inc(lat_T, 1)
                    pe.wait_ge(wqkv_in, 32)
                    pe.wait_ge(cT_dve, 1)
                    pe.wait_ge(cT_act, 1)
                    pe.wait_ge(proj_dve, 4)
                    pe.wait_ge(proj_act, 4)
                    for t in range(TT):
                        for b, w in ((0, 512), (1, 256)):
                            for k in range(2):
                                last = pe.matmul(banks[q_bank[t][b]][:, 0:w], cT[:, k, t * P:(t + 1) * P],
                                                 WQB[:, k, 512 * b:512 * b + w], start=(k == 0), stop=(k == 1))
                            last.then_inc(qkv_done, 1)
                        for b in range(2):
                            if t and b:
                                pe.wait_ge(q_out, 1)
                            pe.matmul(banks[kv_bank[t][b]][:, :], cT[:, 2, t * P:(t + 1) * P],
                                      WKVB[:, 512 * b:512 * b + 512], start=True, stop=True).then_inc(qkv_done, 1)
                    multiply_units(pe, 3 * KC + 3, MOD_END, banks[7], c_rep0)
                    pe.wait_ge(q_out, 6)
                    pe.wait_ge(kv_out, 8)
                    pe.wait_ge(hd_ready, 2)
                    for i, g in enumerate(TURN):
                        if i >= 6:
                            if i % 2:
                                pe.wait_ge(hdT_act, (i - 5) // 2)
                            else:
                                pe.wait_ge(hdT_dve, (i - 4) // 2)
                        if g == 0:
                            pe.wait_ge(hd_ready, 4)
                        for r in range(2):
                            for t in range(TT):
                                if g < 8:
                                    src = QK[:, t, 2 * g + r, :]
                                else:
                                    c0 = NA0 + (2 * (g - 8) + r) * P
                                    src = proj[:, t, c0:c0 + P]
                                last = pe.transpose(banks[i % 6][0:QK_W if g < 8 else P,
                                                                 r * T + t * P:r * T + (t + 1) * P], src, ident)
                        last.then_inc(hdT, 1)
                    pe.wait_ge(hdT_act, 6)
                    pe.wait_ge(hdT_dve, 6)
                    pe.wait_ge(row_copied, 4)

                    def scores(g):
                        if g >= 2:
                            pe.wait_ge(exp_done, g - 1)
                        for q in range(2):
                            if g < 8:
                                lhs, rhs = QKT[:, g, q * P:(q + 1) * P], QKT[:, 8 + g, :]
                            else:
                                h = g - 8
                                b = 64 * (h % 2)
                                lhs, rhs = NT[b:b + 64, h // 2, q * P:(q + 1) * P], NT[b:b + 64, 4 + h // 2, :]
                            last = pe.matmul(banks[g % 2][:, q * T:(q + 1) * T], lhs, rhs, start=True, stop=True)
                        last.then_inc(s_done, 1)

                    def values(g):
                        pe.wait_ge(pT_ready, g + 1)
                        kind, h = g // 8, g % 8
                        for q in range(2):
                            for kt in range(2):
                                v = V[:, kt, h, :] if kind == 0 else \
                                    proj[:, kt, NA0 + 1024 + h * HDV:NA0 + 1024 + (h + 1) * HDV]
                                last = pe.matmul(banks[4 + 2 * q + kind][:, h * HDV:(h + 1) * HDV],
                                                 probT[:, g % 2, kt, q * P:(q + 1) * P], v,
                                                 start=(kt == 0), stop=(kt == 1))
                        last.then_inc(pv_done, 1)

                    scores(0)
                    scores(1)
                    for g in range(16):
                        pe.wait_ge(exp_done, g + 1)
                        if g >= 2:
                            pe.wait_ge(pT_ready, g - 1)
                        for kt in range(2):
                            for q in range(2):
                                last = pe.transpose(banks[2 + g % 2][:, kt * T + q * P:kt * T + (q + 1) * P],
                                                    prob[:, g % 2, q, kt * P:(kt + 1) * P], ident)
                        last.then_inc(pT_done, 1)
                        if g + 2 < 16:
                            scores(g + 2)
                        if g:
                            values(g - 1)
                    values(15)
                    pe.wait_ge(cat_ready, 4)
                    for k in range(KC):
                        for t in range(TT):
                            last = pe.transpose(banks[k // 2][:, (k % 2) * T + t * P:(k % 2) * T + (t + 1) * P],
                                                CAT[:, t, k * P:(k + 1) * P], ident)
                        if k % 2:
                            last.then_inc(catT_done, 1)
                    pe.wait_ge(catT_dve, 2)
                    pe.wait_ge(catT_act, 2)
                    pe.wait_ge(wout_in, 16)
                    for t in range(TT):
                        for h in range(2):
                            for k in range(KC):
                                last = pe.matmul(banks[4 + 2 * t + h][:, :], catT[:, k, t * P:(t + 1) * P],
                                                 WOUT[:, k, 512 * h:512 * h + 512], start=(k == 0), stop=(k == KC - 1))
                            last.then_inc(mix_done, 1)

        stored = sem("stored")

        def moe(l):
            ns = norm_sems(f"moe{l}_norm")
            names = ("router_in gate_in consts_set logits_done score_ready mask_ready hb_done hb_hi hb_lo "
                     "sh_in sgu_done sg_ready su_ready suT_done suT_ready ssd_done pos_done pos_ready "
                     "first_done table_ready pgT_done pgT_ready pgb_done pgb_ready own_dve "
                     "pick_ready pt_done pT_ready ga_done xg_act xg_dve gu_done silu_done u_ready "
                     "uT_done uT_ready d_done o_hi o_lo sc_done y_done gated").split()
            (router_in, gate_in, consts_set, logits_done, score_ready, mask_ready, hb_done, hb_hi, hb_lo,
             sh_in, sgu_done, sg_ready, su_ready, suT_done, suT_ready, ssd_done, pos_done, pos_ready,
             first_done, table_ready, pgT_done, pgT_ready, pgb_done, pgb_ready, own_dve,
             pick_ready, pt_done, pT_ready, ga_done, xg_act, xg_dve, gu_done, silu_done, u_ready,
             uT_done, uT_ready, d_done, o_hi, o_lo, sc_done, y_done, gated) = (sem(n) for n in names)
            x_done = [sem(f"x_done{t}") for t in range(TT)]
            gu_in = [sem(f"gate_up_in{i}") for i in range(4)]
            dn_in = [sem(f"down_in{i}") for i in range(4)]

            wpos[0] = TT * D
            RW = carve(KC * E_N).rearrange("p (k e) -> p k e", k=KC)
            RB = carve(E_N)
            SG = carve(FF)
            U = carve(FF).rearrange("p (j f) -> p j f", j=2)
            UT = carve(FF).rearrange("p (j s) -> p j s", j=2)
            reused = carve(2 * KC * P)
            SU = reused[:, 0:512].rearrange("p (t j f) -> p t j f", t=TT, j=2)
            SSG = reused[:, 512:1024].rearrange("p (t f) -> p t f", t=TT)
            SUT = reused[:, 1024:1536].rearrange("p (j t) -> p j t", j=2)
            xgT = reused.rearrange("p (u k s) -> p u k s", u=2, k=KC)
            score = carve(TT * E_N).rearrange("p (t e) -> p t e", t=TT)
            sel = carve(TT * E_N).rearrange("p (t e) -> p t e", t=TT)
            top2 = carve(TT * GROUPS * 8).rearrange("p (t g m) -> p t g m", t=TT, g=GROUPS)
            gsc = carve(TT * GROUPS).rearrange("p (t g) -> p t g", t=TT)
            beat = carve(TT * 64).rearrange("p (t g o) -> p t g o", t=TT, g=GROUPS)
            tie = carve(TT * 64).rearrange("p (t g o) -> p t g o", t=TT, g=GROUPS)
            rank = carve(TT * GROUPS).rearrange("p (t g) -> p t g", t=TT)
            gon = carve(TT * GROUPS).rearrange("p (t g) -> p t g", t=TT)
            goff = carve(TT * GROUPS).rearrange("p (t g) -> p t g", t=TT)
            best = carve(TT * 8).rearrange("p (t m) -> p t m", t=TT)
            left = carve(TT * E_N).rearrange("p (t e) -> p t e", t=TT)
            mask = carve(TT * E_N).rearrange("p (t e) -> p t e", t=TT)
            table = carve(2 * TT * NB).rearrange("p (a t b) -> p a t b", a=2, t=TT)
            pg = table[:, :, :, 0:E_N]
            gsum = carve(TT)
            pgT = carve(2 * TT * P)[0:E_N].rearrange("p (a t q) -> p a t q", a=2, t=TT)
            count = carve(4)
            nblk = count[0:E_N, 1:2]
            first = count[0:E_N, 2:3]
            off = carve(NX)[0:E_N]
            has = carve(NX)[0:E_N]
            ge0 = carve(NX)[0:E_N]
            rnd = carve(NX)[0:E_N]
            gcur = carve(2 * TT * 2).rearrange("p (u t b) -> p u t b", u=2, t=TT)
            gslot = carve(1)
            minus = carve(P)[0:E_N]
            ones = carve(P)
            shared = carve(SLOT_W)
            gbias = W[:, 0:D]

            def gu(w, k):
                return w[:, 0:2 * KC * FF].rearrange("p (m k f) -> p k m f", m=2, k=KC)[:, k]

            def down(w, j, h):
                return w[:, 2 * KC * FF:].rearrange("p (j n) -> p j n", j=2)[:, j, 512 * h:512 * h + 512]

            def wait(eng, s, v):
                if not isinstance(v, int) or v > 0:
                    eng.wait_ge(s, v)

            def each_pair(eng, main, tail, total, no_tail=None):
                half = MAIN_PAIRS // 2
                main(0, 0, 0)
                main(1, 1, 0)
                with eng.Fori(1, half) as i:
                    main(i * 2, 0, i)
                    main(i * 2 + 1, 1, i)
                tail(None, None, None)
                more = total(eng)
                with eng.If(more > 0):
                    tail(MAIN_PAIRS, 0, half)
                if no_tail:
                    with eng.If(more < 1):
                        no_tail()
                with eng.If(more > 2):
                    tail(MAIN_PAIRS + 1, 1, half)
                    with eng.Fori(1, TAIL_STEPS) as i:
                        for v in range(2):
                            with eng.If(more > i * 4 + 2 * v):
                                tail(i * 2 + (MAIN_PAIRS + v), v, i + half)

            def total_blocks(eng):
                return eng.value_load(ids[0:1, NX:NX + 1], min_val=0, max_val=NX)

            with nc.Block() as block:
                @block.sync
                def _(sp):
                    sp.dma_start(RW, router_w[l].rearrange("(p k) e -> p k e", k=KC)).then_inc(router_in, 16)
                    with nc.allow_non_contiguous_dma("rows for every partition"):
                        sp.dma_start(RB, router_b[l].partition_broadcast(P)).then_inc(router_in, 16)
                        sp.dma_start(gate_bc[:, :], mod_dram[l, 5 * D:6 * D].partition_broadcast(P)
                                     ).then_inc(gate_in, 16)
                    g3 = shared[:, 0:2 * KC * FF].rearrange("p (m k f) -> p m k f", m=2, k=KC)
                    sp.dma_start(g3[:, 0], sh_w_gate[l].rearrange("(p k) f -> p k f", k=KC)).then_inc(sh_in, 16)
                    sp.dma_start(g3[:, 1], sh_w_up[l].rearrange("(p k) f -> p k f", k=KC)).then_inc(sh_in, 16)
                    sp.dma_start(shared[:, 2 * KC * FF:].rearrange("p (j n) -> p j n", j=2),
                                 sh_w_down[l].rearrange("(f j) n -> f j n", j=2)).then_inc(sh_in, 16)

                    def load(n, u, e):
                        sp.wait_ge(gu_done, n - 1)
                        load_gate_up(sp, l, u, e, gu_in[2 * u:2 * u + 2])
                        sp.wait_ge(d_done, n * 2 - 2)
                        load_down(sp, l, u, e, dn_in[2 * u:2 * u + 2])

                    def main(n, u, m):
                        if isinstance(n, int):
                            if n == 0:
                                load_first_pair(sp, l, n)
                        else:
                            load(n, u, [n * 2, n * 2 + 1])

                    def tail(n, u, m):
                        if n is None:
                            sp.wait_ge(table_ready, 1)
                        else:
                            load(n, u, [sp.value_load(ids[0:1, bass.ds(n * 2 + (b - E_N), 1)],
                                                      min_val=0, max_val=E_N - 1) for b in range(2)])

                    each_pair(sp, main, tail, total_blocks)
                    if l == 0:
                        sp.wait_ge(d_done, 2 * MAIN_PAIRS)
                        with sp.If(total_blocks(sp) > 2):
                            sp.wait_ge(y_done, 1)
                        load_conv_weights(sp, low=False)
                        sp.wait_ge(y_done, 1)
                        load_conv_weights(sp, low=True)
                    else:
                        for t in range(TT):
                            sp.wait_ge(x_done[t], 2)
                            sp.dma_start(out[0, t * P:(t + 1) * P, :], X[:, t, :]).then_inc(stored, 16)
                        sp.wait_ge(stored, 16 * TT)

                @block.gpsimd
                def _(pool):
                    norm_pool(pool, ns)
                    clear_last_phase(pool)
                    pool.memset(minus, -float(SLOTS)).then_inc(consts_set, 1)
                    pool.memset(zeros[:, :].bitcast(F32), 0.0).then_inc(consts_set, 1)
                    pool.memset(ones, 1.0).then_inc(consts_set, 1)
                    for h in range(2):
                        cols = slice(512 * h, 512 * h + 512)
                        pool.wait_ge(gated, h + 1)
                        pool.tensor_tensor(X[:, 0, cols], X[:, 0, cols], reused[:, cols], ALU.add
                                           ).then_inc(x_done[0], 1)

                @block.scalar
                def _(act):
                    norm_act(act, ns, l, 1)
                    act.wait_ge(logits_done, 1)
                    act.activation(score, banks[4][:, 0:TT * E_N].rearrange("p (t e) -> p t e", t=TT),
                                   ACT.Sigmoid).then_inc(score_ready, 1)
                    act.wait_ge(ns["xn"], 2)
                    for g in range(4):
                        act.wait_ge(hb_done, g + 1)
                        act.copy(H_hi[:, g // 2, 512 * (g % 2):512 * (g % 2) + 512], banks[g][:, :]).then_inc(hb_hi, 1)
                    for t in range(TT):
                        act.wait_ge(sgu_done, t + 1)
                        act.activation(SSG[:, t], banks[6 + t][:, 0:FF], ACT.Silu).then_inc(sg_ready, 1)
                    act.wait_ge(ns["turned"], 4)
                    act.dma_start(gbias, ada_b[l, 5 * D:6 * D].partition_broadcast(P)).then_inc(gate_in, 16)

                    def take(n, u):
                        act.wait_ge(ga_done, n * 2 + 1)
                        wait(act, gu_done, n - 1)
                        act.copy(xgT[:, u, 0:4, :], banks[6][:, :].rearrange("p (k s) -> p k s", k=4)
                                 ).then_inc(xg_act, 1)

                    act.wait_ge(suT_done, 1)
                    take(0, 0)

                    def pair(n, u, m):
                        act.wait_ge(gu_done, n + 1)
                        wait(act, u_ready, n)
                        act.activation(SG, banks[4][:, 0:FF], ACT.Silu).then_inc(silu_done, 1)
                        if isinstance(n, int) and n == 0:
                            act.wait_ge(ssd_done, 1)
                        take(n + 1, 1 - u)
                        wait(act, sc_done, n)
                        act.wait_ge(pT_ready, n + 1)
                        for h in range(2):
                            act.wait_ge(d_done, n * 2 + (h + 1))
                            act.activation(O_hi[:, 512 * h:512 * h + 512], banks[6 + h][:, :], ACT.Copy,
                                           scale=gslot[:, 0:1]).then_inc(o_hi, 1)

                    def tail(n, u, m):
                        if n is None:
                            act.wait_ge(table_ready, 1)
                        else:
                            pair(n, u, m)

                    each_pair(act, pair, tail, total_blocks)

                @block.vector
                def _(dve):
                    own = Chain(dve, own_dve)
                    norm_dve(dve, ns, l, 1)
                    dve.wait_ge(con_in, 16)
                    dve.wait_ge(router_in, 32)
                    dve.wait_ge(score_ready, 1)
                    own.link(dve.tensor_tensor(sel, score, RB.unsqueeze(1).broadcast_to([P, TT, E_N]), ALU.add))
                    for t in range(TT):
                        for g in range(GROUPS):
                            last = dve.max(top2[:, t, g, :], sel[:, t, g * PER_G:(g + 1) * PER_G])
                    own.link(last)
                    own.link(dve.tensor_tensor(gsc, top2[:, :, :, 0], top2[:, :, :, 1], ALU.add))
                    glt = con[:, C_GLT:C_GLT + 64].rearrange("p (g o) -> p g o", g=GROUPS)
                    for t in range(TT):
                        mine = gsc[:, t].unsqueeze(2).broadcast_to([P, GROUPS, GROUPS])
                        other = gsc[:, t].unsqueeze(1).broadcast_to([P, GROUPS, GROUPS])
                        dve.tensor_tensor(beat[:, t], other, mine, ALU.is_gt)
                        own.link(dve.tensor_tensor(tie[:, t], other, mine, ALU.is_equal))
                        own.link(dve.tensor_tensor(tie[:, t], tie[:, t], glt, ALU.mult))
                        own.link(dve.tensor_tensor(beat[:, t], beat[:, t], tie[:, t], ALU.add))
                        own.link(dve.tensor_reduce(rank[:, t], beat[:, t], AX, ALU.add))
                    own.link(dve.tensor_scalar(gon, rank, float(GROUPS_ON), None, ALU.is_lt))
                    own.link(dve.tensor_scalar(goff, gon, -1.0, -NEG, ALU.add, ALU.mult))
                    sel4 = sel.rearrange("p t (g e) -> p (t g) e", g=GROUPS)
                    gon3 = gon.rearrange("p t g -> p (t g)").unsqueeze(2).broadcast_to([P, TT * GROUPS, PER_G])
                    goff3 = goff.rearrange("p t g -> p (t g)").unsqueeze(2).broadcast_to([P, TT * GROUPS, PER_G])
                    own.link(dve.tensor_tensor(sel4, sel4, gon3, ALU.mult))
                    own.link(dve.tensor_tensor(sel4, sel4, goff3, ALU.add))
                    for t in range(TT):
                        own.link(dve.max(best[:, t], sel[:, t]))
                        own.link(dve.match_replace(left[:, t], best[:, t], sel[:, t], -3.0e38))
                    dve.tensor_scalar(mask, left, -2.0e38, None, ALU.is_lt).then_inc(mask_ready, 1)
                    dve.wait_ge(mask_ready, 1)
                    own.link(dve.tensor_tensor(pg[:, 1], score, mask, ALU.mult))
                    own.link(dve.tensor_reduce(gsum, pg[:, 1], AX, ALU.add))
                    own.link(dve.reciprocal(gsum, gsum))
                    for t in range(TT):
                        own.link(dve.tensor_scalar(pg[:, 1, t], pg[:, 1, t], gsum[:, t:t + 1], SCALE_R,
                                                   ALU.mult, ALU.mult))
                    for g in range(4):
                        cols = slice(512 * (g % 2), 512 * (g % 2) + 512)
                        dve.wait_ge(hb_hi, g + 1)
                        dve.tensor_tensor(H_lo[:, g // 2, cols], banks[g][:, :],
                                          H_hi[:, g // 2, cols].bitcast(F32), ALU.subtract).then_inc(hb_lo, 1)

                    def shared_hidden(t):
                        dve.wait_ge(sg_ready, t + 1)
                        dve.tensor_tensor(SU[:, t].rearrange("p j f -> p f j"),
                                          SSG[:, t].rearrange("p (f j) -> p f j", j=2),
                                          banks[6 + t][:, FF:2 * FF].rearrange("p (f j) -> p f j", j=2),
                                          ALU.mult).then_inc(su_ready, 1)

                    places = con[:, C_SLOT:C_SLOT + SLOTS]

                    def choose(n, u):
                        wait(dve, pt_done, n - 1)
                        dve.tensor_copy(gcur[:, u], table[:, 1, :, bass.ds(n * 2, 2)])
                        for t in range(TT):
                            ins = dve.tensor_tensor(pick[:, u, t, :].rearrange("p (b s) -> p b s", b=2),
                                                    table[:, 0, t, bass.ds(n * 2, 2)].unsqueeze(2)
                                                    .broadcast_to([P, 2, SLOTS]),
                                                    places.unsqueeze(1).broadcast_to([P, 2, SLOTS]), ALU.is_equal)
                        ins.then_inc(pick_ready, 1)

                    def take(n, u):
                        dve.wait_ge(ga_done, n * 2 + 2)
                        wait(dve, gu_done, n - 1)
                        dve.tensor_copy(xgT[:, u, 4:8, :], banks[7][:, :].rearrange("p (k s) -> p k s", k=4)
                                        ).then_inc(xg_dve, 1)

                    dve.wait_ge(pos_done, 1)
                    own.link(dve.tensor_tensor(pg[:, 0], banks[4][:, 128:256].rearrange("p (t e) -> p t e", t=TT),
                                               mask, ALU.mult))
                    own.link(dve.tensor_copy(count[0:E_N, 0:1], banks[4][0:E_N, 256:257]))
                    own.link(dve.tensor_scalar(nblk, count[0:E_N, 0:1], float(SLOTS), None, ALU.is_gt))
                    for r in range(2, T // SLOTS):
                        ins = dve.scalar_tensor_tensor(nblk, count[0:E_N, 0:1], float(r * SLOTS), nblk,
                                                       ALU.is_gt, ALU.add)
                        if r < T // SLOTS - 1:
                            own.link(ins)
                    ins.then_inc(pos_ready, 1)
                    choose(0, 0)
                    for t in range(TT):
                        shared_hidden(t)
                    dve.wait_ge(suT_done, 1)
                    dve.tensor_copy(SUT, banks[5][:, :].rearrange("p (j t) -> p j t", j=2)).then_inc(suT_ready, 1)
                    take(0, 0)

                    def turned_table():
                        dve.wait_ge(pgT_done, 1)
                        dve.tensor_copy(pgT, banks[3][0:E_N, :].rearrange("p (a t q) -> p a t q", a=2, t=TT)
                                        ).then_inc(pgT_ready, 1)

                    def further_blocks():
                        dve.wait_ge(first_done, 1)
                        own.link(dve.tensor_copy(first, banks[4][0:E_N, 260:261]))
                        own.link(dve.tensor_scalar(off, con[0:E_N, C_BLK:C_BLK + NX], first, None, ALU.subtract))
                        own.link(dve.tensor_scalar(ge0, off, 0.0, None, ALU.is_ge))
                        own.link(dve.scalar_tensor_tensor(has, off, nblk, ge0, ALU.is_lt, ALU.mult))
                        dve.scalar_tensor_tensor(rnd, off, 1.0, has, ALU.add, ALU.mult).then_inc(pos_ready, 1)

                    def keep_table():
                        dve.wait_ge(pgb_done, 1)
                        dve.tensor_copy(ids[0:1, 0:NX + 1], banks[4][0:1, 272:272 + NX + 1]).then_inc(table_ready, 1)
                        dve.tensor_copy(table[:, :, :, E_N:NB],
                                        banks[4][:, 320:320 + 2 * TT * NX].rearrange("p (a t b) -> p a t b", a=2, t=TT)
                                        ).then_inc(pgb_ready, 1)
                        dve.wait_ge(pgb_ready, 1)

                    def pair(n, u, m):
                        choose(n + 1, 1 - u)
                        dve.wait_ge(silu_done, n + 1)
                        wait(dve, uT_done, n)
                        dve.tensor_tensor(U.rearrange("p j f -> p f j"), SG.rearrange("p (f j) -> p f j", j=2),
                                          banks[4][:, FF:2 * FF].rearrange("p (f j) -> p f j", j=2),
                                          ALU.mult).then_inc(u_ready, 1)
                        first_pair = isinstance(n, int) and n == 0
                        if first_pair:
                            turned_table()
                        dve.wait_ge(pt_done, n + 1)
                        wait(dve, sc_done, n)
                        wait(dve, o_hi, n * 2)
                        dve.tensor_copy(gslot, banks[5][:, T:T + 1])
                        dve.tensor_copy(pickT[:, :], banks[5][:, 0:T]).then_inc(pT_ready, 1)
                        dve.wait_ge(uT_done, n + 1)
                        wait(dve, d_done, n * 2)
                        dve.tensor_copy(UT, banks[5][:, 0:2 * P].rearrange("p (j s) -> p j s", j=2)
                                        ).then_inc(uT_ready, 1)
                        if first_pair:
                            further_blocks()
                        take(n + 1, 1 - u)
                        if first_pair:
                            keep_table()
                        for h in range(2):
                            cols = slice(512 * h, 512 * h + 512)
                            dve.wait_ge(o_hi, n * 2 + (h + 1))
                            dve.wait_ge(pT_ready, n + 1)
                            dve.scalar_tensor_tensor(O_lo[:, cols], banks[6 + h][:, :], gslot[:, 0:1],
                                                     O_hi[:, cols].bitcast(F32), ALU.mult,
                                                     ALU.subtract).then_inc(o_lo, 1)

                    def tail(n, u, m):
                        if n is None:
                            dve.wait_ge(gate_in, 32)
                            own.link(dve.tensor_tensor(gate_bc[:, :], gate_bc[:, :], gbias, ALU.add))
                        else:
                            pair(n, u, m)

                    each_pair(dve, pair, tail, total_blocks)
                    dve.wait_ge(y_done, 1)
                    for t in range(TT):
                        for h in range(2):
                            cols = slice(512 * h, 512 * h + 512)
                            tmp = reused[:, 512 * (2 * t + h):512 * (2 * t + h + 1)]
                            dve.tensor_tensor(tmp, banks[2 * t + h][:, :], gate_bc[:, cols], ALU.mult
                                              ).then_inc(gated, 1)
                    for h in range(2):
                        cols = slice(512 * h, 512 * h + 512)
                        dve.wait_ge(gated, h + 3)
                        dve.tensor_tensor(X[:, 1, cols], X[:, 1, cols], reused[:, 1024 + 512 * h:1536 + 512 * h],
                                          ALU.add).then_inc(x_done[1], 1)

                @block.tensor
                def _(pe):
                    def gather(n, u, half):
                        pe.wait_ge(pick_ready, n + 1)
                        for k in range(4):
                            kk = 4 * half + k
                            for t in range(TT):
                                for part in (H_hi, H_lo):
                                    last = pe.matmul(banks[6 + half][:, k * P:(k + 1) * P],
                                                     part[:, t, kk * P:(kk + 1) * P], pick[:, u, t, :],
                                                     start=(t == 0 and part is H_hi),
                                                     stop=(t == 1 and part is H_lo))
                        last.then_inc(ga_done, 1)

                    norm_pe(pe, ns)
                    wait_h(pe, ns)
                    pe.wait_ge(router_in, 32)
                    for t in range(TT):
                        for k in range(KC):
                            last = pe.matmul(banks[4][:, t * E_N:(t + 1) * E_N], hT[:, k, t * P:(t + 1) * P],
                                             RW[:, k, :], start=(k == 0), stop=(k == KC - 1))
                    last.then_inc(logits_done, 1)
                    for g in range(4):
                        for k in range(4):
                            kk = 4 * (g % 2) + k
                            last = pe.transpose(banks[g][:, k * P:(k + 1) * P],
                                                hT[:, kk, (g // 2) * P:(g // 2 + 1) * P], ident)
                        last.then_inc(hb_done, 1)
                    def shared_gate_up(t):
                        for k in range(KC):
                            last = pe.matmul(banks[6 + t][:, :], hT[:, k, t * P:(t + 1) * P], gu(shared, k),
                                             start=(k == 0), stop=(k == KC - 1))
                        last.then_inc(sgu_done, 1)

                    pe.wait_ge(sh_in, 48)
                    shared_gate_up(0)
                    pe.wait_ge(mask_ready, 1)
                    pe.wait_ge(consts_set, 3)
                    tri = con[:, C_TRI:C_TRI + P]
                    pe.matmul(banks[4][:, 128:192], tri, mask[:, 0, :], start=True, stop=True)
                    pe.matmul(banks[4][:, 192:256], tri, mask[:, 1, :], start=True, stop=False)
                    pe.matmul(banks[4][:, 192:256], ones, mask[:, 0, :], start=False, stop=True)
                    for t in range(TT):
                        last = pe.matmul(banks[4][0:E_N, 256:257], mask[:, t, :], ones[:, 0:1],
                                         start=(t == 0), stop=(t == 1))
                    last.then_inc(pos_done, 1)
                    shared_gate_up(1)
                    pe.wait_ge(hb_lo, 4)
                    pe.wait_ge(su_ready, 1)
                    gather(0, 0, 0)
                    pe.wait_ge(su_ready, 2)
                    for j in range(2):
                        for t in range(TT):
                            last = pe.transpose(banks[5][:, j * T + t * P:j * T + (t + 1) * P], SU[:, t, j, :], ident)
                    last.then_inc(suT_done, 1)
                    pe.wait_ge(pos_ready, 1)
                    gather(0, 0, 1)

                    def shared_down():
                        for a in range(2):
                            for t in range(TT):
                                last = pe.transpose(banks[3][0:E_N, (2 * a + t) * P:(2 * a + t + 1) * P],
                                                    pg[:, a, t, :], ident)
                        last.then_inc(pgT_done, 1)
                        pe.wait_ge(suT_ready, 1)
                        for t in range(TT):
                            for h in range(2):
                                if t and h:
                                    pe.wait_ge(pgT_ready, 1)
                                for j in range(2):
                                    last = pe.matmul(banks[2 * t + h][:, :], SUT[:, j, t * P:(t + 1) * P],
                                                     down(shared, j, h), start=(j == 0), stop=False,
                                                     skip_group_check=True)
                        last.then_inc(ssd_done, 1)

                    def first_blocks():
                        pe.matmul(banks[4][0:E_N, 260:261], con[0:E_N, C_STRICT:C_STRICT + E_N], nblk,
                                  start=True, stop=True)
                        pe.matmul(banks[4][0:1, 272 + NX:273 + NX], ones[0:E_N, 0:1], nblk,
                                  start=True, stop=True).then_inc(first_done, 1)

                    def block_table():
                        pe.wait_ge(pos_ready, 2)
                        pe.matmul(banks[4][0:1, 272:272 + NX], con[0:E_N, C_EIDX:C_EIDX + 1], has,
                                  start=True, stop=True)
                        for t in range(TT):
                            at = 320 + t * NX
                            pe.matmul(banks[4][:, at:at + NX], pgT[:, 0, t, :], has, start=True, stop=False)
                            pe.matmul(banks[4][:, at:at + NX], minus, rnd, start=False, stop=True)
                        for t in range(TT):
                            at = 320 + (2 + t) * NX
                            last = pe.matmul(banks[4][:, at:at + NX], pgT[:, 1, t, :], has, start=True, stop=True)
                        last.then_inc(pgb_done, 1)

                    def scatter(n):
                        pe.wait_ge(pT_ready, n)
                        pe.wait_ge(o_lo, n * 2)
                        for t in range(TT):
                            for h in range(2):
                                for part in (O_hi, O_lo):
                                    last = pe.matmul(banks[2 * t + h][:, :], pickT[:, t * P:(t + 1) * P],
                                                     part[:, 512 * h:512 * h + 512], start=False, stop=False,
                                                     skip_group_check=True)
                        last.then_inc(sc_done, 1)

                    def pair(n, u, m, in_tail=False):
                        first_further = isinstance(n, int) and n == MAIN_PAIRS
                        if isinstance(n, int) and n < 2:
                            pe.wait_ge(first_gu[l][n], 64)
                        else:
                            for b in range(2):
                                pe.wait_ge(gu_in[2 * u + b], m * 32)
                        pe.wait_ge(xg_act, n + 1)
                        pe.wait_ge(xg_dve, n + 1)
                        wait(pe, u_ready, n)
                        if isinstance(n, int) and n == 1:
                            pe.wait_ge(pgb_ready, 1)
                        for k in range(KC):
                            for b in range(2):
                                last = pe.matmul(banks[4][64 * b:64 * b + 64, :], xgT[:, u, k, 64 * b:64 * b + 64],
                                                 gu(slot(2 * u + b), k), start=(k == 0), stop=(k == KC - 1))
                        last.then_inc(gu_done, 1)
                        if isinstance(n, int) and n == 0:
                            shared_down()
                        elif not in_tail or first_further:
                            scatter(n)
                        wait(pe, uT_ready, n)
                        for t in range(TT):
                            pe.transpose(banks[5][:, t * P:(t + 1) * P], pick[:, u, t, :].bitcast(F32), ident)
                        for b in range(2):
                            for t in range(TT):
                                last = pe.matmul(banks[5][64 * b:64 * b + 64, T:T + 1],
                                                 pick[:, u, t, 64 * b:64 * b + 64].bitcast(F32),
                                                 gcur[:, u, t, b:b + 1], start=(t == 0), stop=(t == 1))
                        last.then_inc(pt_done, 1)
                        gather(n + 1, 1 - u, 0)
                        pe.wait_ge(u_ready, n + 1)
                        pe.wait_ge(pT_ready, n + 1)
                        for j in range(2):
                            last = pe.transpose(banks[5][:, j * P:(j + 1) * P], U[:, j, :], ident)
                        last.then_inc(uT_done, 1)
                        if isinstance(n, int) and n == 0:
                            first_blocks()
                        gather(n + 1, 1 - u, 1)
                        if isinstance(n, int) and n == 0:
                            block_table()
                        if isinstance(n, int) and n < 2:
                            pe.wait_ge(first_dn[l][n], 32)
                        else:
                            for b in range(2):
                                pe.wait_ge(dn_in[2 * u + b], m * 16)
                        pe.wait_ge(uT_ready, n + 1)
                        for h in range(2):
                            pe.wait_ge(xg_dve if h else xg_act, n + 2)
                            for j in range(2):
                                for b in range(2):
                                    last = pe.matmul(banks[6 + h][64 * b:64 * b + 64, :], UT[:, j, 64 * b:64 * b + 64],
                                                     down(slot(2 * u + b), j, h), start=(j == 0), stop=(j == 1))
                            last.then_inc(d_done, 1)
                        if in_tail:
                            scatter(n + 1)

                    def tail(n, u, m):
                        if n is not None:
                            pair(n, u, m, in_tail=True)

                    each_pair(pe, pair, tail, total_blocks, lambda: scatter(MAIN_PAIRS))
                    pe.wait_ge(pgb_ready, 1)
                    for b in range(4):
                        last = pe.matmul(banks[b][:, :], zeros[:, :], pick[:, :, :, :].rearrange("p u t q -> p (u t q)"),
                                         start=False, stop=True, skip_group_check=True)
                    last.then_inc(y_done, 1)

        PW1_HIGH = 2 * SLOT_W // (2 * D)
        pw1_high = ring[:, 2 * SLOT_W:4 * SLOT_W].rearrange("p (k n) -> p k n", k=PW1_HIGH)
        pw1_low = ring[:, 0:(KC - PW1_HIGH) * 2 * D].rearrange("p (k n) -> p k n", n=2 * D)
        PW2 = ring[:, (KC - PW1_HIGH) * 2 * D:2 * SLOT_W].rearrange("p (k n) -> p k n", k=KC)

        def PW1(k):
            return pw1_high[:, k] if k < PW1_HIGH else pw1_low[:, k - PW1_HIGH]

        pw1_in, pw2_in = sem("pw1_in"), sem("pw2_in")

        def load_conv_weights(sp, low):
            v = pw1_w[0].rearrange("(p k) n -> p k n", k=KC)
            if low:
                sp.dma_start(pw1_low, v[:, PW1_HIGH:KC]).then_inc(pw1_in, 16)
                sp.dma_start(PW2, pw2_w[0].rearrange("(p k) n -> p k n", k=KC)).then_inc(pw2_in, 16)
            else:
                for k in range(0, PW1_HIGH, 2):
                    sp.dma_start(pw1_high[:, k:k + 2], v[:, k:k + 2]).then_inc(pw1_in, 16)

        def conv():
            ns = norm_sems("conv_norm")
            names = ("cvec_in gate_in pads_clear pw1_done sig_ready glu_ready tap_done diag_ready diag_used y_act "
                     "mean_done cen_ready csq_ready var_done var_ready rs_ready yn_ready act_ready pw2_done own_dve ones_set").split()
            (cvec_in, gate_in, pads_clear, pw1_done, sig_ready, glu_ready, tap_done, diag_ready, diag_used, y_act,
             mean_done, cen_ready, csq_ready, var_done, var_ready, rs_ready, yn_ready, act_ready, pw2_done, own_dve,
             ones_set) = (sem(n) for n in names)
            wpos[0] = TT * D
            GW = T + 2 * PAD
            G = carve(KC * GW).rearrange("p (m t) -> p m t", m=KC)
            Y = carve(KC * T).rearrange("p (m t) -> p m t", m=KC)
            Ysq = carve(KC * T).rearrange("p (m t) -> p m t", m=KC)
            sig = carve(2 * T).rearrange("p (b t) -> p b t", b=2)
            b1 = carve(2 * KC).rearrange("p (s k) -> p s k", s=2)
            taps = carve(CONV_W * KC).rearrange("p (w k) -> p w k", w=CONV_W)
            vec = carve(3 * KC).rearrange("p (a k) -> p a k", a=3)
            ones = carve(P)
            var = carve(T)
            rs = carve(T)
            b2 = carve(D)
            gbias = carve(D)
            row = carve(ADA_N // 4)
            c_rep = carve(KC * 32).rearrange("p (k m) -> p k m", k=KC)
            S = hT
            VEC_CHUNKS = 6
            HALF_V = VEC_CHUNKS // 2
            BOTH = VEC_CHUNKS - 1
            SPLIT = 24
            PE_TAPS = [(BOTH, w) for w in range(SPLIT, CONV_W)] + \
                      [(m, w) for m in range(VEC_CHUNKS, KC) for w in range(CONV_W)]
            PE_BANK = {BOTH: 2, VEC_CHUNKS: 4, VEC_CHUNKS + 1: 5}
            VEC_TAPS = [(m, w) for a in range(2) for w in range(CONV_W) for m in range(HALF_V * a, HALF_V * (a + 1))
                        if m != BOTH or w < SPLIT]
            VEC_TAPS.insert(VEC_TAPS.index((HALF_V, CONV_W - 4)), (BOTH, "sum"))
            GLU_BEFORE = {(0, 7): 3, (0, 13): 4, (0, 19): 5, (0, 25): 6, (HALF_V, 0): 7}

            def taps_done(m, w):
                return VEC_TAPS.index((m, w)) + 1
            RING = TT * D // P
            diag = W[:, 0:TT * D].rearrange("p (i c) -> p i c", i=RING)
            MOD_FIRST, MOD_MID, MOD_END = 4 * KC, 5 * KC, 6 * KC

            with nc.Block() as block:
                @block.sync
                def _(sp):
                    with nc.allow_non_contiguous_dma("vectors by (p, k), rows for every partition"):
                        sp.dma_start(b1, pw1_b[0].rearrange("(s p k) -> p s k", s=2, k=KC)).then_inc(cvec_in, 16)
                        sp.dma_start(taps, dw_w[0].rearrange("w (p k) -> p w k", k=KC)).then_inc(cvec_in, 16)
                        for a, src in enumerate((dw_b, conv_ln_w, conv_ln_b)):
                            sp.dma_start(vec[:, a], pk(src[0])).then_inc(cvec_in, 16)
                        sp.dma_start(gbias, ada_b[1, 2 * D:3 * D].partition_broadcast(P)).then_inc(gate_in, 16)
                        sp.dma_start(b2, pw2_b[0].partition_broadcast(P)).then_inc(gate_in, 16)
                        sp.wait_ge(pw1_done, KC)
                        load_units(sp, MOD_FIRST, MOD_END)
                        sp.wait_ge(row_stored, 16 * 5)
                        sp.dma_start(gate_bc[:, :], mod_dram[1, 2 * D:3 * D].partition_broadcast(P)
                                     ).then_inc(gate_in, 16)
                    sp.wait_ge(ada_done, MOD_END)
                    sp.wait_ge(mod_in, 64)
                    load_first_pair(sp, 1, 1)

                @block.gpsimd
                def _(pool):
                    pool.memset(ones, 1.0).then_inc(ones_set, 1)
                    norm_pool(pool, ns)
                    clear_last_phase(pool)
                    pool.memset(G[:, :, 0:PAD], 0.0)
                    pool.memset(G[:, :, PAD + T:GW], 0.0).then_inc(pads_clear, 1)

                @block.scalar
                def _(act):
                    norm_act(act, ns, 1, 0)
                    act.wait_ge(cvec_in, 80)
                    act.wait_ge(ns["turned"], 4)

                    def diagonal(i):
                        m, w = PE_TAPS[i]
                        if i >= RING:
                            act.wait_ge(diag_used, i - RING + 1)
                        act.activation(diag[:, i % RING, :], ident, ACT.Copy,
                                       scale=taps[:, w, m:m + 1]).then_inc(diag_ready, 1)

                    for i in range(RING):
                        diagonal(i)
                    for m in range(KC):
                        act.wait_ge(pw1_done, m + 1)
                        if m >= 2:
                            act.wait_ge(glu_ready, m - 1)
                        act.activation(sig[:, m % 2], banks[m][:, T:2 * T], ACT.Sigmoid,
                                       bias=b1[:, 1, m:m + 1]).then_inc(sig_ready, 1)
                    for i in range(RING, len(PE_TAPS)):
                        diagonal(i)
                    for m in range(VEC_CHUNKS, KC):
                        act.wait_ge(diag_used, PE_TAPS.index((m, CONV_W - 1)) + 1)
                        act.activation(Y[:, m], banks[PE_BANK[m]][:, 0:T], ACT.Identity, bias=vec[:, 0, m:m + 1]
                                       ).then_inc(y_act, 1)
                    row_out(act, 4, banks[3], row)
                    half = KC // 2
                    for a in range(2):
                        act.wait_ge(cen_ready, a + 1)
                        act.activation(Ysq[:, half * a:half * (a + 1)], Y[:, half * a:half * (a + 1)], ACT.Square
                                       ).then_inc(csq_ready, 1)
                    act.wait_ge(var_ready, 1)
                    act.activation(rs, var, ACT.Sqrt).then_inc(rs_ready, 1)
                    for m in range(KC):
                        act.wait_ge(yn_ready, 2 * m // KC + 1)
                        act.activation(S[:, m], Y[:, m], ACT.Silu, bias=vec[:, 2, m:m + 1],
                                       scale=vec[:, 1, m:m + 1]).then_inc(act_ready, 1)
                    row_out(act, 5, banks[3], row)
                    load_mod(act, 1, 3, 5, 6)

                @block.vector
                def _(dve):
                    own = Chain(dve, own_dve)
                    norm_dve(dve, ns, 1, 0)
                    dve.wait_ge(pads_clear, 1)
                    dve.wait_ge(cvec_in, 80)
                    dve.tensor_copy(c_rep, csil.unsqueeze(2).broadcast_to([P, KC, 32])).then_inc(c_rep_ready, 1)

                    def glu(m):
                        dve.wait_ge(sig_ready, m + 1)
                        dve.scalar_tensor_tensor(G[:, m, PAD:PAD + T], banks[m][:, 0:T], b1[:, 0, m:m + 1],
                                                 sig[:, m % 2], ALU.add, ALU.mult).then_inc(glu_ready, 1)

                    for m in range(HALF_V):
                        glu(m)
                    for m, w in VEC_TAPS:
                        if (m, w) in GLU_BEFORE:
                            glu(GLU_BEFORE[m, w])
                        if w == 0:
                            dve.wait_ge(glu_ready, m + 1)
                            ins = dve.tensor_scalar(Y[:, m], G[:, m, 0:T], taps[:, 0, m:m + 1],
                                                    vec[:, 0, m:m + 1], ALU.mult, ALU.add)
                        elif w == "sum":
                            dve.wait_ge(tap_done, taps_done(m, SPLIT - 1))
                            dve.wait_ge(diag_used, CONV_W - SPLIT)
                            ins = dve.tensor_tensor(Y[:, m], banks[PE_BANK[m]][:, 0:T], Y[:, m], ALU.add)
                        else:
                            dve.wait_ge(tap_done, taps_done(m, w - 1))
                            ins = dve.scalar_tensor_tensor(Y[:, m], G[:, m, w:w + T], taps[:, w, m:m + 1],
                                                           Y[:, m], ALU.mult, ALU.add)
                        ins.then_inc(tap_done, 1)
                    dve.wait_ge(mean_done, 1)
                    half = KC // 2
                    for a in range(2):
                        Ya = Y[:, half * a:half * (a + 1)]
                        dve.scalar_tensor_tensor(Ya, banks[0][:, 0:T].unsqueeze(1).broadcast_to([P, half, T]),
                                                 -1.0 / D, Ya, ALU.mult, ALU.add).then_inc(cen_ready, 1)
                    dve.wait_ge(var_done, 1)
                    dve.tensor_scalar(var, banks[1][:, 0:T], 1.0 / D, EPS, ALU.mult, ALU.add).then_inc(var_ready, 1)
                    dve.wait_ge(rs_ready, 1)
                    own.link(dve.reciprocal(rs, rs))
                    for a in range(2):
                        Ya = Y[:, half * a:half * (a + 1)]
                        dve.tensor_tensor(Ya, Ya, rs.unsqueeze(1).broadcast_to([P, half, T]), ALU.mult
                                          ).then_inc(yn_ready, 1)
                    dve.wait_ge(gate_in, 48)
                    own.link(dve.tensor_tensor(gate_bc[:, :], gate_bc[:, :], gbias, ALU.add))
                    own.link(dve.tensor_tensor(b2, b2, gate_bc[:, :], ALU.mult))
                    for t in range(TT):
                        own.link(dve.tensor_tensor(X[:, t], X[:, t], b2, ALU.add))
                    dve.wait_ge(mod_in, 64)
                    affine(dve, mod_chain[0], 1, 1)
                    for t in range(TT):
                        for h in range(2):
                            cols = slice(512 * h, 512 * h + 512)
                            dve.wait_ge(pw2_done, 2 * t + h + 1)
                            tmp = Ysq.rearrange("p m t -> p (m t)")[:, 512 * (2 * t + h):512 * (2 * t + h + 1)]
                            own.link(dve.tensor_tensor(tmp, banks[4 + 2 * t + h][:, :], gate_bc[:, cols], ALU.mult))
                            dve.tensor_tensor(X[:, t, cols], X[:, t, cols], tmp, ALU.add)

                @block.tensor
                def _(pe):
                    norm_pe(pe, ns)
                    wait_h(pe, ns)
                    pe.wait_ge(pw1_in, 64)
                    for m in range(KC):
                        for s in range(2):
                            for k in range(KC):
                                last = pe.matmul(banks[m][:, s * T:(s + 1) * T], PW1(k)[:, s * D + m:(s + 1) * D:KC],
                                                 hT[:, k, :], start=(k == 0), stop=(k == KC - 1))
                        last.then_inc(pw1_done, 1)
                    pe.wait_ge(c_rep_ready, 2)
                    pe.wait_ge(pads_clear, 1)
                    pe.wait_ge(ones_set, 1)
                    every = -(-len(PE_TAPS) // (MOD_MID - MOD_FIRST))
                    for i, (m, w) in enumerate(PE_TAPS):
                        if i % every == every - 1 or i == len(PE_TAPS) - 1:
                            n = MOD_FIRST + i // every
                            multiply_units(pe, n, n + 1, banks[3], c_rep)
                        first = w == (SPLIT if m == BOTH else 0)
                        if first:
                            pe.wait_ge(glu_ready, m + 1)
                        pe.wait_ge(diag_ready, i + 1)
                        pe.matmul(banks[PE_BANK[m]][:, 0:T], diag[:, i % RING, :], G[:, m, w:w + T],
                                  start=first, stop=(w == CONV_W - 1)).then_inc(diag_used, 1)
                    for m in range(KC):
                        if m < VEC_CHUNKS:
                            pe.wait_ge(tap_done, taps_done(m, "sum" if m == BOTH else CONV_W - 1))
                        else:
                            pe.wait_ge(y_act, m - VEC_CHUNKS + 1)
                        last = pe.matmul(banks[0][:, 0:T], ones, Y[:, m], start=(m == 0), stop=(m == KC - 1))
                    last.then_inc(mean_done, 1)
                    multiply_units(pe, MOD_MID, MOD_MID + 3, banks[3], c_rep)
                    for m in range(KC):
                        pe.wait_ge(csq_ready, 2 * m // KC + 1)
                        last = pe.matmul(banks[1][:, 0:T], ones, Ysq[:, m], start=(m == 0), stop=(m == KC - 1))
                    last.then_inc(var_done, 1)
                    multiply_units(pe, MOD_MID + 3, MOD_END, banks[3], c_rep)
                    pe.wait_ge(pw2_in, 16)
                    for t in range(TT):
                        for h in range(2):
                            for k in range(KC):
                                pe.wait_ge(act_ready, k + 1)
                                last = pe.matmul(banks[4 + 2 * t + h][:, :], S[:, k, t * P:(t + 1) * P],
                                                 PW2[:, k, 512 * h:512 * h + 512], start=(k == 0), stop=(k == KC - 1))
                            last.then_inc(pw2_done, 1)

        with phase("attention"):
            attention()
        with phase("moe0"):
            moe(0)
        with phase("conv"):
            conv()
        with phase("moe1"):
            moe(1)
        for old in last_stack:
            old.close()


def constants():
    import numpy as np
    a = np.zeros((P, C_N), np.float32)
    q = np.arange(P)
    a[:, C_ID:C_ID + P] = np.eye(P)
    a[:, C_TRI:C_TRI + P] = q[:, None] <= q[None, :]
    a[:, C_STRICT:C_STRICT + E_N] = q[:, None] < np.arange(E_N)[None, :]
    a[:, C_SLOT:C_SLOT + SLOTS] = np.arange(1, SLOTS + 1)
    a[:, C_BLK:C_BLK + NX] = np.arange(NX)
    g = np.arange(GROUPS)
    a[:, C_GLT:C_GLT + 64] = (g[None, :] < g[:, None]).reshape(-1)
    a[:, C_EIDX] = q
    n_freq = ROPE // 4
    inv = np.float32(10000.0) ** (-np.arange(n_freq, dtype=np.float32) / np.float32(n_freq))
    t = np.arange(T)
    ang = np.concatenate([(t // GRID_W).astype(np.float32)[:, None] * inv,
                          (t % GRID_W).astype(np.float32)[:, None] * inv], -1).astype(np.float32)
    co, si = np.cos(ang), np.sin(ang)
    for i in range(TT):
        r = slice(i * P, (i + 1) * P)
        a[:, C_COS + i * ROPE:C_COS + (i + 1) * ROPE] = np.concatenate([co[r], co[r]], -1)
        a[:, C_SIN + i * ROPE:C_SIN + (i + 1) * ROPE] = np.concatenate([-si[r], si[r]], -1)
    col = q % GRID_W
    start = np.clip(col - NA_KW // 2, 0, GRID_W - NA_KW)[:, None]
    key = np.arange(GRID_W)[None, :]
    a[:, C_WIN:C_WIN + GRID_W] = np.where((key >= start) & (key < start + NA_KW), 0.0, NEG)
    return a


_INS = ["x", "c", "norm1_w", "norm2_w", "ada_w", "ada_b", "w_in", "q_a_norm_w", "kv_a_norm_w", "w_q_b", "w_kv_b",
        "mla_q_norm_w", "mla_k_norm_w", "na_q_norm_w", "na_k_norm_w", "na_rpb", "w_out", "pw1_w", "pw1_b", "dw_w",
        "dw_b", "conv_ln_w", "conv_ln_b", "pw2_w", "pw2_b", "router_w", "router_b", "exp_w_gate", "exp_w_up",
        "exp_w_down", "sh_w_gate", "sh_w_up", "sh_w_down"]


def kernel(**inputs):
    import numpy as np
    import concourse.bacc as bacc
    from concourse.bass_utils import run_bass_kernel_spmd

    nc = bacc.Bacc("TRN2", target_bir_lowering=False, num_devices=1)
    arrays, args = {}, []
    for name in _INS:
        a = np.ascontiguousarray(inputs[name])
        arrays[f"in_{name}"] = a
        args.append(nc.dram_tensor(f"in_{name}", a.shape, mybir.dt.from_np(a.dtype), kind="ExternalInput").ap())
    arrays["in_consts"] = constants()
    args.append(nc.dram_tensor("in_consts", (P, C_N), F32, kind="ExternalInput").ap())
    args.append(nc.dram_tensor("out_0", (1, T, D), F32, kind="ExternalOutput").ap())
    build_encoder(nc, *args)
    r = run_bass_kernel_spmd(nc, [arrays], core_ids=[0])
    return r.results[0]["out_0"]
```
